# Optimizing a Trainium2 kernel written in Bass

```python
import math
import jax, jax.numpy as jnp
from jax import lax
import numpy as np

D_MODEL = 1024
BATCH = 1
SEQ = 1024
DEPTH = 2
DEC_BATCH = 8
DEC_SEQ = 4
PAST_LEN = 256
PAGE_SIZE = 128

N_A_LAYERS = (DEPTH + 1) // 2
N_C_LAYERS = DEPTH // 2
NSA_HEADS = 8
NSA_KV_HEADS = 2
HEAD_DIM = 64
HPG = NSA_HEADS // NSA_KV_HEADS
NSA_WIDTH = NSA_HEADS * HEAD_DIM
KV_WIDTH = NSA_KV_HEADS * HEAD_DIM
CMP_BLOCK = 64
N_SEL = 16
WINDOW = 512
Q_BLOCK = 128
GMLP_GROUPS = 4
GMLP_CHUNK = 128
GMLP_WIDTH = D_MODEL // 2
GMLP_GROUP_DIM = GMLP_WIDTH // GMLP_GROUPS
LRU_WIDTH = D_MODEL
LRU_HEADS = 8
LRU_BLOCK = LRU_WIDTH // LRU_HEADS
CONV_WIDTH = 4
LRU_C = 8.0
REL_BUCKETS = 32
REL_MAX_DIST = 1024
EPS = 1e-6
NEG = -1e30
SPLIT_A = (NSA_WIDTH, 6 * KV_WIDTH, 3 * NSA_HEADS, NSA_WIDTH, GMLP_WIDTH, GMLP_WIDTH, GMLP_WIDTH)
PROJ_A = sum(SPLIT_A)
OUT_A = NSA_WIDTH + GMLP_WIDTH

kernel_name = 'hybrid_nsa_gmlp_rglru_step'

def rms_norm(x, g):
    xf = x.astype(jnp.float32)
    y = xf * lax.rsqrt(jnp.mean(xf * xf, axis=-1, keepdims=True) + EPS)
    return (y * g.astype(jnp.float32)).astype(x.dtype)

def rel_bucket(d):
    max_exact = REL_BUCKETS // 2
    df = jnp.maximum(d, 1).astype(jnp.float32)
    large = max_exact + (jnp.log(df / max_exact) / math.log(REL_MAX_DIST / max_exact)
                         * (REL_BUCKETS - max_exact)).astype(jnp.int32)
    return jnp.where(d < max_exact, d, jnp.minimum(large, REL_BUCKETS - 1))

def nsa_block(qb, qpos, kc, vc, kc_end, ks_t, vs_t, kw, vw, wpos, rel_bias):
    B, Tb = qb.shape[0], qb.shape[1]
    f32 = jnp.float32
    scale = HEAD_DIM ** -0.5
    qg = qb.reshape(B, Tb, NSA_KV_HEADS, HPG, HEAD_DIM)
    tab = rel_bias.astype(f32).reshape(REL_BUCKETS, NSA_KV_HEADS, HPG)
    s_c = jnp.einsum('btghd,bngd->bghtn', qg, kc).astype(f32) * scale
    d_c = qpos[:, None] - kc_end[None, :]
    ok_c = d_c >= 0
    s_c = s_c + jnp.transpose(tab[rel_bucket(jnp.maximum(d_c, 0))], (2, 3, 0, 1))
    p_c = jax.nn.softmax(jnp.where(ok_c, s_c, NEG), axis=-1) * ok_c
    o_c = jnp.einsum('bghtn,bngd->btghd', p_c.astype(vc.dtype), vc)
    n_blk = kc.shape[1]
    blk = jnp.arange(n_blk, dtype=jnp.int32)[None, :]
    cur = (qpos // CMP_BLOCK)[:, None]
    forced = (blk == 0) | (blk == cur) | (blk == cur - 1)
    score = jnp.where(forced, jnp.inf, jnp.where(blk < cur, p_c.sum(axis=2), -jnp.inf))
    top_s, top_i = lax.top_k(score, min(N_SEL, n_blk))
    bi = jnp.arange(B)[:, None, None, None]
    gi = jnp.arange(NSA_KV_HEADS)[None, :, None, None]
    k_s = ks_t[bi, gi, top_i]
    v_s = vs_t[bi, gi, top_i]
    kpos = top_i[..., None] * CMP_BLOCK + jnp.arange(CMP_BLOCK, dtype=jnp.int32)
    d_s = qpos[None, None, :, None, None] - kpos
    ok_s = (top_s > -jnp.inf)[..., None] & (d_s >= 0)
    tab_g = jnp.transpose(tab, (1, 0, 2))
    b_s = jnp.moveaxis(tab_g[gi[..., None], rel_bucket(jnp.maximum(d_s, 0))], -1, 2)
    s_s = jnp.einsum('btghd,bgtkcd->bghtkc', qg, k_s).astype(f32) * scale + b_s
    s_s = jnp.where(ok_s[:, :, None], s_s, NEG)
    n_key = s_s.shape[-2] * CMP_BLOCK
    p_s = jax.nn.softmax(s_s.reshape(B, NSA_KV_HEADS, HPG, Tb, n_key), axis=-1)
    o_s = jnp.einsum('bghtk,bgtkd->btghd', p_s.astype(v_s.dtype),
                     v_s.reshape(B, NSA_KV_HEADS, Tb, n_key, HEAD_DIM))
    s_w = jnp.einsum('btghd,bkgd->bghtk', qg, kw).astype(f32) * scale
    d_w = qpos[:, None] - wpos[None, :]
    ok_w = (d_w >= 0) & (d_w <= WINDOW) & (wpos >= 0)[None, :]
    s_w = s_w + jnp.transpose(tab[rel_bucket(jnp.maximum(d_w, 0))], (2, 3, 0, 1))
    p_w = jax.nn.softmax(jnp.where(ok_w, s_w, NEG), axis=-1)
    o_w = jnp.einsum('bghtk,bkgd->btghd', p_w.astype(vw.dtype), vw)
    shp = (B, Tb, NSA_HEADS, HEAD_DIM)
    return (o_c.reshape(shp), o_s.reshape(shp), o_w.reshape(shp))

def mixer_ab(h, pos0, past_kv, win_kv, w_in, b_gate, pe_cmp, w_cmp, ln_g, ln_b, w_sp, b_sp, w_out, rel_bias):
    B, T, _ = h.shape
    f32 = jnp.float32
    idx = [int(i) for i in np.cumsum(SPLIT_A)[:-1]]
    proj = jnp.einsum('btd,de->bte', h, w_in)
    q, kv6, g_logit, z_nsa, u, v, z_g = jnp.split(proj, idx, axis=-1)
    q = q.reshape(B, T, NSA_HEADS, HEAD_DIM)
    kv6 = kv6.reshape(B, T, 6, NSA_KV_HEADS, HEAD_DIM)
    new_rows = kv6[:, :, :4]
    win_rows = kv6[:, :, 4:]
    full = new_rows if past_kv is None else jnp.concatenate([past_kv.astype(new_rows.dtype), new_rows], axis=1)
    L = full.shape[1]
    n_blk = -(-L // CMP_BLOCK)
    fb = jnp.pad(full, ((0, 0), (0, n_blk * CMP_BLOCK - L), (0, 0), (0, 0), (0, 0)))
    fb = fb.reshape(B, n_blk, CMP_BLOCK, 4, NSA_KV_HEADS, HEAD_DIM)
    kc = jnp.einsum('bngd,de->bnge', jnp.mean(fb[:, :, :, 0] + pe_cmp[0][None, None, :, None, :], axis=2), w_cmp[0])
    vc = jnp.einsum('bngd,de->bnge', jnp.mean(fb[:, :, :, 1] + pe_cmp[1][None, None, :, None, :], axis=2), w_cmp[1])
    kc_end = jnp.arange(n_blk, dtype=jnp.int32) * CMP_BLOCK + (CMP_BLOCK - 1)
    ks_t = jnp.transpose(fb[:, :, :, 2], (0, 3, 1, 2, 4))
    vs_t = jnp.transpose(fb[:, :, :, 3], (0, 3, 1, 2, 4))
    if win_kv is None:
        nb = T // Q_BLOCK
        wpad = jnp.pad(win_rows, ((0, 0), (WINDOW, 0), (0, 0), (0, 0), (0, 0)))

        def body(i):
            start = i * Q_BLOCK
            qb = lax.dynamic_slice_in_dim(q, start, Q_BLOCK, axis=1)
            wb = lax.dynamic_slice_in_dim(wpad, start, WINDOW + Q_BLOCK, axis=1)
            qpos = pos0 + start + jnp.arange(Q_BLOCK, dtype=jnp.int32)
            wpos = pos0 + start - WINDOW + jnp.arange(WINDOW + Q_BLOCK, dtype=jnp.int32)
            return nsa_block(qb, qpos, kc, vc, kc_end, ks_t, vs_t, wb[:, :, 0], wb[:, :, 1], wpos, rel_bias)

        oc, osl, ow = lax.map(body, jnp.arange(nb, dtype=jnp.int32))
        oc = jnp.swapaxes(oc, 0, 1).reshape(B, T, NSA_HEADS, HEAD_DIM)
        osl = jnp.swapaxes(osl, 0, 1).reshape(B, T, NSA_HEADS, HEAD_DIM)
        ow = jnp.swapaxes(ow, 0, 1).reshape(B, T, NSA_HEADS, HEAD_DIM)
        win_state = win_rows[:, T - min(WINDOW, T):]
    else:
        wb_len = win_kv.shape[1]
        wk = jnp.concatenate([win_kv.astype(win_rows.dtype), win_rows], axis=1)
        wpos = pos0 - wb_len + jnp.arange(wb_len + T, dtype=jnp.int32)
        qpos = pos0 + jnp.arange(T, dtype=jnp.int32)
        oc, osl, ow = nsa_block(q, qpos, kc, vc, kc_end, ks_t, vs_t, wk[:, :, 0], wk[:, :, 1], wpos, rel_bias)
        win_state = win_rows
    g = jax.nn.sigmoid((g_logit + b_gate).astype(f32)).reshape(B, T, 3, NSA_HEADS, 1)
    o = (g[:, :, 0] * oc + g[:, :, 1] * osl + g[:, :, 2] * ow).astype(h.dtype).reshape(B, T, NSA_WIDTH)
    y_nsa = o * jax.nn.silu(z_nsa)
    vf = v.astype(f32)
    mu = jnp.mean(vf, axis=-1, keepdims=True)
    var = jnp.mean(jnp.square(vf - mu), axis=-1, keepdims=True)
    vn = ((vf - mu) * lax.rsqrt(var + EPS) * ln_g.astype(f32) + ln_b.astype(f32)).astype(v.dtype)
    tc = min(T, GMLP_CHUNK)
    nc = T // tc
    wm = jnp.tril(w_sp[:, :tc, :tc])
    vb = vn.reshape(B, nc, tc, GMLP_GROUPS, GMLP_GROUP_DIM)
    mix = jnp.einsum('gij,bnjgd->bnigd', wm, vb) + jnp.transpose(b_sp[:, :tc])[None, None, :, :, None]
    y_g = (u.reshape(B, nc, tc, GMLP_GROUPS, GMLP_GROUP_DIM) * mix).reshape(B, T, GMLP_WIDTH) * jax.nn.silu(z_g)
    out = jnp.einsum('bte,ed->btd', jnp.concatenate([y_nsa, y_g], axis=-1), w_out)
    return out, new_rows, win_state, vn

def mixer_c(h, h0, conv0, w_in, conv_w, conv_b, w_ra, b_ra, w_rx, b_rx, lam, w_out):
    B, T, _ = h.shape
    f32 = jnp.float32
    xb, z = jnp.split(jnp.einsum('btd,de->bte', h, w_in), 2, axis=-1)
    xin = jnp.concatenate([conv0.astype(xb.dtype), xb], axis=1)
    xc = conv_b + xin[:, 0:T] * conv_w[0]
    for k in range(1, CONV_WIDTH):
        xc = xc + xin[:, k:k + T] * conv_w[k]
    xr = xc.reshape(B, T, LRU_HEADS, LRU_BLOCK)
    r = jax.nn.sigmoid((jnp.einsum('bthi,hij->bthj', xr, w_ra).reshape(B, T, LRU_WIDTH) + b_ra).astype(f32))
    ig = jax.nn.sigmoid((jnp.einsum('bthi,hij->bthj', xr, w_rx).reshape(B, T, LRU_WIDTH) + b_rx).astype(f32))
    log_a = -LRU_C * r * jax.nn.softplus(-lam.astype(f32))
    a = jnp.exp(log_a)
    bt = jnp.sqrt(-jnp.expm1(2.0 * log_a)) * ig * xc.astype(f32)

    def step(hc, ab):
        hn = ab[0] * hc + ab[1]
        return hn, hn

    h_last, hs = lax.scan(step, h0.astype(f32), (jnp.swapaxes(a, 0, 1), jnp.swapaxes(bt, 0, 1)))
    y = jnp.swapaxes(hs, 0, 1).astype(h.dtype) * jax.nn.silu(z)
    return jnp.einsum('btw,wd->btd', y, w_out), h_last, xin[:, -(CONV_WIDTH - 1):]

def setup_inputs(seed: int = 0) -> dict:
    key = jax.random.key(seed)
    ks = jax.random.split(key, 32)
    n_pages = PAST_LEN // PAGE_SIZE
    n_pool = (5 * DEC_BATCH * n_pages + 3) // 4

    def nrm(k, shape, scale):
        return jax.random.normal(k, shape, jnp.float32) * scale

    u = jax.random.uniform(ks[25], (N_C_LAYERS, LRU_WIDTH), jnp.float32, minval=0.9, maxval=0.999)
    return {
        'x_prompt': nrm(ks[0], (BATCH, SEQ, D_MODEL), 1.0),
        'x_sample': nrm(ks[1], (DEC_BATCH, DEC_SEQ, D_MODEL), 1.0),
        'cache_nsa': nrm(ks[2], (N_A_LAYERS, n_pool, PAGE_SIZE, 4, NSA_KV_HEADS, HEAD_DIM), 1.0),
        'cache_win': nrm(ks[3], (N_A_LAYERS, DEC_BATCH, min(WINDOW, PAST_LEN), 2, NSA_KV_HEADS, HEAD_DIM), 1.0),
        'state_lru_h': nrm(ks[4], (N_C_LAYERS, DEC_BATCH, LRU_WIDTH), 0.5),
        'state_lru_conv': nrm(ks[5], (N_C_LAYERS, DEC_BATCH, CONV_WIDTH - 1, LRU_WIDTH), 1.0),
        'page_table': jax.random.permutation(ks[6], n_pool)[:DEC_BATCH * n_pages].reshape(DEC_BATCH, n_pages).astype(jnp.int32),
        'norm_a': 1.0 + nrm(ks[7], (N_A_LAYERS, D_MODEL), 0.05),
        'w_in_a': nrm(ks[8], (N_A_LAYERS, D_MODEL, PROJ_A), D_MODEL ** -0.5),
        'b_gate_a': nrm(ks[9], (N_A_LAYERS, 3 * NSA_HEADS), 0.1),
        'pe_cmp': nrm(ks[10], (N_A_LAYERS, 2, CMP_BLOCK, HEAD_DIM), 0.1),
        'w_cmp': nrm(ks[11], (N_A_LAYERS, 2, HEAD_DIM, HEAD_DIM), math.sqrt(CMP_BLOCK / HEAD_DIM)),
        'gmlp_ln_g': 1.0 + nrm(ks[12], (N_A_LAYERS, GMLP_WIDTH), 0.05),
        'gmlp_ln_b': nrm(ks[13], (N_A_LAYERS, GMLP_WIDTH), 0.02),
        'w_spatial': nrm(ks[14], (N_A_LAYERS, GMLP_GROUPS, GMLP_CHUNK, GMLP_CHUNK), GMLP_CHUNK ** -0.5),
        'b_spatial': 1.0 + nrm(ks[15], (N_A_LAYERS, GMLP_GROUPS, GMLP_CHUNK), 0.1),
        'w_out_a': nrm(ks[16], (N_A_LAYERS, OUT_A, D_MODEL), OUT_A ** -0.5),
        'norm_c': 1.0 + nrm(ks[17], (N_C_LAYERS, D_MODEL), 0.05),
        'w_in_c': nrm(ks[18], (N_C_LAYERS, D_MODEL, 2 * LRU_WIDTH), D_MODEL ** -0.5),
        'conv_w': nrm(ks[19], (N_C_LAYERS, CONV_WIDTH, LRU_WIDTH), CONV_WIDTH ** -0.5),
        'conv_b': nrm(ks[20], (N_C_LAYERS, LRU_WIDTH), 0.02),
        'w_rg_a': nrm(ks[21], (N_C_LAYERS, LRU_HEADS, LRU_BLOCK, LRU_BLOCK), LRU_BLOCK ** -0.5),
        'b_rg_a': nrm(ks[22], (N_C_LAYERS, LRU_WIDTH), 0.1),
        'w_rg_x': nrm(ks[23], (N_C_LAYERS, LRU_HEADS, LRU_BLOCK, LRU_BLOCK), LRU_BLOCK ** -0.5),
        'b_rg_x': nrm(ks[24], (N_C_LAYERS, LRU_WIDTH), 0.1),
        'lru_lambda': jnp.log(u) - jnp.log1p(-u),
        'w_out_c': nrm(ks[26], (N_C_LAYERS, LRU_WIDTH, D_MODEL), LRU_WIDTH ** -0.5),
        'rel_bias': nrm(ks[27], (REL_BUCKETS, NSA_HEADS), 0.2),
        'final_norm': 1.0 + nrm(ks[28], (D_MODEL,), 0.05),
    }

def reference(x_prompt, x_sample, cache_nsa, cache_win, state_lru_h, state_lru_conv, page_table,
              norm_a, w_in_a, b_gate_a, pe_cmp, w_cmp, gmlp_ln_g, gmlp_ln_b, w_spatial, b_spatial, w_out_a,
              norm_c, w_in_c, conv_w, conv_b, w_rg_a, b_rg_a, w_rg_x, b_rg_x, lru_lambda, w_out_c,
              rel_bias, final_norm):
    dec_b, n_pages = page_table.shape
    past_len = n_pages * PAGE_SIZE
    bp = x_prompt.shape[0]
    yp, ys = x_prompt, x_sample
    nsa_p, nsa_s, win_p, win_s, gv_s = [], [], [], [], []
    h_p, h_s, cv_p, cv_s = [], [], [], []
    for layer in range(DEPTH):
        if layer % 2 == 0:
            a = layer // 2
            op, rows_p, wp, _ = mixer_ab(rms_norm(yp, norm_a[a]), 0, None, None,
                                         w_in_a[a], b_gate_a[a], pe_cmp[a], w_cmp[a], gmlp_ln_g[a], gmlp_ln_b[a],
                                         w_spatial[a], b_spatial[a], w_out_a[a], rel_bias)
            past = cache_nsa[a][page_table].reshape(dec_b, past_len, 4, NSA_KV_HEADS, HEAD_DIM)
            os_, rows_s, ws, vn_s = mixer_ab(rms_norm(ys, norm_a[a]), past_len, past, cache_win[a],
                                             w_in_a[a], b_gate_a[a], pe_cmp[a], w_cmp[a], gmlp_ln_g[a], gmlp_ln_b[a],
                                             w_spatial[a], b_spatial[a], w_out_a[a], rel_bias)
            nsa_p.append(rows_p); nsa_s.append(rows_s); win_p.append(wp); win_s.append(ws); gv_s.append(vn_s)
        else:
            c = layer // 2
            op, hp_, cp_ = mixer_c(rms_norm(yp, norm_c[c]), jnp.zeros((bp, LRU_WIDTH), jnp.float32),
                                   jnp.zeros((bp, CONV_WIDTH - 1, LRU_WIDTH), yp.dtype),
                                   w_in_c[c], conv_w[c], conv_b[c], w_rg_a[c], b_rg_a[c], w_rg_x[c], b_rg_x[c],
                                   lru_lambda[c], w_out_c[c])
            os_, hs_, cs_ = mixer_c(rms_norm(ys, norm_c[c]), state_lru_h[c], state_lru_conv[c],
                                    w_in_c[c], conv_w[c], conv_b[c], w_rg_a[c], b_rg_a[c], w_rg_x[c], b_rg_x[c],
                                    lru_lambda[c], w_out_c[c])
            h_p.append(hp_); h_s.append(hs_); cv_p.append(cp_); cv_s.append(cs_)
        yp = yp + op
        ys = ys + os_
    y_prompt = rms_norm(yp, final_norm)
    y_sample = rms_norm(ys, final_norm)
    return (y_prompt, y_sample, jnp.stack(nsa_p), jnp.stack(nsa_s), jnp.stack(win_p), jnp.stack(win_s),
            jnp.stack(gv_s), jnp.stack(h_p), jnp.stack(h_s), jnp.stack(cv_p), jnp.stack(cv_s))


_drawn_inputs = setup_inputs


def setup_inputs(seed=0):
    import zlib

    import numpy as np

    out = dict(_drawn_inputs(seed))
    spreads = {}
    factors = {'b_gate_a': 8.0, 'gmlp_ln_b': 2.872}
    for name, (base, spread) in spreads.items():
        noise = np.random.default_rng([zlib.crc32(name.encode()), seed]).standard_normal(out[name].shape)
        drawn = base * np.exp(spread * noise) if base else spread * noise
        out[name] = __import__('jax').numpy.asarray(drawn.astype(out[name].dtype))
    for name, factor in factors.items():
        out[name] = (out[name] * factor).astype(out[name].dtype)
    return out
```

```python
import math
from contextlib import ExitStack

import concourse.bass as bass
from concourse import mybir
import numpy as np

ALU = mybir.AluOpType
ACT = mybir.ActivationFunctionType
AX = mybir.AxisListType
F32 = mybir.dt.float32

P = 128
D = 1024
KC = D // P
SEQ = 1024
NSEQ, NNEW = 8, 4
NS = NSEQ * NNEW
TOK = SEQ + NS
TILES = SEQ // P + 1
PT = SEQ // P
THIRD = TOK // 3
HEADS, KVH, HD = 8, 2, 64
HPG = HEADS // KVH
KV = 6 * KVH * HD
NG = 3 * HEADS
KVG = KV + NG
BLK = 64
NB = SEQ // BLK
WIN = 512
WCOLS = WIN + P
PAST = 256
PAGE = 128
NBP = PAST // BLK
BUCKETS, MAX_DIST = 32, 1024
REL = SEQ + P
REL_TOP = SEQ - 1
BIG = 1e30
EPS = 1e-6
Q0, KV0, G0, Z0 = 0, 512, 512 + KV, 512 + KV + NG
U0, V0, ZG0 = Z0 + 512, Z0 + 1024, Z0 + 1536
HALF = NSEQ // 2
SROWS = HALF * HEADS * NNEW
VEC = {"norm_a": 0, "norm_c": 8, "conv_w": 16, "conv_b": 48, "b_rg_a": 56, "b_rg_x": 64, "lru_lambda": 72}
NVEC = 80


def rows(i):
    return P if i < PT else NS


def tok(i):
    return slice(i * P, i * P + rows(i))


def constants():
    c = {}
    d = np.arange(REL_TOP, REL_TOP - REL, -1)
    exact = BUCKETS // 2
    df = np.maximum(d, 1).astype(np.float32)
    large = exact + (np.log(df / np.float32(exact)) / np.float32(math.log(MAX_DIST / exact))
                     * np.float32(BUCKETS - exact)).astype(np.int32)
    bucket = np.where(d < exact, d, np.minimum(large, BUCKETS - 1))
    hot = np.zeros((BUCKETS + 1, REL), np.float32)
    hot[bucket[d >= 0], np.nonzero(d >= 0)[0]] = -1.0
    hot[BUCKETS, d < 0] = 1.0
    c["c_hot"] = hot
    k = np.arange(P)
    c["c_ident"] = np.eye(P, dtype=np.float32)
    c["c_tril"] = (k[:, None] <= k[None, :]).astype(np.float32)
    c["c_far"] = np.where(k[None, :] < k[:, None], BIG, 0.0).astype(np.float32)
    c["c_avg"] = ((k[:, None] // BLK == np.arange(2)[None, :]) / BLK).astype(np.float32)
    c["c_rowok"] = (k[:, None] >= BLK - 1).astype(np.float32)
    c["c_headrow"] = (k[:, None] // NB == np.arange(HEADS)[None, :]).astype(np.float32)
    r = np.arange(SROWS)
    s, h, t = r // (HEADS * NNEW), r // NNEW % HEADS, r % NNEW
    c["c_hsel"] = (h[:, None] == np.arange(HEADS)[None, :]).astype(np.float32)
    n = np.arange(NS)
    c["c_tsel"] = np.concatenate(
        [(n[:, None] == ((HALF * f + s) * NNEW + t)[None, :]) for f in range(2)], 1).astype(np.float32)
    c["c_tril_s"] = ((n[:, None] // NNEW == n[None, :] // NNEW)
                     & (n[:, None] % NNEW <= n[None, :] % NNEW)).astype(np.float32)
    return c


def attention_units():
    units = []
    for i in range(PT):
        units.append(("c", i, 0))
        for h in range(HEADS):
            units += [("s", i, h), ("w", i, h)]
    return units


def key_cols(kind, i):
    if kind == "c":
        return 2 * i + 2, 0
    first = 0 if kind == "s" else max(0, i - WIN // P)
    return (i + 1 - first) * P, first * P


def attention_steps():
    units = attention_units()
    steps = []
    per = 1 + 2 * HEADS
    for n in range(len(units) + 2):
        if n < len(units):
            steps.append(("scores", n))
        if n >= 2:
            steps.append(("values", n - 2))
        if 1 <= n <= len(units):
            steps.append(("turn", n - 1))
        m = n - 2 - 3
        if m >= per - 1 and (m + 1) % per == 0:
            steps.append(("out", (m + 1) // per - 1))
    steps.append(("out", PT - 1))
    return steps


def chunk_plan():
    units, plan, done = attention_units(), [], {"act": 0, "dve": 0}
    for what, n in attention_steps():
        if what == "turn":
            kind, i, _ = units[n]
            cols = P if kind == "c" else key_cols(kind, i)[0]
            for a in range(0, cols, 512):
                plan.append((what, n, a, min(512, cols - a), "act" if kind == "s" else "dve"))
        elif what == "values" and units[n][0] == "c":
            plan.append((what, n, 0, 512, "dve"))
        elif what == "out":
            plan.append((what, n, 0, 512, "dve"))
    out = []
    for what, n, a, w, who in plan:
        done[who] += 1
        out.append((what, n, a, w, who, done[who]))
    return out


FM_A = ([("z", j, "act") for j in range(4)]
        + [x for j in range(4) for x in (("zg", j, "act"), ("u", j, "dve"))]
        + [("q", j, "dve") for j in range(4)])


def build(nc, ins, outs):
    ctx = ExitStack()
    with ctx:
        def sb(name, shape):
            return ctx.enter_context(nc.sbuf_tensor(name, shape, F32))

        def sem(name):
            return ctx.enter_context(nc.semaphore(name))

        ps = ctx.enter_context(nc.psum_tensor("ps", [P, 8, 512], F32))
        flat = ps[:, :, :].rearrange("p b n -> p (b n)")
        region_y = sb("region_y", [P, 8 * TOK])
        region_q = sb("region_q", [P, 8640])
        region_w = sb("region_w", [P, 27904])

        def view(region, at, *shape):
            n = int(np.prod(shape))
            v = region[:, at:at + n]
            if len(shape) == 2:
                v = v.rearrange("p (a b) -> p a b", a=shape[0])
            if len(shape) == 3:
                v = v.rearrange("p (a b c) -> p a b c", a=shape[0], b=shape[1])
            return v

        w_kvg = view(region_y, 0, KC, KVG)
        yT = view(region_y, 0, 8, TOK)
        hot = view(region_q, 0, REL)
        rel_rows = view(region_q, REL, REL)
        wsp_in = view(region_q, 2 * REL, 4, P)
        vec_in = view(region_q, 2 * REL + 512, P)
        state_in = view(region_q, 2 * REL + 640, D)
        pe_in = view(region_q, 2 * REL + 640 + D, 2, P)
        qT = view(region_q, 0, HPG, TOK)
        kT_s = view(region_q, 4 * TOK, TOK)
        kT_w = view(region_q, 5 * TOK, TOK)
        v_s = view(region_q, 6 * TOK, TILES, P)
        v_w = view(region_q, 6 * TOK + TILES * P, TILES, P)
        h1T = view(region_q, 0, KC, TOK)
        hT = view(region_w, 0, KC, TOK)
        w_v = view(region_w, 8448, KC, 512)
        w_fm = [view(region_w, 12544 + D * j, KC, P) for j in range(4)]
        vn = view(region_w, 16640, TILES, 512)
        kv_row = [view(region_w, 21248 + KVG * j, KVG) for j in range(2)]
        x_row = [view(region_w, 22832 + D * j, D) for j in range(3)]
        junk = view(region_w, 25904, D)
        bias = view(region_w, 0, HEADS, SEQ)
        bias_w = view(region_w, 8192, HEADS, WCOLS)
        logits = [view(region_w, 13312 + D * j, D) for j in range(2)]
        probT = [view(region_w, 15360 + D * j, D) for j in range(2)]
        ls_s = view(region_w, 17408, PAST + NS)
        ls_w = view(region_w, 17696, PAST + NS)
        ls_c = view(region_w, 17984, 16)
        pt_s = view(region_w, 18000, 3, P)
        pt_w = view(region_w, 18384, 3, P)
        pt_c = view(region_w, 18768, P)
        res_s = view(region_w, 18896, P)
        mean_s = view(region_w, 19024, 2, 16)
        kc_s = view(region_w, 19056, 16)
        vc_s = view(region_w, 19072, P)
        gate_rows = view(region_w, 19200, 3, HEADS)
        coef_s = view(region_w, 19224, 3)
        coef_g = view(region_w, 19227, 3)
        sum_s = view(region_w, 19230, 3)
        neg_s = view(region_w, 19233, 3)
        pages = view(region_w, 19456, 2 * HALF, 512)
        wins = view(region_w, 23552, 2 * HALF, 256)
        kTc_s = view(region_w, 25600, 2 * HALF * P)
        kTc_w = view(region_w, 26624, 2 * HALF * P)
        w_outa = view(region_w, 0, KC, D)
        x_again = [view(region_w, 8192 + D * j, D) for j in range(2)]
        x1 = view(region_w, 10496, TILES, D)
        h1 = [view(region_w, 19712 + D * j, D) for j in range(2)]
        w_c = [view(region_w, D * j, KC, P) for j in range(3)]
        xin = view(region_w, 3072, 3 + SEQ)
        xin_s = view(region_w, 3072 + 1027, NSEQ, 7)
        xc = [view(region_w, 4160 + TOK * j, TOK) for j in range(2)]
        r_buf = view(region_w, 6272, TOK)
        t_buf = view(region_w, 7328, TOK)
        e_buf = view(region_w, 8384, TOK)
        ig_buf = view(region_w, 9440, TOK)
        w_outc = view(region_w, 19712, KC, D)
        sz_buf = [r_buf, ig_buf]
        y_row = [view(region_w, D * j, D) for j in range(2)]

        ident = sb("ident", [P, P])
        tril = sb("tril", [P, P])
        far = sb("far", [P, P])
        avg = sb("avg", [P, 2])
        rowok = sb("rowok", [P, 1])
        headrow = sb("headrow", [P, HEADS])
        hsel = sb("hsel", [P, HEADS])
        tsel = sb("tsel", [NS, 2 * SROWS])
        tril_s = sb("tril_s", [NS, NS])
        rel_in = sb("rel_in", [BUCKETS + 1, HEADS])
        vecT = sb("vecT", [P, NVEC])
        region_m = sb("region_m", [P, 1024])
        wspT = view(region_m, 0, 4, P)
        b_sp = view(region_m, 512, 4, P)
        aS = view(region_m, 0, KC, NSEQ, NNEW + 1)
        bS = view(region_m, 320, KC, NSEQ, NNEW + 1)
        small_out = view(region_m, 640, KC, 36)
        region_g = sb("region_g", [P, D])
        ln_g = region_g[:, 0:512]
        ln_b = region_g[:, 512:1024]
        fin_g = region_g
        wspT_s = sb("wspT_s", [NS, 4, NS])
        b_gate = sb("b_gate", [P, NG])
        wc_k = sb("wc_k", [P, P])
        wc_v = sb("wc_v", [P, P])
        pe_mean = sb("pe_mean", [P, 2])
        mean_p = sb("mean_p", [P, 2, NB])
        mean_rep = sb("mean_rep", [P, HEADS, NB])
        kc_bd = sb("kc_bd", [P, KVH, NB])
        vc_bd = sb("vc_bd", [P, KVH, HPG, HD])
        gates = sb("gates", [P, TILES, NG])
        half_neg = sb("half_neg", [P, 1])
        ss = sb("ss", [P, 3, TILES])
        ms = sb("ms", [P, 3, TILES])
        rstd = sb("rstd", [P, 3, TILES])
        bn = sb("bn", [P, 6])
        mv = sb("mv", [P, TILES, 2])
        mv_e = sb("mv_e", [P, TILES])
        rstd_v = sb("rstd_v", [P, TILES])
        negm = sb("negm", [P, 4])
        sums = sb("sums", [P, 2, 3, HEADS])
        inv = sb("inv", [P, 3, HEADS])
        coef = sb("coef", [P, 3, HEADS])
        lc = sb("lc", [P, HEADS, NB])
        lmin = sb("lmin", [P, HEADS])
        acc = sb("acc", [P, 512])
        acc_c = sb("acc_c", [P, 512])
        part_sb = sb("part_sb", [P, 512])
        part_2 = sb("part_2", [P, 512])
        parts = [part_sb, part_2]
        bias_c = sb("bias_c", [P, PAST])
        bias_n = sb("bias_n", [P, 2, NS])
        bias_b = sb("bias_b", [P, 16])
        qbd = sb("qbd", [P, NSEQ, KVH, HPG, NNEW])
        stT = sb("stT", [P, KC, NS])
        lam = sb("lam", [P, 6, KC])
        pt_tab = sb("pt_tab", [1, NSEQ * 2])
        pt_tab = pt_tab[:, :].bitcast(mybir.dt.int32)

        rel_dram = nc.dram_tensor("rel_rows_dram", (HEADS, P * (REL + 1)), F32, kind="Internal").ap()

        def rel_skewed(first_head, heads, shifts, at, n):
            dims = [[P * (REL + 1), heads], [REL, shifts], [1, n]]
            return bass.AP(rel_dram.tensor, first_head * P * (REL + 1) + at, dims)

        zeroed = sem("zeroed")
        consts_in = sem("consts_in")
        diag_in = sem("diag_in")
        x_in = [sem(f"x_in{j}") for j in range(3)]
        kvg_in = sem("kvg_in")
        wv_in = sem("wv_in")
        fmw_in = [sem(f"fmw_in{j}") for j in range(4)]
        prep_pe = sem("prep_pe")
        prep_dve = sem("prep_dve")
        rel_out = sem("rel_out")
        squared = sem("squared")
        scaled = sem("scaled")
        normed = sem("normed")
        x_turned = sem("x_turned")
        hT_ready = sem("hT_ready")
        kvA_done = sem("kvA_done")
        v_done = sem("v_done")
        kvA_out = sem("kvA_out")
        v_out = sem("v_out")
        kvB_out = sem("kvB_out")
        k_turned = sem("k_turned")
        kT_ready = sem("kT_ready")
        rows_out = [sem(f"rows_out{j}") for j in range(2)]
        ln_stats = sem("ln_stats")
        ln_scaled = sem("ln_scaled")
        ln_mid = sem("ln_mid")
        vn_ready = sem("vn_ready")
        vn_out = sem("vn_out")
        fm_done = sem("fm_done")
        fm_act = sem("fm_act")
        fm_dve = sem("fm_dve")
        cmp_rep = sem("cmp_rep")
        cmp_pe = sem("cmp_pe")
        cmp_ready = sem("cmp_ready")
        mix_done = sem("mix_done")
        mix_used = sem("mix_used")
        gates_ready = sem("gates_ready")
        bias_in = sem("bias_in")
        biasw_ready = sem("biasw_ready")
        bias_s_in = sem("bias_s_in")
        scores_done = sem("scores_done")
        logits_ready = sem("logits_ready")
        probs_ready = sem("probs_ready")
        turned = sem("turned")
        chunk_act = sem("chunk_act")
        chunk_dve = sem("chunk_dve")
        values_done = sem("values_done")
        o_free = sem("o_free")
        acc_ready = sem("acc_ready")
        samp_in = [sem("samp_in0"), sem("samp_in1")]
        samp_pe = sem("samp_pe")
        samp_q = sem("samp_q")
        samp_dve = sem("samp_dve")
        samp_act = sem("samp_act")
        outa_in = sem("outa_in")
        xa_in = [sem(f"xa_in{j}") for j in range(2)]
        outa_done = sem("outa_done")
        x1_ready = sem("x1_ready")
        h1_ready = sem("h1_ready")
        h1_turned = sem("h1_turned")
        h1T_ready = sem("h1T_ready")
        wc_in = [sem(f"wc_in{j}") for j in range(3)]
        wg_in = sem("wg_in")
        fin_in = sem("fin_in")
        aS_zero = sem("aS_zero")
        lam_exp = sem("lam_exp")
        lam_ready = sem("lam_ready")
        pc_done = sem("pc_done")
        pc_act = sem("pc_act")
        conv_ready = sem("conv_ready")
        ta_ready = sem("ta_ready")
        m_ready = sem("m_ready")
        sq_ready = sem("sq_ready")
        h_ready = sem("h_ready")
        y_ready = sem("y_ready")
        outc_in = sem("outc_in")
        outc_done = sem("outc_done")
        o_ready = sem("o_ready")
        y_row_ready = sem("y_row_ready")
        y_out = [sem(f"y_out{j}") for j in range(2)]
        small_ready = sem("small_ready")
        small_pe = sem("small_pe")
        small_rows = sem("small_rows")
        small_sent = sem("small_sent")
        dve_chain = sem("dve_chain")
        pool_chain = sem("pool_chain")
        act_chain = sem("act_chain")

        w_rg = view(region_w, 19712, 2, KC, P)

        units = attention_units()
        chunks = chunk_plan()
        nchunk = {}
        for k, (what, n, a, w, who, m) in enumerate(chunks):
            nchunk.setdefault((what, n), []).append(k)

        def spread(ap, n, axis=2):
            x = ap.unsqueeze(axis)
            shape = list(x.shape)
            shape[axis] = n
            return x.to_broadcast(shape)

        def chunk_wait(eng, k):
            if k >= 2:
                who, m = chunks[k - 2][4:6]
                eng.wait_ge(chunk_act if who == "act" else chunk_dve, m)

        fm_count = []
        counts = {"act": 0, "dve": 0}
        for _, _, who in FM_A:
            counts[who] += 1
            fm_count.append(counts[who])

        def fm_wait(eng, n):
            eng.wait_ge(fm_act if FM_A[n][2] == "act" else fm_dve, fm_count[n])

        order_c = []
        for c in range(KC + 1):
            if c < KC:
                order_c.append(("x", c))
            if c >= 1:
                order_c += [("r", c - 1), ("i", c - 1)]
        order_c += [("z", c) for c in range(KC)]
        order_c_at = {x: n for n, x in enumerate(order_c)}

        def pc_of(n):
            if n == KC:
                return order_c_at[("z", 0)] + 1
            return order_c_at[("x", n) if n < KC else ("z", n - KC)] + 1

        small_tm = view(region_w, 3072, D)

        def sent_rows(i):
            return sum(2 if j >= (SEQ - WIN) // P else 1 for j in range(i % 2, i, 2))

        SAMP_DVE = ["keys0", "keys1", "means", "cmp", "logits", "probT", "res", "out"]
        SAMP_PE = ["keys0", "keys1", "cmp", "scores", "turned", "values", "out"]

        def samp_at(step, f):
            return f * len(SAMP_DVE) + SAMP_DVE.index(step) + 1

        def samp_pe_at(step, f):
            return f * len(SAMP_PE) + SAMP_PE.index(step) + 1

        block = ctx.enter_context(nc.Block())
        w_in_k = ins["w_in_a"][0].rearrange("(k p) n -> p k n", p=P)
        w_inc_k = ins["w_in_c"][0].rearrange("(k p) n -> p k n", p=P)
        hot_h = [(ident, "c_ident"), (tril, "c_tril"), (far, "c_far"), (avg, "c_avg"), (rowok, "c_rowok"),
                 (headrow, "c_headrow"), (hsel, "c_hsel"), (tsel, "c_tsel"), (tril_s, "c_tril_s")]
        const_loads = [(t[:, :], ins[n]) for t, n in hot_h]
        const_loads += [(hot[0:BUCKETS + 1, :], ins["c_hot"])]
        const_loads += [(vec_in[VEC[n]:VEC[n] + 8, :], ins[n][0].rearrange("(k p) -> k p", p=P))
                        for n in ("norm_a", "norm_c", "conv_b", "b_rg_a", "b_rg_x", "lru_lambda")]
        const_loads += [(vec_in[16:48, :], ins["conv_w"][0].rearrange("t (k p) -> (t k) p", p=P))]
        const_loads += [(wsp_in, ins["w_spatial"][0].rearrange("g i j -> i g j"))]
        const_loads += [(state_in[0:24, :], ins["state_lru_conv"][0].rearrange("s k c -> (s k) c")),
                        (state_in[24:32, :], ins["state_lru_h"][0])]
        const_loads += [(pe_in[0:BLK, kind, g * HD:(g + 1) * HD], ins["pe_cmp"][0, kind])
                        for kind in range(2) for g in range(2)]
        const_loads += [(b_sp[:, :, :], ins["b_spatial"][0].partition_broadcast(P)),
                        (ln_g, ins["gmlp_ln_g"][0].partition_broadcast(P)),
                        (ln_b, ins["gmlp_ln_b"][0].partition_broadcast(P)),
                        (b_gate[:, :], ins["b_gate_a"][0].partition_broadcast(P)),
                        (pt_tab, ins["page_table"].rearrange("s j -> (s j)").rearrange("(a n) -> a n", a=1)),
                        (rel_in[0:BUCKETS, :], ins["rel_bias"])]
        NCONST = 16 * len(const_loads)

        @block.sync
        def _(sp):
            def load_x(i):
                if i >= 3:
                    sp.wait_ge(x_turned, i - 2)
                src = ins["x_prompt"][0, tok(i), :] if i < PT else ins["x_sample"].rearrange("s t d -> (s t) d")
                sp.dma_start(x_row[i % 3][0:rows(i), :], src).then_inc(x_in[i % 3], 16)

            load_x(0)
            load_x(1)
            for k in range(0, KC, 4):
                sp.dma_start(w_kvg[:, k:k + 4, :], w_in_k[:, k:k + 4, KV0:KV0 + KVG]).then_inc(kvg_in, 16)
            load_x(2)
            for k in range(0, KC, 4):
                sp.dma_start(w_v[:, k:k + 4, :], w_in_k[:, k:k + 4, V0:V0 + 512]).then_inc(wv_in, 16)

            def load_fm(n):
                kind, j, _ = FM_A[n]
                if n >= 4:
                    sp.wait_ge(fm_done, n - 3)
                dst, s = w_fm[n % 4], fmw_in[n % 4]
                if kind == "q":
                    for g in range(2):
                        c0 = Q0 + (g * HPG + j) * HD
                        sp.dma_start(dst[:, :, g * HD:(g + 1) * HD], w_in_k[:, :, c0:c0 + HD]).then_inc(s, 16)
                else:
                    c0 = {"z": Z0, "zg": ZG0, "u": U0}[kind] + j * P
                    sp.dma_start(dst, w_in_k[:, :, c0:c0 + P]).then_inc(s, 16)

            for i in range(3, TILES):
                load_x(i)
            for n in range(len(FM_A)):
                load_fm(n)
            sp.wait_ge(rel_out, 16 * HEADS)
            sp.wait_ge(fm_done, len(FM_A))
            for h in range(HEADS):
                sp.dma_start(bias[:, h, :], rel_skewed(h, 1, P, P - 1, SEQ)).then_inc(bias_in, 16)

            def load_outa():
                sp.wait_ge(logits_ready, len(units))
                for k in range(0, KC, 4):
                    sp.dma_start(w_outa[:, k:k + 4, :],
                                 ins["w_out_a"][0].rearrange("(k p) n -> p k n", p=P)[:, k:k + 4, :]
                                 ).then_inc(outa_in, 16)

            for f in range(2):
                if f == 0:
                    sp.wait_ge(mix_used, TILES)
                    sp.wait_ge(vn_out, 16)
                    sp.wait_ge(rows_out[0], 16 * 8)
                    sp.wait_ge(rows_out[1], 16 * 6)
                    sp.wait_ge(consts_in, NCONST)
                else:
                    load_outa()
                    sp.wait_ge(samp_pe, 6)
                for j in range(2 * HALF):
                    at = f * 2 * HALF + j
                    page = sp.value_load(pt_tab[0:1, at:at + 1], min_val=0,
                                         max_val=ins["cache_nsa"].shape[1] - 1)
                    sp.dma_start(pages[:, j, :],
                                 ins["cache_nsa"][0, bass.ds(page, 1), :, :, :, :].rearrange(
                                     "a t k g d -> (a t) (k g d)")).then_inc(samp_in[f], 16)
                for s in range(HALF):
                    sp.dma_start(wins[:, 2 * s:2 * s + 2, :],
                                 ins["cache_win"][0, f * HALF + s].rearrange(
                                     "(j t) k g d -> t j (k g d)", t=P)).then_inc(samp_in[f], 16)

            for i in range(TILES):
                if i >= 2:
                    sp.wait_ge(x1_ready, i - 1)
                src = ins["x_prompt"][0, tok(i), :] if i < PT else ins["x_sample"].rearrange("s t d -> (s t) d")
                sp.dma_start(x_again[i % 2][0:rows(i), :], src).then_inc(xa_in[i % 2], 16)

            sp.dma_start(fin_g[:, :], ins["final_norm"].partition_broadcast(P)).then_inc(fin_in, 16)

            for n in range(2 * KC):
                if n == 0:
                    sp.wait_ge(outa_done, TILES)
                if n >= 3:
                    sp.wait_ge(pc_done, pc_of(n - 3))
                sp.dma_start(w_c[n % 3], w_inc_k[:, :, n * P:(n + 1) * P]).then_inc(wc_in[n % 3], 16)
                if n == 0:
                    sp.wait_ge(h1_turned, TILES)
                    for m, name in enumerate(("w_rg_a", "w_rg_x")):
                        sp.dma_start(w_rg[:, m], ins[name][0].rearrange("c i j -> i c j")).then_inc(wg_in, 16)
            sp.wait_ge(pc_done, pc_of(KC))
            for k in range(0, KC, 4):
                sp.dma_start(w_outc[:, k:k + 4, :],
                             ins["w_out_c"][0].rearrange("(k p) n -> p k n", p=P)[:, k:k + 4, :]
                             ).then_inc(outc_in, 16)

            sp.wait_ge(small_rows, 1)
            so = small_tm
            sp.dma_start(outs["lru_h_sample"][0], so[0:8, :]).then_inc(small_sent, 16)
            sp.dma_start(outs["lru_conv_sample"][0].rearrange("s k c -> (s k) c"), so[8:32, :]
                         ).then_inc(small_sent, 16)
            sp.dma_start(outs["lru_h_prompt"][0], so[32:33, :]).then_inc(small_sent, 16)
            sp.dma_start(outs["lru_conv_prompt"][0, 0], so[33:36, :]).then_inc(small_sent, 16)
            for i in range(TILES):
                sp.wait_ge(y_row_ready, i + 1)
                dst = outs["y_prompt"][0, tok(i), :] if i < PT else outs["y_sample"].rearrange("s t d -> (s t) d")
                sp.dma_start(dst, y_row[i % 2][0:rows(i), :]).then_inc(y_out[i % 2], 16)
            sp.wait_ge(small_sent, 64)
            sp.wait_ge(y_out[0], 16 * 5)
            sp.wait_ge(y_out[1], 16 * 4)

        @block.gpsimd
        def _(pool):
            pool.memset(rel_in[:, :], BIG).then_inc(zeroed, 1)
            pool.memset(wc_k[:, :], 0.0).then_inc(zeroed, 1)
            pool.memset(wc_v[:, :], 0.0).then_inc(zeroed, 1)
            pool.memset(wspT_s[:, :, :], 0.0).then_inc(zeroed, 1)
            pool.memset(half_neg[:, :], -0.5).then_inc(zeroed, 1)
            pool.memset(lc[:, :, :], 0.0).then_inc(zeroed, 1)
            pool.memset(kc_bd[:, :, :], 0.0).then_inc(zeroed, 1)
            pool.memset(qbd[:, :, :, :, :], 0.0).then_inc(zeroed, 1)
            pool.memset(bias_n[:, :, :], BIG).then_inc(zeroed, 1)
            pool.memset(bias_b[:, :], BIG).then_inc(zeroed, 1)
            pool.wait_ge(zeroed, 10)
            for kind, t in ((0, wc_k), (1, wc_v)):
                for g in range(2):
                    pool.dma_start(t[g * HD:(g + 1) * HD, g * HD:(g + 1) * HD], ins["w_cmp"][0, kind]
                                   ).then_inc(diag_in, 16)
            corner = ins["w_spatial"][0, :, 0:NNEW, 0:NNEW]
            with nc.allow_non_contiguous_dma("4 x 4 corners of the spatial weights"):
                for g in range(4):
                    for s in range(NSEQ):
                        pool.dma_start(wspT_s[s * NNEW:(s + 1) * NNEW, g, s * NNEW:(s + 1) * NNEW],
                                       corner[g].rearrange("i j -> j i")).then_inc(diag_in, 16)

            rms_chain = [0]

            def rms(norm, i, want):
                r = rows(i)
                pool.wait_ge(squared, want)
                pool.tensor_scalar(ms[0:r, norm, i:i + 1], ss[0:r, norm, i:i + 1], 1.0 / D, EPS,
                                   ALU.mult, ALU.add).then_inc(pool_chain, 1)
                rms_chain[0] += 1
                pool.wait_ge(pool_chain, rms_chain[0])
                pool.tensor_tensor(rstd[0:r, norm, i:i + 1], ms[0:r, norm, i:i + 1], half_neg[0:r, :],
                                   ALU.pow).then_inc(scaled, 1)

            def ln(i):
                r = rows(i)
                pool.wait_ge(ln_stats, i + 1)
                pool.tensor_scalar(mv_e[0:r, i:i + 1], mv[0:r, i, 1:2], EPS, None, ALU.add
                                   ).then_inc(pool_chain, 1)
                rms_chain[0] += 1
                pool.wait_ge(pool_chain, rms_chain[0])
                pool.tensor_tensor(rstd_v[0:r, i:i + 1], mv_e[0:r, i:i + 1], half_neg[0:r, :],
                                   ALU.pow).then_inc(ln_scaled, 1)

            def ln_affine(i):
                r = rows(i)
                pool.wait_ge(ln_mid, i + 1)
                pool.wait_ge(consts_in, NCONST)
                pool.tensor_tensor(vn[0:r, i, :], vn[0:r, i, :], ln_g[0:r, :], ALU.mult).then_inc(pool_chain, 1)
                rms_chain[0] += 1
                pool.wait_ge(pool_chain, rms_chain[0])
                pool.tensor_tensor(vn[0:r, i, :], vn[0:r, i, :], ln_b[0:r, :], ALU.add).then_inc(vn_ready, 1)

            def send_rows(i):
                pool.wait_ge(kvA_out, i + 1)
                pool.wait_ge(kvB_out, i + 1)
                src = kv_row[i % 2]
                if i < PT:
                    pool.dma_start(outs["nsa_rows_prompt"][0, 0, tok(i)].rearrange("t k g d -> t (k g d)"),
                                   src[:, 0:512]).then_inc(rows_out[i % 2], 16)
                    if i >= (SEQ - WIN) // P:
                        at = i * P - (SEQ - WIN)
                        pool.dma_start(outs["win_rows_prompt"][0, 0, at:at + P].rearrange("t k g d -> t (k g d)"),
                                       src[:, 512:768]).then_inc(rows_out[i % 2], 16)
                else:
                    pool.dma_start(outs["nsa_rows_sample"][0].rearrange("s t k g d -> (s t) (k g d)"),
                                   src[0:NS, 0:512]).then_inc(rows_out[i % 2], 16)
                    pool.dma_start(outs["win_rows_sample"][0].rearrange("s t k g d -> (s t) (k g d)"),
                                   src[0:NS, 512:768]).then_inc(rows_out[i % 2], 16)

            rms(0, 0, 1)
            rms(0, 1, 2)
            pool.wait_ge(prep_dve, 1)
            for h in range(HEADS):
                pool.dma_start(bass.AP(rel_dram.tensor, h * P * (REL + 1), [[REL, 1], [REL + 1, P], [1, REL]]),
                               spread(rel_rows[h:h + 1, :], P, 1)).then_inc(rel_out, 16)
            for i in range(TILES):
                if i + 2 < TILES:
                    rms(0, i + 2, i + 3)
                if i >= 1:
                    ln(i - 1)
                    ln_affine(i - 1)
                send_rows(i)
            ln(TILES - 1)
            ln_affine(TILES - 1)
            pool.wait_ge(vn_ready, TILES)
            pool.dma_start(outs["gmlp_v_sample"][0].rearrange("s t c -> (s t) c"), vn[0:NS, PT, :]
                           ).then_inc(vn_out, 16)
            pool.wait_ge(rel_out, 16 * HEADS)
            for s in range(HALF):
                o = 32 * s
                pool.dma_start(bias_c[o:o + 32, :],
                               rel_skewed(0, HEADS, NNEW, REL_TOP - PAST, PAST)
                               ).then_inc(bias_s_in, 16)
                for f in range(2):
                    c0 = (f * HALF + s) * NNEW
                    pool.dma_start(bias_n[o:o + 32, f, c0:c0 + NNEW],
                                   rel_skewed(0, HEADS, NNEW, REL_TOP, NNEW)
                                   ).then_inc(bias_s_in, 16)
            pool.wait_ge(mix_used, TILES)
            pool.memset(aS, 0.0).then_inc(aS_zero, 1)
            for i in range(TILES):
                rms(1, i, TILES + i + 1)
            for i in range(TILES):
                rms(2, i, 2 * TILES + i + 1)
            pool.wait_ge(vn_out, 16)
            pool.wait_ge(rows_out[0], 16 * 8)
            pool.wait_ge(rows_out[1], 16 * 6)

        @block.scalar
        def _(act):
            with nc.allow_non_contiguous_dma("small vectors"):
                for n, (dst, src) in enumerate(const_loads):
                    if n == len(const_loads) - 1:
                        act.wait_ge(zeroed, 1)
                    act.dma_start(dst, src).then_inc(consts_in, 16)
            def square(i):
                act.wait_ge(x_in[i % 3], 16 * (i // 3 + 1))
                if i >= 1:
                    act.wait_ge(squared, i)
                r = rows(i)
                nc.scalar.activation(junk[0:r, :], x_row[i % 3][0:r, :], ACT.Square,
                                     accum_out=ss[0:r, 0, i:i + 1]).then_inc(squared, 1)

            square(0)
            square(1)
            for i in range(TILES):
                r = rows(i)
                if i + 2 < TILES:
                    square(i + 2)
                act.wait_ge(kvA_done, i + 1)
                if i >= 2:
                    n = i % 2
                    act.wait_ge(rows_out[n], 16 * sent_rows(i))
                    act.wait_ge(k_turned, i - 1)
                nc.scalar.copy(kv_row[i % 2][0:r, 0:512], ps[0:r, 0, :])
                nc.scalar.copy(v_s[0:r, i, :], ps[0:r, 0, 384:512]).then_inc(kvA_out, 1)
                act.wait_ge(v_done, i + 1)
                nc.scalar.copy(vn[0:r, i, :], ps[0:r, 2, :]).then_inc(v_out, 1)

            for n, (kind, j, who) in enumerate(FM_A):
                if who != "act":
                    continue
                act.wait_ge(fm_done, n + 1)
                dst = yT[:, j if kind == "z" else 4 + j, :].rearrange("p (a b) -> p a b", a=3)
                nc.scalar.activation(dst, ps[:, 3 * (n % 2):3 * (n % 2) + 3, 0:THIRD], ACT.Silu
                                     ).then_inc(fm_act, 1)
            act.wait_ge(kvB_out, TILES)
            nc.scalar.activation(gates[:, 0:PT, :], gates[:, 0:PT, :], ACT.Sigmoid)
            nc.scalar.activation(gates[0:NS, PT, :], gates[0:NS, PT, :], ACT.Sigmoid).then_inc(gates_ready, 1)

            for step, (what, n) in enumerate(attention_steps()):
                if what == "scores":
                    kind, i, h = units[n]
                    cols, _ = key_cols(kind, i)
                    act.wait_ge(logits_ready, n + 1)
                    if kind == "c":
                        nc.scalar.activation(lc[:, :, 0:cols], lc[:, :, 0:cols], ACT.Exp, scale=-1.0
                                             ).then_inc(probs_ready, 1)
                    else:
                        buf = logits[n % 2][:, 0:cols]
                        b = 1 if kind == "s" else 2
                        nc.scalar.activation(buf, buf, ACT.Exp, bias=negm[:, n % 4:n % 4 + 1], scale=-1.0,
                                             accum_out=sums[:, i % 2, b, h:h + 1]).then_inc(probs_ready, 1)
                if what == "turn":
                    for k in nchunk[("turn", n)]:
                        _, _, a, w, who, _ = chunks[k]
                        if who == "act":
                            act.wait_ge(turned, k + 1)
                            nc.scalar.copy(probT[n % 2][:, a:a + w], ps[:, 4 + k % 2, 0:w]).then_inc(chunk_act, 1)

            for f in range(2):
                act.wait_ge(samp_dve, samp_at("logits", f))
                for b, (buf, w) in enumerate(((ls_c, 16), (ls_s, PAST + NS), (ls_w, PAST + NS))):
                    e = nc.scalar.activation(buf[:, 0:w], buf[:, 0:w], ACT.Exp, bias=neg_s[:, b:b + 1],
                                             scale=-1.0, accum_out=sum_s[:, b:b + 1])
                e.then_inc(samp_act, 1)

            for i in range(TILES):
                r = rows(i)
                act.wait_ge(x1_ready, i + 1)
                if i >= 2:
                    act.wait_ge(h1_turned, i - 1)
                nc.scalar.activation(h1[i % 2][0:r, :], x1[0:r, i, :], ACT.Square,
                                     accum_out=ss[0:r, 1, i:i + 1]).then_inc(squared, 1)

            act.wait_ge(lam_ready, 1)
            nc.scalar.activation(lam[:, 1, :], lam[:, 0, :], ACT.Exp, scale=-1.0).then_inc(lam_exp, 1)

            def bank3(n):
                return ps[:, 3 * (n % 2):3 * (n % 2) + 3, 0:THIRD]

            for n, (kind, c) in enumerate(order_c):
                act.wait_ge(pc_done, n + 1)
                if kind == "x":
                    if c >= 1:
                        act.wait_ge(conv_ready, c)
                    b0 = 3 * (n % 2)
                    nc.scalar.copy(xin[:, 3:3 + 2 * THIRD].rearrange("p (a b) -> p a b", a=2),
                                   ps[:, b0:b0 + 2, 0:THIRD])
                    nc.scalar.copy(xin[:, 3 + 2 * THIRD:3 + SEQ], ps[:, b0 + 2, 0:SEQ - 2 * THIRD])
                    nc.scalar.copy(xin_s[:, :, 3:7],
                                   ps[:, b0 + 2, SEQ - 2 * THIRD:THIRD].rearrange("p (s t) -> p s t", t=NNEW)
                                   ).then_inc(pc_act, 1)
                elif kind == "r":
                    if c >= 1:
                        act.wait_ge(h_ready, c)
                    if c == 0:
                        act.wait_ge(lam_ready, 2)
                    nc.scalar.activation(r_buf.rearrange("p (a b) -> p a b", a=3), bank3(n), ACT.Sigmoid,
                                         bias=vecT[:, VEC["b_rg_a"] + c:VEC["b_rg_a"] + c + 1]
                                         ).then_inc(pc_act, 1)
                    r_at = n
                elif kind == "i":
                    nc.scalar.activation(ig_buf.rearrange("p (a b) -> p a b", a=3), bank3(n), ACT.Sigmoid,
                                         bias=vecT[:, VEC["b_rg_x"] + c:VEC["b_rg_x"] + c + 1]
                                         ).then_inc(pc_act, 1)
                    act.wait_ge(pc_act, n + 1)
                    if c == 0:
                        act.wait_ge(aS_zero, 1)
                    nc.scalar.activation(t_buf, r_buf, ACT.Tanh, scale=lam[:, 4, c:c + 1])
                    nc.scalar.activation(aS[:, c, :, 1:NNEW + 1],
                                         r_buf[:, SEQ:TOK].rearrange("p (s t) -> p s t", t=NNEW),
                                         ACT.Exp, scale=lam[:, 5, c:c + 1]).then_inc(act_chain, 1)
                    act.wait_ge(act_chain, c + 1)
                    nc.scalar.activation(r_buf[:, 0:SEQ], r_buf[:, 0:SEQ], ACT.Exp, scale=lam[:, 5, c:c + 1]
                                         ).then_inc(ta_ready, 1)
                    act.wait_ge(m_ready, c + 1)
                    nc.scalar.activation(t_buf, t_buf, ACT.Sqrt).then_inc(sq_ready, 1)
                else:
                    if c == 0:
                        act.wait_ge(h_ready, KC)
                    if c >= 2:
                        act.wait_ge(y_ready, c - 1)
                    nc.scalar.activation(sz_buf[c % 2].rearrange("p (a b) -> p a b", a=3), bank3(n), ACT.Silu
                                         ).then_inc(pc_act, 1)

            for i in range(TILES):
                r = rows(i)
                act.wait_ge(o_ready, i + 1)
                if i >= 2:
                    act.wait_ge(y_out[i % 2], 16 * (i // 2))
                if i == 0:
                    act.wait_ge(y_ready, KC)
                nc.scalar.activation(y_row[i % 2][0:r, :], x1[0:r, i, :], ACT.Square,
                                     accum_out=ss[0:r, 2, i:i + 1]).then_inc(squared, 1)

        @block.tensor
        def _(pe):
            def mm(out, l, r, start, stop):
                return nc.tensor.matmul(out, l, r, start=start, stop=stop, skip_group_check=True)

            def flip(out, x):
                k = x.shape[0]
                return nc.tensor.transpose(out, x, ident[0:k, 0:k])

            pe.wait_ge(consts_in, NCONST)
            pe.wait_ge(zeroed, 10)
            for j in range(3):
                m = mm(ps[0:HEADS, j, 0:REL // 3], rel_in[:, :], hot[0:BUCKETS + 1, j * 384:(j + 1) * 384],
                       True, True)
            m.then_inc(prep_pe, 1)
            flip(ps[:, 3, 0:NVEC], vec_in[0:NVEC, :])
            for kind in range(2):
                m = mm(ps[:, 3, 128 + kind:129 + kind], pe_in[0:BLK, kind, :], avg[0:BLK, 0:1], True, True)
            for g in range(4):
                flip(ps[:, 4, g * P:(g + 1) * P], wsp_in[:, g, :])
            for k in range(KC):
                m = flip(ps[:, 5, k * NS:(k + 1) * NS], state_in[0:NS, k * P:(k + 1) * P])
            m.then_inc(prep_pe, 1)

            def turn_x(i):
                pe.wait_ge(normed, i + 1)
                if i >= 1:
                    pe.wait_ge(hT_ready, i)
                r = rows(i)
                for k in range(KC):
                    m = flip(ps[:, 6 + k // 4, (k % 4) * P:(k % 4) * P + r], x_row[i % 3][0:r, k * P:(k + 1) * P])
                m.then_inc(x_turned, 1)

            turn_x(0)
            pe.wait_ge(kvg_in, 32)
            for i in range(TILES):
                r = rows(i)
                if i + 1 < TILES:
                    turn_x(i + 1)
                pe.wait_ge(hT_ready, i + 1)
                if i == 0:
                    pe.wait_ge(prep_dve, 5)
                else:
                    pe.wait_ge(kvA_out, i)
                    pe.wait_ge(kvB_out, i)
                for a, b, bank in ((0, 512, 0), (512, KVG, 1)):
                    for k in range(KC):
                        m = mm(ps[0:r, bank, 0:b - a], hT[:, k, tok(i)], w_kvg[:, k, a:b], k == 0, k == KC - 1)
                m.then_inc(kvA_done, 1)
                if i == 0:
                    pe.wait_ge(wv_in, 32)
                else:
                    pe.wait_ge(v_out, i)
                for k in range(KC):
                    m = mm(ps[0:r, 2, :], hT[:, k, tok(i)], w_v[:, k, :], k == 0, k == KC - 1)
                m.then_inc(v_done, 1)
                pe.wait_ge(kvA_out, i + 1)
                pe.wait_ge(kvB_out, i + 1)
                if i >= 1:
                    pe.wait_ge(kT_ready, i)
                row = kv_row[i % 2]
                flip(ps[:, 3, 0:r], row[0:r, 256:384])
                m = flip(ps[:, 3, P:P + r], row[0:r, 512:640])
                if i < PT:
                    for kind in range(2):
                        m = mm(ps[:, 3, 256 + 2 * kind:258 + 2 * kind], row[:, kind * P:(kind + 1) * P],
                               avg[:, :], True, True)
                m.then_inc(k_turned, 1)

            for n, (kind, j, _) in enumerate(FM_A):
                times = 2 if kind == "q" else 1
                before = sum(2 if FM_A[m][0] == "q" else 1 for m in range(n % 4, n, 4))
                pe.wait_ge(fmw_in[n % 4], 16 * (before + times))
                if n == 0:
                    pe.wait_ge(kvB_out, TILES)
                    pe.wait_ge(v_out, TILES)
                elif n == 1:
                    pe.wait_ge(kT_ready, TILES)
                else:
                    fm_wait(pe, n - 2)
                for t in range(3):
                    for k in range(KC):
                        m = mm(ps[:, 3 * (n % 2) + t, 0:THIRD], w_fm[n % 4][:, k, :],
                               hT[:, k, t * THIRD:(t + 1) * THIRD], k == 0, k == KC - 1)
                m.then_inc(fm_done, 1)
                if n == 2:
                    pe.wait_ge(diag_in, 16 * 36)
                    pe.wait_ge(hT_ready, TILES)
                    pe.wait_ge(cmp_rep, 1)
                    mm(ps[:, 6, 0:NB], wc_k[:, :], mean_p[:, 0, :], True, True)
                    mm(ps[:, 6, P:2 * P], mean_rep[:, :, :].rearrange("p h n -> p (h n)"), wc_v[:, :],
                       True, True).then_inc(cmp_pe, 1)

            for i in range(TILES):
                r = rows(i)
                pe.wait_ge(vn_ready, i + 1)
                if i == 0:
                    pe.wait_ge(cmp_ready, 1)
                    pe.wait_ge(prep_dve, 6)
                if i >= 2:
                    pe.wait_ge(mix_used, i - 1)
                for g in range(4):
                    w = wspT[:, g, :] if i < PT else wspT_s[:, g, :]
                    m = mm(ps[:, 6 + i % 2, g * P:g * P + r], vn[0:r, i, g * P:(g + 1) * P], w, True, True)
                m.then_inc(mix_done, 1)

            pe.wait_ge(fm_act, counts["act"])
            pe.wait_ge(fm_dve, counts["dve"])
            pe.wait_ge(mix_used, TILES)

            for what, n in attention_steps():
                if what == "scores":
                    kind, i, h = units[n]
                    cols, first = key_cols(kind, i)
                    slot = 2 * (n % 2)
                    if n >= 2:
                        pe.wait_ge(logits_ready, n - 1)
                    if kind == "c":
                        for c in range(HPG):
                            m = mm(ps[:, slot, c * 2 * NB:(c + 1) * 2 * NB], qT[:, c, tok(i)],
                                   kc_bd[:, :, :].rearrange("p g n -> p (g n)"), True, True)
                    else:
                        g, c = h // HPG, h % HPG
                        kT = kT_s if kind == "s" else kT_w
                        for a in range(0, cols, 512):
                            w = min(512, cols - a)
                            m = mm(ps[:, slot + a // 512, 0:w], qT[g * HD:(g + 1) * HD, c, tok(i)],
                                   kT[g * HD:(g + 1) * HD, first + a:first + a + w], True, True)
                    m.then_inc(scores_done, 1)
                elif what == "turn":
                    kind, i, h = units[n]
                    pe.wait_ge(probs_ready, n + 1)
                    for k in nchunk[("turn", n)]:
                        chunk_wait(pe, k)
                        _, _, a, w, _, _ = chunks[k]
                        if kind == "c":
                            m = flip(ps[:, 4 + k % 2, 0:P], lc[:, :, :].rearrange("p h n -> p (h n)"))
                        else:
                            for b in range(0, w, P):
                                m = flip(ps[:, 4 + k % 2, b:b + P], logits[n % 2][:, a + b:a + b + P])
                        m.then_inc(turned, 1)
                elif what == "values":
                    kind, i, h = units[n]
                    k = nchunk[("turn", n)][-1]
                    pe.wait_ge(chunk_act if chunks[k][4] == "act" else chunk_dve, chunks[k][5])
                    if kind == "c":
                        k = nchunk[("values", n)][0]
                        chunk_wait(pe, k)
                        mm(ps[:, 4 + k % 2, :], probT[n % 2][:, 0:P],
                           vc_bd[:, :, :, :].rearrange("p g h d -> p (g h d)"), True, True).then_inc(turned, 1)
                    else:
                        cols, first = key_cols(kind, i)
                        g = h // HPG
                        vv, bank = (v_s, 6) if kind == "s" else (v_w, 7)
                        if h == 0 and i >= 1:
                            pe.wait_ge(o_free, i)
                        nk = cols // P
                        for b in range(nk):
                            m = mm(ps[:, bank, h * HD:(h + 1) * HD], probT[n % 2][:, b * P:(b + 1) * P],
                                   vv[:, first // P + b, g * HD:(g + 1) * HD], b == 0, b == nk - 1)
                        m.then_inc(values_done, 1)
                else:
                    k = nchunk[("out", n)][0]
                    chunk_wait(pe, k)
                    pe.wait_ge(acc_ready, n + 1)
                    for j in range(4):
                        m = flip(ps[:, 4 + k % 2, j * P:(j + 1) * P], acc[:, j * P:(j + 1) * P])
                    m.then_inc(turned, 1)

            pe.wait_ge(chunk_dve, chunks[-1][5])
            for f in range(2):
                pe.wait_ge(samp_in[f], 16 * (2 * HALF + HALF))
                pe.wait_ge(samp_q, 1)
                if f == 1:
                    pe.wait_ge(samp_dve, samp_at("out", 0))
                for j in range(2 * HALF):
                    m = flip(ps[:, j // 4, (j % 4) * P:(j % 4 + 1) * P], pages[:, j, 256:384])
                m.then_inc(samp_pe, 1)
                for j in range(2 * HALF):
                    m = flip(ps[:, 2 + j // 4, (j % 4) * P:(j % 4 + 1) * P], wins[:, j, 0:P])
                for j in range(2 * HALF):
                    for kind in range(2):
                        m = mm(ps[:, 4, 16 * kind + 2 * j:16 * kind + 2 * j + 2],
                               pages[:, j, kind * P:(kind + 1) * P], avg[:, :], True, True)
                m.then_inc(samp_pe, 1)
                pe.wait_ge(samp_dve, samp_at("means", f))
                mm(ps[:, 4, 64:80], wc_k[:, :], mean_s[:, 0, :], True, True)
                mm(ps[0:16, 4, P:2 * P], mean_s[:, 1, :], wc_v[:, :], True, True)
                mm(ps[:, 4, 256:256 + NG], tsel[:, f * SROWS:(f + 1) * SROWS], gates[0:NS, PT, :],
                   True, True).then_inc(samp_pe, 1)
                pe.wait_ge(samp_dve, samp_at("cmp", f))
                q4 = qbd[:, f * HALF:(f + 1) * HALF].rearrange("p s g c t -> p (s g c t)")
                for bank, kc, kn in ((5, kTc_s, kT_s), (6, kTc_w, kT_w)):
                    for s in range(HALF):
                        mm(ps[32 * s:32 * s + 32, bank, 0:PAST], q4[:, 32 * s:32 * s + 32],
                           kc[:, s * PAST:(s + 1) * PAST], True, True)
                    mm(ps[:, bank, PAST:PAST + NS], q4, kn[:, SEQ:TOK], True, True)
                mm(ps[:, 7, 0:16], q4, kc_s, True, True).then_inc(samp_pe, 1)
                pe.wait_ge(samp_act, f + 1)
                for bank, buf in ((0, ls_s), (1, ls_w)):
                    flip(ps[:, bank, 0:P], buf[:, 0:P])
                    flip(ps[:, bank, P:2 * P], buf[:, P:2 * P])
                    flip(ps[0:NS, bank, 2 * P:3 * P], buf[:, PAST:PAST + NS])
                flip(ps[0:16, 2, 0:P], ls_c).then_inc(samp_pe, 1)
                pe.wait_ge(samp_dve, samp_at("probT", f))
                mm(ps[:, 3, 0:P], pt_c[0:16, :], vc_s[0:16, :], True, True)
                for b, pt, new, old in ((1, pt_s, v_s, lambda s, j: pages[:, 2 * s + j, 384:512]),
                                        (2, pt_w, v_w, lambda s, j: wins[:, 2 * s + j, P:2 * P])):
                    o = ps[:, 3, b * P:(b + 1) * P]
                    m = mm(o, pt[0:NS, 2, :], new[0:NS, PT, :], True, False)
                    for s in range(HALF):
                        for j in range(2):
                            m = mm(ps[32 * s:32 * s + 32, 3, b * P:(b + 1) * P],
                                   pt[:, j, 32 * s:32 * s + 32], old(s, j), False, j == 1)
                m.then_inc(samp_pe, 1)
                pe.wait_ge(samp_dve, samp_at("res", f))
                flip(ps[:, 4, 0:P], res_s).then_inc(samp_pe, 1)

            pe.wait_ge(samp_dve, samp_at("out", 1))
            pe.wait_ge(outa_in, 32)

            def turn_h1(i):
                pe.wait_ge(h1_ready, i + 1)
                if i >= 1:
                    pe.wait_ge(h1T_ready, i)
                r = rows(i)
                for k in range(KC):
                    m = flip(ps[:, 6 + k // 4, (k % 4) * P:(k % 4) * P + r], h1[i % 2][0:r, k * P:(k + 1) * P])
                m.then_inc(h1_turned, 1)

            for i in range(TILES):
                if i >= 3:
                    pe.wait_ge(x1_ready, i - 2)
                b0, r = 2 * (i % 3), rows(i)
                for n in range(2):
                    for k in range(KC):
                        m = mm(ps[0:r, b0 + n, :], yT[:, k, tok(i)], w_outa[:, k, n * 512:(n + 1) * 512],
                               k == 0, k == KC - 1)
                m.then_inc(outa_done, 1)
                if i >= 1:
                    turn_h1(i - 1)
            turn_h1(TILES - 1)

            pe.wait_ge(h1T_ready, TILES)
            for n, (kind, c) in enumerate(order_c):
                if n < 2:
                    pe.wait_ge(x1_ready, TILES)
                else:
                    pe.wait_ge(pc_act, n - 1)
                if kind in "xz":
                    w = c if kind == "x" else KC + c
                    pe.wait_ge(wc_in[w % 3], 16 * (w // 3 + 1))
                    for t in range(3):
                        for k in range(KC):
                            m = mm(ps[:, 3 * (n % 2) + t, 0:THIRD], w_c[w % 3][:, k, :],
                                   h1T[:, k, t * THIRD:(t + 1) * THIRD], k == 0, k == KC - 1)
                else:
                    pe.wait_ge(wg_in, 32)
                    pe.wait_ge(conv_ready, c + 1)
                    for t in range(3):
                        m = mm(ps[:, 3 * (n % 2) + t, 0:THIRD], w_rg[:, 0 if kind == "r" else 1, c, :],
                               xc[c % 2][:, t * THIRD:(t + 1) * THIRD], True, True)
                m.then_inc(pc_done, 1)

            pe.wait_ge(small_ready, 1)
            for c in range(KC):
                m = flip(ps[0:36, 6 + c // 4, (c % 4) * P:(c % 4 + 1) * P], small_out[:, c, :])
            m.then_inc(small_pe, 1)

            pe.wait_ge(outc_in, 32)
            pe.wait_ge(y_ready, KC)
            pe.wait_ge(pc_act, len(order_c))
            for i in range(TILES):
                if i >= 3:
                    pe.wait_ge(o_ready, i - 2)
                b0, r = 2 * (i % 3), rows(i)
                for n in range(2):
                    for k in range(KC):
                        m = mm(ps[0:r, b0 + n, :], yT[:, k, tok(i)], w_outc[:, k, n * 512:(n + 1) * 512],
                               k == 0, k == KC - 1)
                m.then_inc(outc_done, 1)

        @block.vector
        def _(dve):
            v = nc.vector
            chain = [0]

            def link(i):
                chain[0] += 1
                i.then_inc(dve_chain, 1)
                dve.wait_ge(dve_chain, chain[0])

            dve.wait_ge(prep_pe, 1)
            v.tensor_copy(rel_rows[0:HEADS, :].rearrange("p (a b) -> p a b", a=3), ps[0:HEADS, 0:3, 0:REL // 3]
                          ).then_inc(prep_dve, 1)
            dve.wait_ge(prep_pe, 2)
            v.tensor_copy(vecT[:, :], ps[:, 3, 0:NVEC]).then_inc(prep_dve, 1)
            v.tensor_copy(pe_mean[:, :], ps[:, 3, 128:130]).then_inc(prep_dve, 1)
            v.tensor_tensor(wspT[:, :, :], ps[:, 4, :].rearrange("p (g j) -> p g j", g=4),
                            spread(tril[:, :], 4, 1), ALU.mult).then_inc(prep_dve, 1)
            v.tensor_copy(stT[:, :, :], ps[:, 5, 0:KC * NS].rearrange("p (k s) -> p k s", k=KC)
                          ).then_inc(prep_dve, 1)

            def scale_x(i):
                dve.wait_ge(scaled, i + 1)
                r = rows(i)
                x = x_row[i % 3][0:r, :]
                v.tensor_scalar(x, x, rstd[0:r, 0, i:i + 1], None, ALU.mult).then_inc(normed, 1)

            def feature_major(dst, i, norm):
                r = rows(i)
                src = ps[:, 6:8, :].rearrange("p b (k t) -> p (b k) t", t=P)[:, :, 0:r]
                return v.tensor_tensor(dst[:, :, tok(i)], src, spread(vecT[:, norm:norm + KC], r), ALU.mult)

            def keys(i):
                r = rows(i)
                dve.wait_ge(k_turned, i + 1)
                e = v.tensor_copy(kT_s[:, tok(i)], ps[:, 3, 0:r])
                e = v.tensor_copy(kT_w[:, tok(i)], ps[:, 3, P:P + r])
                if i < PT:
                    e = v.tensor_tensor(mean_p[:, :, 2 * i:2 * i + 2],
                                        ps[:, 3, 256:260].rearrange("p (k n) -> p k n", k=2),
                                        spread(pe_mean[:, :], 2), ALU.add)
                e.then_inc(kT_ready, 1)

            def ln_center(i):
                r = rows(i)
                dve.wait_ge(ln_scaled, i + 1)
                v.tensor_scalar(vn[0:r, i, :], vn[0:r, i, :], mv[0:r, i, 0:1], rstd_v[0:r, i:i + 1],
                                ALU.subtract, ALU.mult).then_inc(ln_mid, 1)

            scale_x(0)
            scale_x(1)
            for i in range(TILES):
                r = rows(i)
                dve.wait_ge(x_turned, i + 1)
                feature_major(hT, i, VEC["norm_a"]).then_inc(hT_ready, 1)
                if i + 2 < TILES:
                    scale_x(i + 2)
                if i >= 1:
                    keys(i - 1)
                dve.wait_ge(kvA_done, i + 1)
                if i >= 2:
                    dve.wait_ge(rows_out[i % 2], 16 * sent_rows(i))
                v.tensor_copy(kv_row[i % 2][0:r, 512:768], ps[0:r, 1, 0:256])
                v.tensor_copy(v_w[0:r, i, :], ps[0:r, 1, P:2 * P])
                v.tensor_tensor(gates[0:r, i, :], ps[0:r, 1, 256:KVG - 512], b_gate[0:r, :], ALU.add
                                ).then_inc(kvB_out, 1)
                if i >= 1:
                    ln_center(i - 1)
                dve.wait_ge(v_out, i + 1)
                link(v.bn_stats(bn[0:r, :], vn[0:r, i, :]))
                v.bn_aggr(mv[0:r, i, :], bn[0:r, :]).then_inc(ln_stats, 1)
            keys(TILES - 1)
            ln_center(TILES - 1)
            dve.wait_ge(kT_ready, TILES)
            v.tensor_copy(mean_rep[:, :, :], spread(mean_p[:, 1, :], HEADS, 1)).then_inc(cmp_rep, 1)

            def compressed():
                dve.wait_ge(cmp_pe, 1)
                v.tensor_copy(kc_bd[0:HD, 0, :], ps[0:HD, 6, 0:NB])
                v.tensor_copy(kc_bd[HD:P, 1, :], ps[HD:P, 6, 0:NB])
                v.tensor_tensor(vc_bd[:, :, :, :],
                                spread(ps[:, 6, P:2 * P].rearrange("p (g d) -> p g d", g=KVH), HPG, 2),
                                spread(headrow[:, :].rearrange("p (g h) -> p g h", g=KVH), HD, 3),
                                ALU.mult).then_inc(cmp_ready, 1)
                dve.wait_ge(diag_in, 16 * 36)
                v.tensor_tensor(wspT_s[:, :, :], wspT_s[:, :, :], spread(tril_s[:, :], 4, 1), ALU.mult
                                ).then_inc(prep_dve, 1)

            dve.wait_ge(rel_out, 16 * HEADS)
            for n, (kind, j, who) in enumerate(FM_A):
                if n == 5:
                    compressed()
                if who != "dve":
                    continue
                dve.wait_ge(fm_done, n + 1)
                src = ps[:, 3 * (n % 2):3 * (n % 2) + 3, 0:THIRD]
                if kind == "u":
                    fm_wait(dve, n - 1)
                    y = yT[:, 4 + j, :].rearrange("p (a b) -> p a b", a=3)
                    v.tensor_tensor(y, src, y, ALU.mult).then_inc(fm_dve, 1)
                else:
                    v.tensor_scalar(qT[:, j, :].rearrange("p (a b) -> p a b", a=3), src, -HD ** -0.5, None,
                                    ALU.mult).then_inc(fm_dve, 1)
            for i in range(TILES):
                r = rows(i)
                dve.wait_ge(mix_done, i + 1)
                src = ps[:, 6 + i % 2, :].rearrange("p (g t) -> p g t", t=P)[:, :, 0:r]
                tmp = part_sb[:, 0:4 * r].rearrange("p (g t) -> p g t", g=4)
                if i >= 1:
                    dve.wait_ge(mix_used, i)
                if i < PT:
                    link(v.tensor_tensor(tmp, src, b_sp[:, :, :], ALU.add))
                else:
                    for g in range(4):
                        e = v.tensor_tensor(tmp[:, g, :].rearrange("p (s t) -> p s t", t=NNEW),
                                            src[:, g, :].rearrange("p (s t) -> p s t", t=NNEW),
                                            spread(b_sp[:, g, 0:NNEW], NSEQ, 1), ALU.add)
                    link(e)
                y = yT[:, 4:8, tok(i)]
                v.tensor_tensor(y, y, tmp, ALU.mult).then_inc(mix_used, 1)

            dve.wait_ge(bias_in, 16 * HEADS)
            link(v.tensor_copy(bias_w[:, :, :], bias[:, :, SEQ - WCOLS:SEQ]))
            v.tensor_tensor(bias_w[:, :, 0:P], bias_w[:, :, 0:P], spread(far[:, :], HEADS, 1), ALU.add
                            ).then_inc(biasw_ready, 1)
            dve.wait_ge(biasw_ready, 1)
            dve.wait_ge(gates_ready, 1)

            def tile_sum(i):
                dve.wait_ge(values_done, 2 * HEADS * (i + 1))
                if i >= 1:
                    dve.wait_ge(acc_ready, i)
                link(v.reciprocal(inv[:, 1:3, :], sums[:, i % 2, 1:3, :]))
                g3 = gates[:, i, :].rearrange("p (b h) -> p b h", b=3)
                link(v.tensor_tensor(coef[:, 1:3, :], inv[:, 1:3, :], g3[:, 1:3, :], ALU.mult))
                if i >= 1:
                    dve.wait_ge(turned, nchunk[("out", i - 1)][0] + 1)
                for b in (1, 2):
                    e = v.tensor_tensor(parts[b - 1][:, :].rearrange("p (h d) -> p h d", d=HD),
                                        ps[:, 5 + b, :].rearrange("p (h d) -> p h d", d=HD),
                                        spread(coef[:, b, :], HD), ALU.mult)
                e.then_inc(o_free, 1)
                dve.wait_ge(o_free, i + 1)
                link(v.tensor_tensor(acc[:, :], part_sb[:, :], acc_c[:, :], ALU.add))
                v.tensor_tensor(acc[:, :], acc[:, :], part_2[:, :], ALU.add).then_inc(acc_ready, 1)

            for what, n in attention_steps():
                if what == "scores":
                    kind, i, h = units[n]
                    cols, first = key_cols(kind, i)
                    slot = 2 * (n % 2)
                    dve.wait_ge(scores_done, n + 1)
                    if kind == "c":
                        if i >= 1:
                            dve.wait_ge(turned, nchunk[("turn", n - 17)][0] + 1)
                            dve.wait_ge(logits_ready, n - 16)
                        m0 = 14 - 2 * i
                        src = ps[:, slot, 0:HPG * 2 * NB].rearrange("p (c g n) -> p g c n", c=HPG, g=KVH)
                        table = bias[:, :, BLK - 1::BLK]
                        for g in range(KVH):
                            hs = slice(g * HPG, (g + 1) * HPG)
                            e = v.tensor_tensor(lc[:, hs, 0:cols], src[:, g, :, 0:cols],
                                                table[:, hs, m0:m0 + cols], ALU.add)
                        link(e)
                        link(v.tensor_reduce(lmin[:, :], lc[:, :, 0:cols], AX.X, ALU.min))
                        v.tensor_tensor(lc[:, :, 0:cols], lc[:, :, 0:cols], spread(lmin[:, :], cols),
                                        ALU.subtract).then_inc(logits_ready, 1)
                    else:
                        buf = logits[n % 2][:, 0:cols]
                        if n >= 2:
                            k = nchunk[("turn", n - 2)][-1]
                            dve.wait_ge(turned, k + 1)
                        tab = (bias_w[:, h, :] if kind == "w" and i >= WIN // P
                               else bias[:, h, SEQ - cols:SEQ])
                        v.tensor_tensor_reduce(buf, flat[:, slot * 512:slot * 512 + cols], tab, 1.0, 3e38,
                                               ALU.add, ALU.min, negm[:, n % 4:n % 4 + 1]
                                               ).then_inc(logits_ready, 1)
                elif what == "turn":
                    for k in nchunk[("turn", n)]:
                        _, _, a, w, who, _ = chunks[k]
                        if who == "dve":
                            dve.wait_ge(turned, k + 1)
                            v.tensor_copy(probT[n % 2][:, a:a + w], ps[:, 4 + k % 2, 0:w]).then_inc(chunk_dve, 1)
                    if units[n][0] == "c":
                        i = units[n][1]
                        dve.wait_ge(probs_ready, n + 1)
                        link(v.tensor_reduce(sums[:, i % 2, 0, :], lc[:, :, 0:2 * i + 2], AX.X, ALU.add))
                        link(v.reciprocal(inv[:, 0, :], sums[:, i % 2, 0, :]))
                        if i >= 1:
                            dve.wait_ge(chunk_dve, chunks[nchunk[("values", n - 17)][0]][5])
                        link(v.tensor_tensor(coef[:, 0, :], inv[:, 0, :], gates[:, i, 0:HEADS], ALU.mult))
                        if i == 0:
                            link(v.tensor_scalar(coef[:, 0, :], coef[:, 0, :], rowok[:, 0:1], None, ALU.mult))
                elif what == "values":
                    kind, i, h = units[n]
                    if kind == "c":
                        k = nchunk[("values", n)][0]
                        dve.wait_ge(turned, k + 1)
                        v.tensor_tensor(acc_c[:, :].rearrange("p (h d) -> p h d", d=HD),
                                        ps[:, 4 + k % 2, :].rearrange("p (h d) -> p h d", d=HD),
                                        spread(coef[:, 0, :], HD), ALU.mult).then_inc(chunk_dve, 1)
                    if kind == "w" and h == HEADS - 1:
                        tile_sum(i)
                else:
                    k = nchunk[("out", n)][0]
                    dve.wait_ge(turned, k + 1)
                    y = yT[:, 0:4, tok(n)]
                    v.tensor_tensor(y, ps[:, 4 + k % 2, :].rearrange("p (j t) -> p j t", t=P), y, ALU.mult
                                    ).then_inc(chunk_dve, 1)

            dve.wait_ge(bias_s_in, 16 * 12)
            for s in range(HALF):
                o = slice(32 * s, 32 * s + 32)
                e = v.tensor_copy(bias_b[o, NBP * s:NBP * s + NBP], bias_c[o, BLK - 1::BLK])
            for g in range(KVH):
                gp = slice(g * HD, (g + 1) * HD)
                for s in range(NSEQ):
                    e = v.tensor_copy(qbd[gp, s, g, :, :], qT[gp, :, SEQ + s * NNEW:SEQ + (s + 1) * NNEW])
            e.then_inc(samp_q, 1)
            for f in range(2):
                if f == 1:
                    dve.wait_ge(samp_dve, samp_at("out", 0))
                dve.wait_ge(samp_pe, samp_pe_at("keys0", f))
                v.tensor_copy(kTc_s, flat[:, 0:1024]).then_inc(samp_dve, 1)
                dve.wait_ge(samp_pe, samp_pe_at("keys1", f))
                v.tensor_copy(kTc_w, flat[:, 1024:2048]).then_inc(samp_dve, 1)
                v.tensor_tensor(mean_s, ps[:, 4, 0:32].rearrange("p (k n) -> p k n", k=2),
                                spread(pe_mean[:, :], 16), ALU.add).then_inc(samp_dve, 1)
                dve.wait_ge(samp_pe, samp_pe_at("cmp", f))
                v.tensor_copy(kc_s, ps[:, 4, 64:80])
                v.tensor_copy(vc_s[0:16, :], ps[0:16, 4, P:2 * P])
                link(v.tensor_tensor(gate_rows, ps[:, 4, 256:256 + NG].rearrange("p (b h) -> p b h", b=3),
                                     spread(hsel[:, :], 3, 1), ALU.mult))
                v.tensor_reduce(coef_g, gate_rows, AX.X, ALU.add).then_inc(samp_dve, 1)
                dve.wait_ge(samp_pe, samp_pe_at("scores", f))

                def add_min(buf, src, tab, at, first):
                    return v.tensor_tensor_reduce(buf, src, tab, 1.0, first, ALU.add, ALU.min, at)

                e = add_min(ls_c, ps[:, 7, 0:16], bias_b[:, :], neg_s[:, 0:1], 3e38)
                for b, bank, buf in ((1, 5, ls_s), (2, 6, ls_w)):
                    link(add_min(buf[:, 0:PAST], ps[:, bank, 0:PAST], bias_c[:, :], lmin[:, b:b + 1], 3e38))
                    link(add_min(buf[:, PAST:PAST + NS], ps[:, bank, PAST:PAST + NS], bias_n[:, f, :],
                                 lmin[:, 4 + b:5 + b], 3e38))
                v.tensor_tensor(neg_s[:, 1:3], lmin[:, 1:3], lmin[:, 5:7], ALU.min).then_inc(samp_dve, 1)
                dve.wait_ge(samp_pe, samp_pe_at("turned", f))
                for bank, pt in ((0, pt_s), (1, pt_w)):
                    v.tensor_copy(pt[:, 0:2, :], ps[:, bank, 0:2 * P].rearrange("p (a b) -> p a b", a=2))
                    v.tensor_copy(pt[0:NS, 2, :], ps[0:NS, bank, 2 * P:3 * P])
                v.tensor_copy(pt_c[0:16, :], ps[0:16, 2, 0:P]).then_inc(samp_dve, 1)
                link(v.reciprocal(coef_s, sum_s))
                link(v.tensor_tensor(coef_s, coef_s, coef_g, ALU.mult))
                dve.wait_ge(samp_pe, samp_pe_at("values", f))
                link(v.tensor_scalar(res_s, ps[:, 3, 0:P], coef_s[:, 0:1], None, ALU.mult))
                link(v.scalar_tensor_tensor(out=res_s, in0=ps[:, 3, P:2 * P], scalar=coef_s[:, 1:2], in1=res_s,
                                            op0=ALU.mult, op1=ALU.add))
                v.scalar_tensor_tensor(out=res_s, in0=ps[:, 3, 2 * P:3 * P], scalar=coef_s[:, 2:3], in1=res_s,
                                       op0=ALU.mult, op1=ALU.add).then_inc(samp_dve, 1)
                dve.wait_ge(samp_pe, samp_pe_at("out", f))
                for h in range(HEADS):
                    g, j, o = h // HPG, h // 2, (h % 2) * HD
                    c0 = SEQ + f * HALF * NNEW
                    y = yT[o:o + HD, j, c0:c0 + HALF * NNEW].rearrange("p (s t) -> p s t", t=NNEW)
                    src = ps[g * HD:(g + 1) * HD, 4, 0:P].rearrange("p (s h t) -> p s h t", s=HALF, h=HEADS)
                    e = v.tensor_tensor(y, src[:, :, h, :], y, ALU.mult)
                e.then_inc(samp_dve, 1)

            lm = vecT[:, VEC["lru_lambda"]:VEC["lru_lambda"] + KC]
            link(v.tensor_scalar(lam[:, 2, :], lm, -1.0, None, ALU.mult))
            v.tensor_tensor(lam[:, 0, :], lm, lam[:, 2, :], ALU.max).then_inc(lam_ready, 1)

            def fm_h1(i):
                dve.wait_ge(h1_turned, i + 1)
                feature_major(h1T, i, VEC["norm_c"]).then_inc(h1T_ready, 1)

            for i in range(TILES):
                r, b0 = rows(i), 2 * (i % 3) * 512
                dve.wait_ge(outa_done, i + 1)
                dve.wait_ge(xa_in[i % 2], 16 * (i // 2 + 1))
                v.tensor_tensor(x1[0:r, i, :], flat[0:r, b0:b0 + D], x_again[i % 2][0:r, :], ALU.add
                                ).then_inc(x1_ready, 1)
                if i >= 1:
                    fm_h1(i - 1)
                dve.wait_ge(scaled, TILES + i + 1)
                v.tensor_scalar(h1[i % 2][0:r, :], x1[0:r, i, :], rstd[0:r, 1, i:i + 1], None, ALU.mult
                                ).then_inc(h1_ready, 1)
            fm_h1(TILES - 1)
            dve.wait_ge(lam_exp, 1)
            link(v.tensor_scalar(lam[:, 3, :], lam[:, 1, :], 2.0, None, ALU.add))
            link(v.reciprocal(lam[:, 3, :], lam[:, 3, :]))
            link(v.tensor_tensor(lam[:, 3, :], lam[:, 3, :], lam[:, 1, :], ALU.mult))
            link(v.tensor_tensor(lam[:, 4, :], lam[:, 3, :], lam[:, 3, :], ALU.mult))
            link(v.tensor_scalar(lam[:, 5, :], lam[:, 4, :], 1.0 / 17, 1.0 / 15, ALU.mult, ALU.add))
            for k in (13, 11, 9, 7, 5, 3, 1):
                link(v.tensor_tensor(lam[:, 5, :], lam[:, 5, :], lam[:, 4, :], ALU.mult))
                link(v.tensor_scalar(lam[:, 5, :], lam[:, 5, :], 1.0 / k, None, ALU.add))
            link(v.tensor_tensor(lam[:, 5, :], lam[:, 5, :], lam[:, 3, :], ALU.mult))
            link(v.tensor_scalar(lam[:, 5, :], lam[:, 5, :], 2.0, None, ALU.mult))
            link(v.tensor_scalar(lam[:, 2, :], lam[:, 2, :], 0.0, None, ALU.max))
            link(v.tensor_tensor(lam[:, 5, :], lam[:, 5, :], lam[:, 2, :], ALU.add))
            link(v.tensor_scalar(lam[:, 4, :], lam[:, 5, :], 8.0, None, ALU.mult))
            v.tensor_scalar(lam[:, 5, :], lam[:, 4, :], -1.0, None, ALU.mult).then_inc(lam_ready, 1)

            link(v.memset(xin[:, 0:3], 0.0))
            link(v.tensor_copy(bS[:, :, :, 0], stT[:, :, 24:32]))

            def conv(c):
                n = order_c_at[("x", c)]
                dve.wait_ge(pc_act, n + 1)
                if c >= 1:
                    dve.wait_ge(conv_ready, c)
                link(v.tensor_copy(xin_s[:, :, 0:3], stT[:, c, 0:24].rearrange("p (s k) -> p s k", k=3)))
                v.tensor_copy(small_out[:, c, 8:32].rearrange("p (s k) -> p s k", k=3), xin_s[:, :, 4:7])
                v.tensor_copy(small_out[:, c, 33:36], xin[:, SEQ:SEQ + 3])
                cw = VEC["conv_w"] + c
                cb = vecT[:, VEC["conv_b"] + c:VEC["conv_b"] + c + 1]
                outp = xc[c % 2][:, 0:SEQ]
                outs_ = xc[c % 2][:, SEQ:TOK].rearrange("p (s t) -> p s t", t=NNEW)
                v.tensor_scalar(outp, xin[:, 0:SEQ], vecT[:, cw:cw + 1], cb, ALU.mult, ALU.add)
                link(v.tensor_scalar(outs_, xin_s[:, :, 0:NNEW], vecT[:, cw:cw + 1], cb, ALU.mult, ALU.add))
                for k in range(1, 4):
                    w = vecT[:, cw + 8 * k:cw + 8 * k + 1]
                    v.scalar_tensor_tensor(out=outp, in0=xin[:, k:k + SEQ], scalar=w, in1=outp,
                                           op0=ALU.mult, op1=ALU.add)
                    e = v.scalar_tensor_tensor(out=outs_, in0=xin_s[:, :, k:k + NNEW], scalar=w, in1=outs_,
                                               op0=ALU.mult, op1=ALU.add)
                    if k < 3:
                        link(e)
                e.then_inc(conv_ready, 1)

            def recur(c):
                dve.wait_ge(ta_ready, c + 1)
                link(v.tensor_scalar(e_buf, t_buf, 1.0, None, ALU.add))
                link(v.reciprocal(e_buf, e_buf))
                v.scalar_tensor_tensor(out=t_buf, in0=t_buf, scalar=2.0, in1=e_buf, op0=ALU.mult, op1=ALU.mult
                                       ).then_inc(m_ready, 1)
                v.tensor_tensor(ig_buf, ig_buf, xc[c % 2], ALU.mult).then_inc(dve_chain, 1)
                chain[0] += 1
                dve.wait_ge(dve_chain, chain[0])
                dve.wait_ge(sq_ready, c + 1)
                link(v.tensor_tensor(t_buf, t_buf, ig_buf, ALU.mult))
                v.tensor_copy(bS[:, c, :, 1:NNEW + 1], t_buf[:, SEQ:TOK].rearrange("p (s t) -> p s t", t=NNEW))
                v.tensor_tensor_scan(yT[:, c, 0:SEQ], r_buf[:, 0:SEQ], t_buf[:, 0:SEQ], 0.0, ALU.mult, ALU.add
                                     ).then_inc(h_ready, 1)

            for c in range(KC):
                if c < 1:
                    conv(c)
                if c + 1 < KC:
                    conv(c + 1)
                recur(c)
            hS = t_buf[:, 0:KC * NSEQ * (NNEW + 1)]
            dve.wait_ge(h_ready, KC)
            link(v.tensor_tensor_scan(hS, aS[:, :, :, :].rearrange("p c s t -> p (c s t)"),
                                      bS[:, :, :, :].rearrange("p c s t -> p (c s t)"), 0.0,
                                      ALU.mult, ALU.add))
            hS4 = hS.rearrange("p (c s t) -> p c s t", c=KC, s=NSEQ)
            for c in range(KC):
                v.tensor_copy(yT[:, c, SEQ:TOK].rearrange("p (s t) -> p s t", t=NNEW), hS4[:, c, :, 1:NNEW + 1])
            v.tensor_copy(small_out[:, :, 0:8], hS4[:, :, :, NNEW])
            v.tensor_copy(small_out[:, :, 32:33], yT[:, :, SEQ - 1:SEQ]).then_inc(small_ready, 1)
            dve.wait_ge(small_ready, 1)
            for c in range(KC):
                n = order_c_at[("z", c)]
                dve.wait_ge(pc_act, n + 1)
                v.tensor_tensor(yT[:, c, :], yT[:, c, :], sz_buf[c % 2], ALU.mult).then_inc(y_ready, 1)
            dve.wait_ge(small_pe, 1)
            v.tensor_copy(small_tm[0:36, :], flat[0:36, 6 * 512:8 * 512]).then_inc(small_rows, 1)

            def finish(i):
                r = rows(i)
                if i == 0:
                    dve.wait_ge(fin_in, 16)
                dve.wait_ge(scaled, 2 * TILES + i + 1)
                v.scalar_tensor_tensor(out=y_row[i % 2][0:r, :], in0=x1[0:r, i, :], scalar=rstd[0:r, 2, i:i + 1],
                                       in1=fin_g[0:r, :], op0=ALU.mult, op1=ALU.mult).then_inc(y_row_ready, 1)

            for i in range(TILES):
                r, b0 = rows(i), 2 * (i % 3) * 512
                dve.wait_ge(outc_done, i + 1)
                v.tensor_tensor(x1[0:r, i, :], flat[0:r, b0:b0 + D], x1[0:r, i, :], ALU.add).then_inc(o_ready, 1)
                if i >= 1:
                    finish(i - 1)
            finish(TILES - 1)


_WEIGHTS = ["x_prompt", "x_sample", "cache_nsa", "cache_win", "state_lru_h", "state_lru_conv", "page_table",
            "norm_a", "w_in_a", "b_gate_a", "pe_cmp", "w_cmp", "gmlp_ln_g", "gmlp_ln_b", "w_spatial",
            "b_spatial", "w_out_a", "norm_c", "w_in_c", "conv_w", "conv_b", "w_rg_a", "b_rg_a", "w_rg_x",
            "b_rg_x", "lru_lambda", "w_out_c", "rel_bias", "final_norm"]
_OUTS = [("y_prompt", (1, SEQ, D)), ("y_sample", (NSEQ, NNEW, D)),
         ("nsa_rows_prompt", (1, 1, SEQ, 4, KVH, HD)), ("nsa_rows_sample", (1, NSEQ, NNEW, 4, KVH, HD)),
         ("win_rows_prompt", (1, 1, WIN, 2, KVH, HD)), ("win_rows_sample", (1, NSEQ, NNEW, 2, KVH, HD)),
         ("gmlp_v_sample", (1, NSEQ, NNEW, 512)), ("lru_h_prompt", (1, 1, D)), ("lru_h_sample", (1, NSEQ, D)),
         ("lru_conv_prompt", (1, 1, 3, D)), ("lru_conv_sample", (1, NSEQ, 3, D))]


def kernel(**inputs):
    import concourse.bacc as _bacc
    from concourse.bass_utils import run_bass_kernel_spmd as _run

    nc = _bacc.Bacc("TRN2", target_bir_lowering=False, num_devices=1)
    arrays, ins, outs = {}, {}, {}
    given = {n: np.ascontiguousarray(inputs[n]) for n in _WEIGHTS}
    given.update(constants())
    for name, a in given.items():
        arrays[f"in_{name}"] = a
        ins[name] = nc.dram_tensor(f"in_{name}", a.shape, mybir.dt.from_np(a.dtype), kind="ExternalInput").ap()
    for name, shape in _OUTS:
        outs[name] = nc.dram_tensor(f"out_{name}", shape, F32, kind="ExternalOutput").ap()
    build(nc, ins, outs)
    r = _run(nc, [arrays], core_ids=[0])
    return tuple(r.results[0][f"out_{name}"] for name, _ in _OUTS)
```

```python
import math
from contextlib import ExitStack

import concourse.bass as bass
from concourse import mybir
import numpy as np

ALU = mybir.AluOpType
ACT = mybir.ActivationFunctionType
AX = mybir.AxisListType
F32 = mybir.dt.float32
F32R = mybir.dt.float32r

P = 128
D = 1024
KC = D // P
SEQ = 1024
NSEQ, NNEW = 8, 4
NS = NSEQ * NNEW
TOK = SEQ + NS
TILES = SEQ // P + 1
PT = SEQ // P
THIRD = TOK // 3
HEADS, KVH, HD = 8, 2, 64
HPG = HEADS // KVH
KV = 6 * KVH * HD
NG = 3 * HEADS
KVG = KV + NG
BLK = 64
NB = SEQ // BLK
WIN = 512
WCOLS = WIN + P
PAST = 256
PAGE = 128
NBP = PAST // BLK
BUCKETS, MAX_DIST = 32, 1024
REL = SEQ + P
REL_TOP = SEQ - 1
BIG = 1e30
EPS = 1e-6
Q0, KV0, G0, Z0 = 0, 512, 512 + KV, 512 + KV + NG
U0, V0, ZG0 = Z0 + 512, Z0 + 1024, Z0 + 1536
HALF = NSEQ // 2
SROWS = HALF * HEADS * NNEW
VEC = {"norm_a": 0, "norm_c": 8, "conv_w": 16, "conv_b": 48, "b_rg_a": 56, "b_rg_x": 64, "lru_lambda": 72}
NVEC = 80


def rows(i):
    return P if i < PT else NS


def tok(i):
    return slice(i * P, i * P + rows(i))


def constants():
    c = {}
    d = np.arange(REL_TOP, REL_TOP - REL, -1)
    exact = BUCKETS // 2
    df = np.maximum(d, 1).astype(np.float32)
    large = exact + (np.log(df / np.float32(exact)) / np.float32(math.log(MAX_DIST / exact))
                     * np.float32(BUCKETS - exact)).astype(np.int32)
    bucket = np.where(d < exact, d, np.minimum(large, BUCKETS - 1))
    hot = np.zeros((BUCKETS + 1, REL), np.float32)
    hot[bucket[d >= 0], np.nonzero(d >= 0)[0]] = -1.0
    hot[BUCKETS, d < 0] = 1.0
    c["c_hot"] = hot
    k = np.arange(P)
    c["c_ident"] = np.eye(P, dtype=np.float32)
    c["c_two_i"] = np.concatenate([np.eye(HD, dtype=np.float32)] * 2)
    c["c_tril"] = (k[:, None] <= k[None, :]).astype(np.float32)
    c["c_far"] = np.where(k[None, :] < k[:, None], BIG, 0.0).astype(np.float32)
    c["c_avg"] = ((k[:, None] // BLK == np.arange(2)[None, :]) / BLK).astype(np.float32)
    c["c_rowok"] = (k[:, None] >= BLK - 1).astype(np.float32)
    c["c_headrow"] = (k[:, None] // NB == np.arange(HEADS)[None, :]).astype(np.float32)
    r = np.arange(SROWS)
    s, h, t = r // (HEADS * NNEW), r // NNEW % HEADS, r % NNEW
    c["c_hsel"] = (h[:, None] == np.arange(HEADS)[None, :]).astype(np.float32)
    n = np.arange(NS)
    c["c_tsel"] = np.concatenate(
        [(n[:, None] == ((HALF * f + s) * NNEW + t)[None, :]) for f in range(2)], 1).astype(np.float32)
    c["c_tril_s"] = ((n[:, None] // NNEW == n[None, :] // NNEW)
                     & (n[:, None] % NNEW <= n[None, :] % NNEW)).astype(np.float32)
    return c


def attention_units():
    units = []
    for i in range(PT):
        units.append(("c", i, 0))
        for g in range(KVH):
            units += [(kind, i, g * HPG + c) for kind in "sw" for c in range(HPG)]
    return units


GROUPS = [(kind, i, g) for i in range(PT) for g in range(KVH) for kind in "sw"]


def last_unit(j):
    return 17 * (j // 4) + 4 * (j % 4) + 4


def key_cols(kind, i):
    if kind == "c":
        return 2 * i + 2, 0
    first = 0 if kind == "s" else max(0, i - WIN // P)
    return (i + 1 - first) * P, first * P


def attention_steps():
    steps = [("split_q", 0)] + [("scores", n) for n in range(1 + HPG)]
    soon = [[2, ("c_turn", 0)], [3, ("c_values", 0)]]
    unit = 1 + HPG
    waiting = []

    def one_block():
        for x in soon:
            x[0] -= 1
        for x in [x for x in soon if x[0] <= 0]:
            soon.remove(x)
            steps.append(x[1])

    def values():
        j, b = waiting.pop(0)
        kind, i, g = GROUPS[j]
        steps.append(("values", (j, b)))
        if b == key_cols(kind, i)[0] // P - 1:
            steps.append(("copy_o", j))
            if kind == "w":
                soon.append([1 if i == 0 and g == 0 else 2, ("back", (i, g))])
                if g == KVH - 1:
                    soon.append([4, ("out", i)])

    for j, (kind, i, g) in enumerate(GROUPS):
        nk = key_cols(kind, i)[0] // P
        more = []
        if j + 1 < len(GROUPS):
            more = list(range(unit, unit + HPG + (1 if j % 4 == 3 else 0)))
            unit += len(more)
        if j % 4 == 3 and i + 1 < PT:
            soon += [[nk + 4, ("c_turn", i + 1)], [nk + 6, ("c_values", i + 1)]]
        if j % 4 == 1 and i + 1 < PT:
            steps.append(("split_q", i + 1))
        for b in range(nk):
            if len(waiting) == 2:
                values()
            steps.append(("turn", (j, b)))
            waiting.append((j, b))
            take = -(-len(more) // max(1, nk - 1 - b))
            for n in more[:take]:
                steps.append(("scores", n))
            more = more[take:]
            one_block()
    while waiting:
        values()
        one_block()
    while soon:
        one_block()
    return steps


def act_order(steps):
    order, pending = [], []
    for x in steps:
        if x[0] == "scores":
            pending.append(x)
            continue
        need = -1
        if x[0] == "turn":
            need = last_unit(x[1][0])
        elif x[0] == "c_turn":
            need = 17 * x[1]
        while pending and pending[0][1] <= need:
            order.append(pending.pop(0))
        order.append(x)
        if x[0] == "turn":
            order += pending
            pending = []
    return order + pending


def bank_uses(steps):
    return {x: k for k, x in enumerate(x for x in steps
                                       if x[0] in ("c_turn", "c_values", "turn", "back", "out"))}


FM_A = ([("z", j, "act") for j in range(4)]
        + [x for j in range(4) for x in (("zg", j, "act"), ("u", j, "dve"))]
        + [("q", j, "dve") for j in range(4)])


def build(nc, ins, outs):
    ctx = ExitStack()
    with ctx:
        def sb(name, shape):
            return ctx.enter_context(nc.sbuf_tensor(name, shape, F32))

        def sem(name):
            return ctx.enter_context(nc.semaphore(name))

        ps = ctx.enter_context(nc.psum_tensor("ps", [P, 8, 512], F32))
        flat = ps[:, :, :].rearrange("p b n -> p (b n)")
        arena_cols = [8 * TOK, 8640, 27904]
        sb("arena", [P, sum(arena_cols)])
        arena_at = nc.sbuf_base - 4 * sum(arena_cols)

        def placed(name, at, shape, dt):
            return nc.alloc_sbuf_tensor_at(name, shape, dt, offset=arena_at + 4 * at)

        AT_Q, AT_W = arena_cols[0], arena_cols[0] + arena_cols[1]
        region_y = placed("region_y", 0, [P, arena_cols[0]], F32)
        region_q = placed("region_q", AT_Q, [P, arena_cols[1]], F32)
        region_w = placed("region_w", AT_W, [P, arena_cols[2]], F32)

        def view(region, at, *shape):
            n = int(np.prod(shape))
            v = region[:, at:at + n]
            if len(shape) == 2:
                v = v.rearrange("p (a b) -> p a b", a=shape[0])
            if len(shape) == 3:
                v = v.rearrange("p (a b c) -> p a b c", a=shape[0], b=shape[1])
            return v

        w_kvg = view(region_y, 0, KC, KVG)
        yT = view(region_y, 0, 8, TOK)
        hot = view(region_q, 0, REL)
        rel_rows = view(region_q, REL, REL)
        wsp_in = view(region_q, 2 * REL, 4, P)
        vec_in = view(region_q, 2 * REL + 512, P)
        state_in = view(region_q, 2 * REL + 640, D)
        pe_in = view(region_q, 2 * REL + 640 + D, 2, P)
        qT = view(region_q, 0, HPG, TOK)
        kT_s = view(region_q, 4 * TOK, TOK)
        kT_w = view(region_q, 5 * TOK, TOK)
        v_s = view(region_q, 6 * TOK, TILES, P)
        v_w = view(region_q, 6 * TOK + TILES * P, TILES, P)
        h1T = view(region_q, 0, KC, TOK)
        hT = view(region_w, 0, KC, TOK)
        w_v = view(region_w, 8448, KC, 512)
        w_fm = [view(region_w, 12544 + D * j, KC, P) for j in range(4)]
        vn = view(region_w, 16640, TILES, 512)
        kv_row = [view(region_w, 21248 + KVG * j, KVG) for j in range(2)]
        x_row = [view(region_w, 22832 + D * j, D) for j in range(3)]
        junk = view(region_w, 25904, D)
        bias = view(region_w, 0, HEADS, SEQ)
        k_hi = placed("k_hi", AT_W + 8448, [P, 2, KVH, SEQ], F32R)
        k_lo = placed("k_lo", AT_W + 25344, [P, 2, SEQ], F32R)
        v_hl = placed("v_hl", AT_W + 21248, [P, 2, KVH, PT, 2 * HD], F32R)
        q_hl = placed("q_hl", AT_Q + 4 * TOK, [P, 2, HEADS, P], F32R)
        p_hl = placed("p_hl", AT_W + 19200, [P, 2, 2, 512], F32R)
        probs = {"s": view(region_w, 12544, HPG, SEQ), "w": view(region_w, 16640, HPG, WCOLS)}
        bias_far = view(region_q, 6 * TOK, HEADS, P)
        probT_c = view(region_q, 6 * TOK + TILES * P, P)
        ls_s = view(region_w, 17408, PAST + NS)
        ls_w = view(region_w, 17696, PAST + NS)
        ls_c = view(region_w, 17984, 16)
        pt_s = view(region_w, 18000, 3, P)
        pt_w = view(region_w, 18384, 3, P)
        pt_c = view(region_w, 18768, P)
        res_s = view(region_w, 18896, P)
        mean_s = view(region_w, 19024, 2, 16)
        kc_s = view(region_w, 19056, 16)
        vc_s = view(region_w, 19072, P)
        gate_rows = view(region_w, 19200, 3, HEADS)
        coef_s = view(region_w, 19224, 3)
        coef_g = view(region_w, 19227, 3)
        sum_s = view(region_w, 19230, 3)
        neg_s = view(region_w, 19233, 3)
        pages_of = [view(region_w, 8448, 2 * HALF, 512), view(region_w, 21248, 2 * HALF, 512)]
        wins_of = [view(region_w, 25344, 2 * HALF, 256), view(region_w, 12544, 2 * HALF, 256)]
        kTc_s = view(region_w, 14592, 2 * HALF * P)
        kTc_w = view(region_w, 15616, 2 * HALF * P)
        w_outa = view(region_w, 0, KC, D)
        x_again = [view(region_w, 8192 + D * j, D) for j in range(2)]
        x1 = view(region_w, 10496, TILES, D)
        h1 = [view(region_w, 19712 + D * j, D) for j in range(2)]
        w_c = [view(region_w, D * j, KC, P) for j in range(3)]
        xin = view(region_w, 3072, 3 + SEQ)
        xin_s = view(region_w, 3072 + 1027, NSEQ, 7)
        xc = [view(region_w, 4160 + TOK * j, TOK) for j in range(2)]
        r_buf = view(region_w, 6272, TOK)
        t_buf = view(region_w, 7328, TOK)
        e_buf = view(region_w, 8384, TOK)
        ig_buf = view(region_w, 9440, TOK)
        w_outc = view(region_w, 19712, KC, D)
        sz_buf = [r_buf, ig_buf]
        y_row = [view(region_w, D * j, D) for j in range(2)]

        ident = sb("ident", [P, P])
        tril = sb("tril", [P, P])
        far = sb("far", [P, P])
        avg = sb("avg", [P, 2])
        rowok = sb("rowok", [P, 1])
        headrow = sb("headrow", [P, HEADS])
        hsel = sb("hsel", [P, HEADS])
        tsel = sb("tsel", [NS, 2 * SROWS])
        tril_s = sb("tril_s", [NS, NS])
        rel_in = sb("rel_in", [BUCKETS + 1, HEADS])
        vecT = sb("vecT", [P, NVEC])
        region_m = sb("region_m", [P, 1024])
        wspT = view(region_m, 0, 4, P)
        b_sp = view(region_m, 512, 4, P)
        aS = view(region_m, 0, KC, NSEQ, NNEW + 1)
        bS = view(region_m, 320, KC, NSEQ, NNEW + 1)
        small_out = view(region_m, 640, KC, 36)
        region_g = sb("region_g", [P, D])
        ln_g = region_g[:, 0:512]
        ln_b = region_g[:, 512:1024]
        fin_g = region_g
        wspT_s = sb("wspT_s", [NS, 4, NS])
        b_gate = sb("b_gate", [P, NG])
        wc_k = sb("wc_k", [P, P])
        wc_v = sb("wc_v", [P, P])
        pe_mean = sb("pe_mean", [P, 2])
        mean_p = sb("mean_p", [P, 2, NB])
        mean_rep = sb("mean_rep", [P, HEADS, NB])
        kc_bd = sb("kc_bd", [P, KVH, NB])
        vc_bd = sb("vc_bd", [P, KVH, HPG, HD])
        gates = sb("gates", [P, TILES, NG])
        half_neg = sb("half_neg", [P, 1])
        ss = sb("ss", [P, 3, TILES])
        ms = sb("ms", [P, 3, TILES])
        rstd = sb("rstd", [P, 3, TILES])
        bn = sb("bn", [P, 6])
        mv = sb("mv", [P, TILES, 2])
        mv_e = sb("mv_e", [P, TILES])
        rstd_v = sb("rstd_v", [P, TILES])
        negm = sb("negm", [P, 4])
        sums = sb("sums", [P, 2, 3, HEADS])
        inv = sb("inv", [P, 3, HEADS])
        coef = sb("coef", [P, 3, HEADS])
        lc = sb("lc", [P, HEADS, NB])
        lmin = sb("lmin", [P, HEADS])
        acc = sb("acc", [P, 512])
        acc_c = view(region_q, 6 * TOK + TILES * P + P, 512)
        far_min = sb("far_min", [P, 2])
        part_sb = sb("part_sb", [P, 512])
        part_2 = sb("part_2", [P, 512])
        o_T = [part_sb, part_2]
        gated = sb("gated", [P, 2, HPG, HD])
        two_i = sb("two_i", [P, HD])
        k_new = sb("k_new", [P, 2, NS])
        bias_c = sb("bias_c", [P, PAST])
        bias_n = sb("bias_n", [P, 2, NS])
        bias_b = sb("bias_b", [P, 16])
        qbd = sb("qbd", [P, NSEQ, KVH, HPG, NNEW])
        stT = sb("stT", [P, KC, NS])
        lam = sb("lam", [P, 6, KC])
        pt_tab = sb("pt_tab", [1, NSEQ * 2])
        pt_tab = pt_tab[:, :].bitcast(mybir.dt.int32)

        rel_dram = nc.dram_tensor("rel_rows_dram", (HEADS, P * (REL + 1)), F32, kind="Internal").ap()

        def rel_skewed(first_head, heads, shifts, at, n):
            dims = [[P * (REL + 1), heads], [REL, shifts], [1, n]]
            return bass.AP(rel_dram.tensor, first_head * P * (REL + 1) + at, dims)

        zeroed = sem("zeroed")
        first_in = sem("first_in")
        consts_in = sem("consts_in")
        diag_in = sem("diag_in")
        x_in = [sem(f"x_in{j}") for j in range(3)]
        kvg_in = sem("kvg_in")
        wv_in = sem("wv_in")
        fmw_in = [sem(f"fmw_in{j}") for j in range(4)]
        prep_pe = sem("prep_pe")
        prep_dve = sem("prep_dve")
        rel_out = sem("rel_out")
        squared = sem("squared")
        scaled = sem("scaled")
        normed = sem("normed")
        x_turned = sem("x_turned")
        hT_ready = sem("hT_ready")
        kvA_done = sem("kvA_done")
        v_done = sem("v_done")
        kvA_out = sem("kvA_out")
        v_out = sem("v_out")
        kvB_out = sem("kvB_out")
        k_turned = sem("k_turned")
        kT_ready = sem("kT_ready")
        rows_out = [sem(f"rows_out{j}") for j in range(2)]
        ln_stats = sem("ln_stats")
        ln_scaled = sem("ln_scaled")
        ln_mid = sem("ln_mid")
        vn_ready = sem("vn_ready")
        vn_out = sem("vn_out")
        fm_done = sem("fm_done")
        fm_act = sem("fm_act")
        fm_dve = sem("fm_dve")
        cmp_rep = sem("cmp_rep")
        cmp_pe = sem("cmp_pe")
        cmp_ready = sem("cmp_ready")
        mix_done = sem("mix_done")
        mix_used = sem("mix_used")
        gates_ready = sem("gates_ready")
        bias_in = sem("bias_in")
        far_ready = sem("far_ready")
        split_hi = sem("split_hi")
        split_lo = sem("split_lo")
        q_hi = sem("q_hi")
        q_lo = sem("q_lo")
        p_hi = sem("p_hi")
        bias_s_in = sem("bias_s_in")
        scores_done = sem("scores_done")
        logits_ready = sem("logits_ready")
        probs_ready = sem("probs_ready")
        turned = sem("turned")
        bank_empty = sem("bank_empty")
        values_done = sem("values_done")
        o_copied = sem("o_copied")
        acc_ready = sem("acc_ready")
        samp_in = [sem("samp_in0"), sem("samp_in1")]
        samp_pe = sem("samp_pe")
        samp_q = sem("samp_q")
        samp_dve = sem("samp_dve")
        samp_act = sem("samp_act")
        outa_in = sem("outa_in")
        xa_in = [sem(f"xa_in{j}") for j in range(2)]
        outa_done = sem("outa_done")
        x1_ready = sem("x1_ready")
        h1_ready = sem("h1_ready")
        h1_turned = sem("h1_turned")
        h1T_ready = sem("h1T_ready")
        wc_in = [sem(f"wc_in{j}") for j in range(3)]
        wg_in = sem("wg_in")
        fin_in = sem("fin_in")
        aS_zero = sem("aS_zero")
        lam_exp = sem("lam_exp")
        lam_ready = sem("lam_ready")
        pc_done = sem("pc_done")
        pc_act = sem("pc_act")
        conv_ready = sem("conv_ready")
        ta_ready = sem("ta_ready")
        m_ready = sem("m_ready")
        sq_ready = sem("sq_ready")
        h_ready = sem("h_ready")
        y_ready = sem("y_ready")
        outc_in = sem("outc_in")
        outc_done = sem("outc_done")
        o_ready = sem("o_ready")
        y_row_ready = sem("y_row_ready")
        y_out = [sem(f"y_out{j}") for j in range(2)]
        small_ready = sem("small_ready")
        small_pe = sem("small_pe")
        small_rows = sem("small_rows")
        small_sent = sem("small_sent")
        dve_chain = sem("dve_chain")
        pool_chain = sem("pool_chain")
        act_chain = sem("act_chain")

        w_rg = view(region_w, 19712, 2, KC, P)

        units = attention_units()
        steps = attention_steps()
        bank_use = bank_uses(steps)

        turn_order = [x for x in steps if x[0] == "turn"]
        nth_turn = {x[1]: f for f, x in enumerate(turn_order)}

        def spread(ap, n, axis=2):
            x = ap.unsqueeze(axis)
            shape = list(x.shape)
            shape[axis] = n
            return x.to_broadcast(shape)

        fm_count = []
        counts = {"act": 0, "dve": 0}
        for _, _, who in FM_A:
            counts[who] += 1
            fm_count.append(counts[who])

        def fm_wait(eng, n):
            eng.wait_ge(fm_act if FM_A[n][2] == "act" else fm_dve, fm_count[n])

        order_c = []
        for c in range(KC + 1):
            if c < KC:
                order_c.append(("x", c))
            if c >= 1:
                order_c += [("r", c - 1), ("i", c - 1)]
        order_c += [("z", c) for c in range(KC)]
        order_c_at = {x: n for n, x in enumerate(order_c)}

        def pc_of(n):
            if n == KC:
                return order_c_at[("z", 0)] + 1
            return order_c_at[("x", n) if n < KC else ("z", n - KC)] + 1

        small_tm = view(region_w, 3072, D)

        def sent_rows(i):
            return sum(2 if j >= (SEQ - WIN) // P else 1 for j in range(i % 2, i, 2))

        SAMP_DVE = ["keys0", "keys1", "means", "cmp", "logits", "probT", "res", "out"]
        SAMP_PE = ["keys0", "keys1", "cmp", "scores", "turned", "values", "out"]

        def samp_at(step, f):
            return f * len(SAMP_DVE) + SAMP_DVE.index(step) + 1

        def samp_pe_at(step, f):
            return f * len(SAMP_PE) + SAMP_PE.index(step) + 1

        block = ctx.enter_context(nc.Block())
        w_in_k = ins["w_in_a"][0].rearrange("(k p) n -> p k n", p=P)
        w_inc_k = ins["w_in_c"][0].rearrange("(k p) n -> p k n", p=P)
        hot_h = [(tril, "c_tril"), (far, "c_far"), (avg, "c_avg"), (rowok, "c_rowok"),
                 (headrow, "c_headrow"), (hsel, "c_hsel"), (two_i, "c_two_i"), (tsel, "c_tsel"), (tril_s, "c_tril_s")]
        const_loads = [(t[:, :], ins[n]) for t, n in hot_h]
        const_loads += [(hot[0:BUCKETS + 1, :], ins["c_hot"])]
        first_loads = [(ident[:, :], ins["c_ident"])]
        first_loads += [(vec_in[VEC[n]:VEC[n] + 8, :], ins[n][0].rearrange("(k p) -> k p", p=P))
                        for n in ("norm_a", "norm_c", "conv_b", "b_rg_a", "b_rg_x", "lru_lambda")]
        first_loads += [(vec_in[16:48, :], ins["conv_w"][0].rearrange("t (k p) -> (t k) p", p=P))]
        const_loads += [(wsp_in, ins["w_spatial"][0].rearrange("g i j -> i g j"))]
        const_loads += [(state_in[0:24, :], ins["state_lru_conv"][0].rearrange("s k c -> (s k) c")),
                        (state_in[24:32, :], ins["state_lru_h"][0])]
        const_loads += [(pe_in[0:BLK, kind, g * HD:(g + 1) * HD], ins["pe_cmp"][0, kind])
                        for kind in range(2) for g in range(2)]
        const_loads += [(b_sp[:, :, :], ins["b_spatial"][0].partition_broadcast(P)),
                        (ln_g, ins["gmlp_ln_g"][0].partition_broadcast(P)),
                        (ln_b, ins["gmlp_ln_b"][0].partition_broadcast(P)),
                        (b_gate[:, :], ins["b_gate_a"][0].partition_broadcast(P)),
                        (pt_tab, ins["page_table"].rearrange("s j -> (s j)").rearrange("(a n) -> a n", a=1)),
                        (rel_in[0:BUCKETS, :], ins["rel_bias"])]
        NCONST = 16 * len(const_loads)
        NFIRST = 16 * len(first_loads)

        @block.sync
        def _(sp):
            def load_x(i):
                if i >= 3:
                    sp.wait_ge(x_turned, i - 2)
                src = ins["x_prompt"][0, tok(i), :] if i < PT else ins["x_sample"].rearrange("s t d -> (s t) d")
                sp.dma_start(x_row[i % 3][0:rows(i), :], src).then_inc(x_in[i % 3], 16)

            load_x(0)
            with nc.allow_non_contiguous_dma("small vectors"):
                for dst, src in first_loads[0::2]:
                    sp.dma_start(dst, src).then_inc(first_in, 16)
            load_x(1)
            for k in range(0, KC, 4):
                sp.dma_start(w_kvg[:, k:k + 4, :], w_in_k[:, k:k + 4, KV0:KV0 + KVG]).then_inc(kvg_in, 16)
            load_x(2)
            for k in range(0, KC, 4):
                sp.dma_start(w_v[:, k:k + 4, :], w_in_k[:, k:k + 4, V0:V0 + 512]).then_inc(wv_in, 16)

            def load_fm(n):
                kind, j, _ = FM_A[n]
                if n >= 4:
                    sp.wait_ge(fm_done, n - 3)
                dst, s = w_fm[n % 4], fmw_in[n % 4]
                if kind == "q":
                    for g in range(2):
                        c0 = Q0 + (g * HPG + j) * HD
                        sp.dma_start(dst[:, :, g * HD:(g + 1) * HD], w_in_k[:, :, c0:c0 + HD]).then_inc(s, 16)
                else:
                    c0 = {"z": Z0, "zg": ZG0, "u": U0}[kind] + j * P
                    sp.dma_start(dst, w_in_k[:, :, c0:c0 + P]).then_inc(s, 16)

            for i in range(3, TILES):
                load_x(i)
            for n in range(len(FM_A)):
                load_fm(n)
            sp.wait_ge(rel_out, 16 * HEADS)
            sp.wait_ge(fm_done, len(FM_A))
            for h in range(HEADS):
                sp.dma_start(bias[:, h, :], rel_skewed(h, 1, P, P - 1, SEQ)).then_inc(bias_in, 16)

            def load_outa():
                sp.wait_ge(logits_ready, len(units))
                for k in range(0, KC, 4):
                    sp.dma_start(w_outa[:, k:k + 4, :],
                                 ins["w_out_a"][0].rearrange("(k p) n -> p k n", p=P)[:, k:k + 4, :]
                                 ).then_inc(outa_in, 16)

            for f in range(2):
                if f == 0:
                    sp.wait_ge(mix_used, TILES)
                    sp.wait_ge(vn_out, 16)
                    sp.wait_ge(rows_out[0], 16 * 8)
                    sp.wait_ge(rows_out[1], 16 * 6)
                    sp.wait_ge(consts_in, NCONST)
                    sp.wait_ge(scores_done, len(units))
                else:
                    load_outa()
                    sp.wait_ge(bank_empty, len(bank_use))
                for j in range(2 * HALF):
                    at = f * 2 * HALF + j
                    page = sp.value_load(pt_tab[0:1, at:at + 1], min_val=0,
                                         max_val=ins["cache_nsa"].shape[1] - 1)
                    sp.dma_start(pages_of[f][:, j, :],
                                 ins["cache_nsa"][0, bass.ds(page, 1), :, :, :, :].rearrange(
                                     "a t k g d -> (a t) (k g d)")).then_inc(samp_in[f], 16)
                for s in range(HALF):
                    sp.dma_start(wins_of[f][:, 2 * s:2 * s + 2, :],
                                 ins["cache_win"][0, f * HALF + s].rearrange(
                                     "(j t) k g d -> t j (k g d)", t=P)).then_inc(samp_in[f], 16)

            for i in range(TILES):
                if i == 0:
                    sp.wait_ge(samp_pe, samp_pe_at("values", 0))
                if i >= 2:
                    sp.wait_ge(x1_ready, i - 1)
                src = ins["x_prompt"][0, tok(i), :] if i < PT else ins["x_sample"].rearrange("s t d -> (s t) d")
                sp.dma_start(x_again[i % 2][0:rows(i), :], src).then_inc(xa_in[i % 2], 16)

            sp.dma_start(fin_g[:, :], ins["final_norm"].partition_broadcast(P)).then_inc(fin_in, 16)

            for n in range(2 * KC):
                if n == 0:
                    sp.wait_ge(outa_done, TILES)
                if n >= 3:
                    sp.wait_ge(pc_done, pc_of(n - 3))
                sp.dma_start(w_c[n % 3], w_inc_k[:, :, n * P:(n + 1) * P]).then_inc(wc_in[n % 3], 16)
                if n == 0:
                    sp.wait_ge(h1_turned, TILES)
                    for m, name in enumerate(("w_rg_a", "w_rg_x")):
                        sp.dma_start(w_rg[:, m], ins[name][0].rearrange("c i j -> i c j")).then_inc(wg_in, 16)
            sp.wait_ge(pc_done, pc_of(KC))
            for k in range(0, KC, 4):
                sp.dma_start(w_outc[:, k:k + 4, :],
                             ins["w_out_c"][0].rearrange("(k p) n -> p k n", p=P)[:, k:k + 4, :]
                             ).then_inc(outc_in, 16)

            sp.wait_ge(small_rows, 1)
            so = small_tm
            sp.dma_start(outs["lru_h_sample"][0], so[0:8, :]).then_inc(small_sent, 16)
            sp.dma_start(outs["lru_conv_sample"][0].rearrange("s k c -> (s k) c"), so[8:32, :]
                         ).then_inc(small_sent, 16)
            sp.dma_start(outs["lru_h_prompt"][0], so[32:33, :]).then_inc(small_sent, 16)
            sp.dma_start(outs["lru_conv_prompt"][0, 0], so[33:36, :]).then_inc(small_sent, 16)
            for i in range(TILES):
                sp.wait_ge(y_row_ready, i + 1)
                dst = outs["y_prompt"][0, tok(i), :] if i < PT else outs["y_sample"].rearrange("s t d -> (s t) d")
                sp.dma_start(dst, y_row[i % 2][0:rows(i), :]).then_inc(y_out[i % 2], 16)
            sp.wait_ge(small_sent, 64)
            sp.wait_ge(y_out[0], 16 * 5)
            sp.wait_ge(y_out[1], 16 * 4)

        @block.gpsimd
        def _(pool):
            pool.memset(rel_in[:, :], BIG).then_inc(zeroed, 1)
            pool.memset(wc_k[:, :], 0.0).then_inc(zeroed, 1)
            pool.memset(wc_v[:, :], 0.0).then_inc(zeroed, 1)
            pool.memset(wspT_s[:, :, :], 0.0).then_inc(zeroed, 1)
            pool.memset(half_neg[:, :], -0.5).then_inc(zeroed, 1)
            pool.memset(lc[:, :, :], 0.0).then_inc(zeroed, 1)
            pool.memset(kc_bd[:, :, :], 0.0).then_inc(zeroed, 1)
            pool.memset(qbd[:, :, :, :, :], 0.0).then_inc(zeroed, 1)
            pool.memset(bias_n[:, :, :], BIG).then_inc(zeroed, 1)
            pool.memset(bias_b[:, :], BIG).then_inc(zeroed, 1)

            rms_chain = [0]

            def rms(norm, i, want):
                r = rows(i)
                pool.wait_ge(squared, want)
                pool.tensor_scalar(ms[0:r, norm, i:i + 1], ss[0:r, norm, i:i + 1], 1.0 / D, EPS,
                                   ALU.mult, ALU.add).then_inc(pool_chain, 1)
                rms_chain[0] += 1
                pool.wait_ge(pool_chain, rms_chain[0])
                pool.tensor_tensor(rstd[0:r, norm, i:i + 1], ms[0:r, norm, i:i + 1], half_neg[0:r, :],
                                   ALU.pow).then_inc(scaled, 1)

            def ln(i):
                r = rows(i)
                pool.wait_ge(ln_stats, i + 1)
                pool.tensor_scalar(mv_e[0:r, i:i + 1], mv[0:r, i, 1:2], EPS, None, ALU.add
                                   ).then_inc(pool_chain, 1)
                rms_chain[0] += 1
                pool.wait_ge(pool_chain, rms_chain[0])
                pool.tensor_tensor(rstd_v[0:r, i:i + 1], mv_e[0:r, i:i + 1], half_neg[0:r, :],
                                   ALU.pow).then_inc(ln_scaled, 1)

            def ln_affine(i):
                r = rows(i)
                pool.wait_ge(ln_mid, i + 1)
                pool.wait_ge(consts_in, NCONST)
                pool.tensor_tensor(vn[0:r, i, :], vn[0:r, i, :], ln_g[0:r, :], ALU.mult).then_inc(pool_chain, 1)
                rms_chain[0] += 1
                pool.wait_ge(pool_chain, rms_chain[0])
                pool.tensor_tensor(vn[0:r, i, :], vn[0:r, i, :], ln_b[0:r, :], ALU.add).then_inc(vn_ready, 1)

            def send_rows(i):
                pool.wait_ge(kvA_out, i + 1)
                pool.wait_ge(kvB_out, i + 1)
                src = kv_row[i % 2]
                if i < PT:
                    pool.dma_start(outs["nsa_rows_prompt"][0, 0, tok(i)].rearrange("t k g d -> t (k g d)"),
                                   src[:, 0:512]).then_inc(rows_out[i % 2], 16)
                    if i >= (SEQ - WIN) // P:
                        at = i * P - (SEQ - WIN)
                        pool.dma_start(outs["win_rows_prompt"][0, 0, at:at + P].rearrange("t k g d -> t (k g d)"),
                                       src[:, 512:768]).then_inc(rows_out[i % 2], 16)
                else:
                    pool.dma_start(outs["nsa_rows_sample"][0].rearrange("s t k g d -> (s t) (k g d)"),
                                   src[0:NS, 0:512]).then_inc(rows_out[i % 2], 16)
                    pool.dma_start(outs["win_rows_sample"][0].rearrange("s t k g d -> (s t) (k g d)"),
                                   src[0:NS, 512:768]).then_inc(rows_out[i % 2], 16)

            rms(0, 0, 1)
            rms(0, 1, 2)
            for i in range(TILES):
                if i + 2 < TILES:
                    rms(0, i + 2, i + 3)
                if i >= 1:
                    ln(i - 1)
                    ln_affine(i - 1)
                send_rows(i)
                if i == 0:
                    pool.wait_ge(prep_dve, 2)
                    for h in range(HEADS):
                        pool.dma_start(bass.AP(rel_dram.tensor, h * P * (REL + 1), [[REL, 1], [REL + 1, P], [1, REL]]),
                                       spread(rel_rows[h:h + 1, :], P, 1)).then_inc(rel_out, 16)
            pool.wait_ge(zeroed, 10)
            for kind, t in ((0, wc_k), (1, wc_v)):
                for g in range(2):
                    pool.dma_start(t[g * HD:(g + 1) * HD, g * HD:(g + 1) * HD], ins["w_cmp"][0, kind]
                                   ).then_inc(diag_in, 16)
            corner = ins["w_spatial"][0, :, 0:NNEW, 0:NNEW]
            with nc.allow_non_contiguous_dma("4 x 4 corners of the spatial weights"):
                for g in range(4):
                    for s in range(NSEQ):
                        pool.dma_start(wspT_s[s * NNEW:(s + 1) * NNEW, g, s * NNEW:(s + 1) * NNEW],
                                       corner[g].rearrange("i j -> j i")).then_inc(diag_in, 16)
            ln(TILES - 1)
            ln_affine(TILES - 1)
            pool.wait_ge(vn_ready, TILES)
            pool.dma_start(outs["gmlp_v_sample"][0].rearrange("s t c -> (s t) c"), vn[0:NS, PT, :]
                           ).then_inc(vn_out, 16)
            pool.wait_ge(rel_out, 16 * HEADS)
            for s in range(HALF):
                o = 32 * s
                pool.dma_start(bias_c[o:o + 32, :],
                               rel_skewed(0, HEADS, NNEW, REL_TOP - PAST, PAST)
                               ).then_inc(bias_s_in, 16)
                for f in range(2):
                    c0 = (f * HALF + s) * NNEW
                    pool.dma_start(bias_n[o:o + 32, f, c0:c0 + NNEW],
                                   rel_skewed(0, HEADS, NNEW, REL_TOP, NNEW)
                                   ).then_inc(bias_s_in, 16)
            pool.wait_ge(mix_used, TILES)
            pool.memset(aS, 0.0).then_inc(aS_zero, 1)
            for i in range(TILES):
                rms(1, i, TILES + i + 1)
            for i in range(TILES):
                rms(2, i, 2 * TILES + i + 1)
            pool.wait_ge(vn_out, 16)
            pool.wait_ge(rows_out[0], 16 * 8)
            pool.wait_ge(rows_out[1], 16 * 6)

        @block.scalar
        def _(act):
            with nc.allow_non_contiguous_dma("small vectors"):
                for dst, src in first_loads[1::2]:
                    act.dma_start(dst, src).then_inc(first_in, 16)

            def square(i):
                act.wait_ge(x_in[i % 3], 16 * (i // 3 + 1))
                if i >= 1:
                    act.wait_ge(squared, i)
                r = rows(i)
                nc.scalar.activation(junk[0:r, :], x_row[i % 3][0:r, :], ACT.Square,
                                     accum_out=ss[0:r, 0, i:i + 1]).then_inc(squared, 1)

            square(0)
            square(1)
            with nc.allow_non_contiguous_dma("small vectors"):
                for n, (dst, src) in enumerate(const_loads):
                    if n == len(const_loads) - 1:
                        act.wait_ge(zeroed, 1)
                    act.dma_start(dst, src).then_inc(consts_in, 16)
            for i in range(TILES):
                r = rows(i)
                if i + 2 < TILES:
                    square(i + 2)
                act.wait_ge(kvA_done, i + 1)
                if i >= 2:
                    n = i % 2
                    act.wait_ge(rows_out[n], 16 * sent_rows(i))
                    act.wait_ge(k_turned, i - 1)
                nc.scalar.copy(kv_row[i % 2][0:r, 0:512], ps[0:r, 0, :])
                nc.scalar.copy(v_s[0:r, i, :], ps[0:r, 0, 384:512]).then_inc(kvA_out, 1)
                act.wait_ge(v_done, i + 1)
                nc.scalar.copy(vn[0:r, i, :], ps[0:r, 2, :]).then_inc(v_out, 1)

            act.wait_ge(kT_ready, TILES)
            act.wait_ge(v_done, TILES)
            act.wait_ge(rows_out[0], 16 * 8)
            act.wait_ge(rows_out[1], 16 * 6)
            act.wait_ge(squared, TILES)
            for b, (kT, vv) in enumerate(((kT_s, v_s), (kT_w, v_w))):
                for g in range(KVH):
                    gp = slice(g * HD, (g + 1) * HD)
                    for half in range(2):
                        nc.scalar.copy(k_hi[half * HD:(half + 1) * HD, b, g, :], kT[gp, 0:SEQ])
                    e = nc.scalar.copy(v_hl[:, b, g, :, 0:HD], vv[:, 0:PT, gp])
                e.then_inc(split_hi, 1)

            for n, (kind, j, who) in enumerate(FM_A):
                if who != "act":
                    continue
                act.wait_ge(fm_done, n + 1)
                dst = yT[:, j if kind == "z" else 4 + j, :].rearrange("p (a b) -> p a b", a=3)
                nc.scalar.activation(dst, ps[:, 3 * (n % 2):3 * (n % 2) + 3, 0:THIRD], ACT.Silu
                                     ).then_inc(fm_act, 1)
            act.wait_ge(kvB_out, TILES)
            nc.scalar.activation(gates[:, 0:PT, :], gates[:, 0:PT, :], ACT.Sigmoid)
            nc.scalar.activation(gates[0:NS, PT, :], gates[0:NS, PT, :], ACT.Sigmoid).then_inc(gates_ready, 1)

            for what, n in act_order(steps):
                if what == "split_q":
                    if n >= 2:
                        act.wait_ge(scores_done, 17 * (n - 1))
                    if n == 0:
                        act.wait_ge(fm_dve, counts["dve"])
                        act.wait_ge(split_lo, 2)
                        act.wait_ge(vn_out, 16)
                    for g in range(KVH):
                        gp = slice(g * HD, (g + 1) * HD)
                        e = nc.scalar.copy(q_hl[gp, n % 2, g * HPG:(g + 1) * HPG, :], qT[gp, :, tok(n)])
                    e.then_inc(q_hi, 1)
                elif what == "scores":
                    kind, i, h = units[n]
                    cols, _ = key_cols(kind, i)
                    act.wait_ge(logits_ready, n + 1)
                    if kind == "c":
                        nc.scalar.activation(lc[:, :, 0:cols], lc[:, :, 0:cols], ACT.Exp, scale=-1.0
                                             ).then_inc(probs_ready, 1)
                    else:
                        buf = probs[kind][:, h % HPG, 0:cols]
                        b = 1 if kind == "s" else 2
                        nc.scalar.activation(buf, buf, ACT.Exp, bias=negm[:, n % 4:n % 4 + 1], scale=-1.0,
                                             accum_out=sums[:, i % 2, b, h:h + 1]).then_inc(probs_ready, 1)
                elif what == "turn":
                    f = nth_turn[n]
                    k = bank_use[what, n]
                    act.wait_ge(turned, k + 1)
                    if f >= 2:
                        act.wait_ge(values_done, f - 1)
                    nc.scalar.copy(p_hl[:, f % 2, 0, :], ps[:, 4 + k % 2, :]).then_inc(p_hi, 1)
                elif what == "copy_o":
                    kind, i, g = GROUPS[n]
                    last = (n, key_cols(kind, i)[0] // P - 1)
                    act.wait_ge(values_done, nth_turn[last] + 1)
                    if n >= 2:
                        pi, pg = GROUPS[n - 2][1:]
                        act.wait_ge(turned, bank_use["back", (pi, pg)] + 1)
                    nc.scalar.copy(o_T[n % 2][:, :], ps[:, 6 + n % 2, :]).then_inc(o_copied, 1)

            for f in range(2):
                act.wait_ge(samp_dve, samp_at("logits", f))
                for b, (buf, w) in enumerate(((ls_c, 16), (ls_s, PAST + NS), (ls_w, PAST + NS))):
                    e = nc.scalar.activation(buf[:, 0:w], buf[:, 0:w], ACT.Exp, bias=neg_s[:, b:b + 1],
                                             scale=-1.0, accum_out=sum_s[:, b:b + 1])
                e.then_inc(samp_act, 1)

            for i in range(TILES):
                r = rows(i)
                act.wait_ge(x1_ready, i + 1)
                if i >= 2:
                    act.wait_ge(h1_turned, i - 1)
                nc.scalar.activation(h1[i % 2][0:r, :], x1[0:r, i, :], ACT.Square,
                                     accum_out=ss[0:r, 1, i:i + 1]).then_inc(squared, 1)

            act.wait_ge(lam_ready, 1)
            nc.scalar.activation(lam[:, 1, :], lam[:, 0, :], ACT.Exp, scale=-1.0).then_inc(lam_exp, 1)

            def bank3(n):
                return ps[:, 3 * (n % 2):3 * (n % 2) + 3, 0:THIRD]

            for n, (kind, c) in enumerate(order_c):
                act.wait_ge(pc_done, n + 1)
                if kind == "x":
                    if c >= 1:
                        act.wait_ge(conv_ready, c)
                    b0 = 3 * (n % 2)
                    nc.scalar.copy(xin[:, 3:3 + 2 * THIRD].rearrange("p (a b) -> p a b", a=2),
                                   ps[:, b0:b0 + 2, 0:THIRD])
                    nc.scalar.copy(xin[:, 3 + 2 * THIRD:3 + SEQ], ps[:, b0 + 2, 0:SEQ - 2 * THIRD])
                    nc.scalar.copy(xin_s[:, :, 3:7],
                                   ps[:, b0 + 2, SEQ - 2 * THIRD:THIRD].rearrange("p (s t) -> p s t", t=NNEW)
                                   ).then_inc(pc_act, 1)
                elif kind == "r":
                    if c >= 1:
                        act.wait_ge(h_ready, c)
                    if c == 0:
                        act.wait_ge(lam_ready, 2)
                    nc.scalar.activation(r_buf.rearrange("p (a b) -> p a b", a=3), bank3(n), ACT.Sigmoid,
                                         bias=vecT[:, VEC["b_rg_a"] + c:VEC["b_rg_a"] + c + 1]
                                         ).then_inc(pc_act, 1)
                    r_at = n
                elif kind == "i":
                    nc.scalar.activation(ig_buf.rearrange("p (a b) -> p a b", a=3), bank3(n), ACT.Sigmoid,
                                         bias=vecT[:, VEC["b_rg_x"] + c:VEC["b_rg_x"] + c + 1]
                                         ).then_inc(pc_act, 1)
                    act.wait_ge(pc_act, n + 1)
                    if c == 0:
                        act.wait_ge(aS_zero, 1)
                    nc.scalar.activation(t_buf, r_buf, ACT.Tanh, scale=lam[:, 4, c:c + 1])
                    nc.scalar.activation(aS[:, c, :, 1:NNEW + 1],
                                         r_buf[:, SEQ:TOK].rearrange("p (s t) -> p s t", t=NNEW),
                                         ACT.Exp, scale=lam[:, 5, c:c + 1]).then_inc(act_chain, 1)
                    act.wait_ge(act_chain, c + 1)
                    nc.scalar.activation(r_buf[:, 0:SEQ], r_buf[:, 0:SEQ], ACT.Exp, scale=lam[:, 5, c:c + 1]
                                         ).then_inc(ta_ready, 1)
                    act.wait_ge(m_ready, c + 1)
                    nc.scalar.activation(t_buf, t_buf, ACT.Sqrt).then_inc(sq_ready, 1)
                else:
                    if c == 0:
                        act.wait_ge(h_ready, KC)
                    if c >= 2:
                        act.wait_ge(y_ready, c - 1)
                    nc.scalar.activation(sz_buf[c % 2].rearrange("p (a b) -> p a b", a=3), bank3(n), ACT.Silu
                                         ).then_inc(pc_act, 1)

            for i in range(TILES):
                r = rows(i)
                act.wait_ge(o_ready, i + 1)
                if i >= 2:
                    act.wait_ge(y_out[i % 2], 16 * (i // 2))
                if i == 0:
                    act.wait_ge(y_ready, KC)
                nc.scalar.activation(y_row[i % 2][0:r, :], x1[0:r, i, :], ACT.Square,
                                     accum_out=ss[0:r, 2, i:i + 1]).then_inc(squared, 1)

        @block.tensor
        def _(pe):
            def mm(out, l, r, start, stop):
                return nc.tensor.matmul(out, l, r, start=start, stop=stop, skip_group_check=True)

            def flip(out, x):
                k = x.shape[0]
                return nc.tensor.transpose(out, x, ident[0:k, 0:k])

            pe.wait_ge(first_in, NFIRST)
            flip(ps[:, 3, 0:NVEC], vec_in[0:NVEC, :]).then_inc(prep_pe, 1)

            def prepare():
                pe.wait_ge(consts_in, NCONST)
                pe.wait_ge(zeroed, 10)
                pe.wait_ge(kvA_out, 1)
                pe.wait_ge(kvB_out, 1)
                pe.wait_ge(v_out, 1)
                for j in range(3):
                    m = mm(ps[0:HEADS, j, 0:REL // 3], rel_in[:, :], hot[0:BUCKETS + 1, j * 384:(j + 1) * 384],
                           True, True)
                m.then_inc(prep_pe, 1)
                for kind in range(2):
                    m = mm(ps[:, 3, 508 + kind:509 + kind], pe_in[0:BLK, kind, :], avg[0:BLK, 0:1], True, True)
                for g in range(4):
                    flip(ps[:, 4, g * P:(g + 1) * P], wsp_in[:, g, :])
                for k in range(KC):
                    m = flip(ps[:, 5, k * NS:(k + 1) * NS], state_in[0:NS, k * P:(k + 1) * P])
                m.then_inc(prep_pe, 1)

            def turn_x(i):
                pe.wait_ge(normed, i + 1)
                if i >= 1:
                    pe.wait_ge(hT_ready, i)
                r = rows(i)
                for k in range(KC):
                    m = flip(ps[:, 6 + k // 4, (k % 4) * P:(k % 4) * P + r], x_row[i % 3][0:r, k * P:(k + 1) * P])
                m.then_inc(x_turned, 1)

            turn_x(0)
            pe.wait_ge(kvg_in, 32)
            for i in range(TILES):
                r = rows(i)
                if i + 1 < TILES:
                    turn_x(i + 1)
                pe.wait_ge(hT_ready, i + 1)
                if i == 0:
                    pe.wait_ge(prep_dve, 1)
                else:
                    pe.wait_ge(kvA_out, i)
                    pe.wait_ge(kvB_out, i)
                    if i == 1:
                        pe.wait_ge(prep_dve, 5)
                for a, b, bank in ((0, 512, 0), (512, KVG, 1)):
                    for k in range(KC):
                        m = mm(ps[0:r, bank, 0:b - a], hT[:, k, tok(i)], w_kvg[:, k, a:b], k == 0, k == KC - 1)
                m.then_inc(kvA_done, 1)
                if i == 0:
                    pe.wait_ge(wv_in, 32)
                else:
                    pe.wait_ge(v_out, i)
                for k in range(KC):
                    m = mm(ps[0:r, 2, :], hT[:, k, tok(i)], w_v[:, k, :], k == 0, k == KC - 1)
                m.then_inc(v_done, 1)
                pe.wait_ge(kvA_out, i + 1)
                pe.wait_ge(kvB_out, i + 1)
                if i >= 1:
                    pe.wait_ge(kT_ready, i)
                row = kv_row[i % 2]
                flip(ps[:, 3, 0:r], row[0:r, 256:384])
                m = flip(ps[:, 3, P:P + r], row[0:r, 512:640])
                if i < PT:
                    for kind in range(2):
                        m = mm(ps[:, 3, 256 + 2 * kind:258 + 2 * kind], row[:, kind * P:(kind + 1) * P],
                               avg[:, :], True, True)
                m.then_inc(k_turned, 1)
                if i == 0:
                    prepare()

            for n, (kind, j, _) in enumerate(FM_A):
                times = 2 if kind == "q" else 1
                before = sum(2 if FM_A[m][0] == "q" else 1 for m in range(n % 4, n, 4))
                pe.wait_ge(fmw_in[n % 4], 16 * (before + times))
                if n == 0:
                    pe.wait_ge(kvB_out, TILES)
                    pe.wait_ge(v_out, TILES)
                elif n == 1:
                    pe.wait_ge(kT_ready, TILES)
                else:
                    fm_wait(pe, n - 2)
                for t in range(3):
                    for k in range(KC):
                        m = mm(ps[:, 3 * (n % 2) + t, 0:THIRD], w_fm[n % 4][:, k, :],
                               hT[:, k, t * THIRD:(t + 1) * THIRD], k == 0, k == KC - 1)
                m.then_inc(fm_done, 1)
                if n == 2:
                    pe.wait_ge(diag_in, 16 * 36)
                    pe.wait_ge(hT_ready, TILES)
                    pe.wait_ge(cmp_rep, 1)
                    mm(ps[:, 6, 0:NB], wc_k[:, :], mean_p[:, 0, :], True, True)
                    mm(ps[:, 6, P:2 * P], mean_rep[:, :, :].rearrange("p h n -> p (h n)"), wc_v[:, :],
                       True, True).then_inc(cmp_pe, 1)

            for i in range(TILES):
                r = rows(i)
                pe.wait_ge(vn_ready, i + 1)
                if i == 0:
                    pe.wait_ge(cmp_ready, 1)
                    pe.wait_ge(prep_dve, 6)
                if i >= 2:
                    pe.wait_ge(mix_used, i - 1)
                for g in range(4):
                    w = wspT[:, g, :] if i < PT else wspT_s[:, g, :]
                    m = mm(ps[:, 6 + i % 2, g * P:g * P + r], vn[0:r, i, g * P:(g + 1) * P], w, True, True)
                m.then_inc(mix_done, 1)

            pe.wait_ge(split_lo, 2)
            pe.wait_ge(fm_act, counts["act"])
            pe.wait_ge(fm_dve, counts["dve"])
            pe.wait_ge(mix_used, TILES)

            for what, n in steps:
                k = bank_use.get((what, n))
                if k is not None and k >= 2:
                    pe.wait_ge(bank_empty, k - 1)
                if what == "scores":
                    kind, i, h = units[n]
                    cols, first = key_cols(kind, i)
                    slot = 2 * (n % 2)
                    if n >= 2:
                        pe.wait_ge(logits_ready, n - 1)
                    if kind == "c":
                        pe.wait_ge(q_lo, i + 1)
                        for c in range(HPG):
                            m = mm(ps[:, slot, c * 2 * NB:(c + 1) * 2 * NB], qT[:, c, tok(i)],
                                   kc_bd[:, :, :].rearrange("p g n -> p (g n)"), True, True)
                    else:
                        g, b = h // HPG, 0 if kind == "s" else 1
                        gp = slice(g * HD, (g + 1) * HD)
                        for a in range(0, cols, 512):
                            w = min(512, cols - a)
                            o = ps[:, slot + a // 512, 0:w]
                            keys = slice(first + a, first + a + w)
                            mm(o, q_hl[:, i % 2, h, :], k_hi[:, b, g, keys], True, False)
                            m = mm(o, q_hl[gp, i % 2, h, :], k_lo[gp, b, keys], False, True)
                    m.then_inc(scores_done, 1)
                elif what == "c_turn":
                    pe.wait_ge(probs_ready, 17 * n + 1)
                    flip(ps[:, 4 + k % 2, 0:P], lc[:, :, :].rearrange("p h n -> p (h n)")).then_inc(turned, 1)
                elif what == "c_values":
                    pe.wait_ge(bank_empty, bank_use["c_turn", n] + 1)
                    mm(ps[:, 4 + k % 2, :], probT_c, vc_bd[:, :, :, :].rearrange("p g h d -> p (g h d)"),
                       True, True).then_inc(turned, 1)
                elif what == "turn":
                    j, b = n
                    kind, i, g = GROUPS[j]
                    pe.wait_ge(probs_ready, last_unit(j) + 1)
                    for c in range(HPG):
                        m = flip(ps[:, 4 + k % 2, c * P:(c + 1) * P], probs[kind][:, c, b * P:(b + 1) * P])
                    m.then_inc(turned, 1)
                elif what == "values":
                    j, b = n
                    kind, i, g = GROUPS[j]
                    cols, first = key_cols(kind, i)
                    f = nth_turn[n]
                    pe.wait_ge(bank_empty, bank_use["turn", n] + 1)
                    if b == 0 and j >= 2:
                        pe.wait_ge(o_copied, j - 1)
                    v = v_hl[:, 0 if kind == "s" else 1, g, first // P + b, :]
                    o = ps[:, 6 + j % 2, :]
                    mm(o, v, p_hl[:, f % 2, 0, :], b == 0, False)
                    mm(o, v, p_hl[:, f % 2, 1, :], False, b == cols // P - 1).then_inc(values_done, 1)
                elif what == "back":
                    i, g = n
                    pe.wait_ge(o_copied, 4 * i + 2 * g + 2)
                    for b in range(2):
                        for c in range(HPG):
                            m = mm(ps[:, 4 + k % 2, (b * HPG + c) * HD:(b * HPG + c + 1) * HD],
                                   o_T[b][:, c * P:(c + 1) * P], two_i[:, :], True, True)
                    m.then_inc(turned, 1)
                elif what == "out":
                    pe.wait_ge(acc_ready, 2 * (n + 1))
                    for j in range(4):
                        m = flip(ps[:, 4 + k % 2, j * P:(j + 1) * P], acc[:, j * P:(j + 1) * P])
                    m.then_inc(turned, 1)

            pe.wait_ge(bank_empty, len(bank_use))
            for f in range(2):
                pe.wait_ge(samp_in[f], 16 * (2 * HALF + HALF))
                pages, wins = pages_of[f], wins_of[f]
                pe.wait_ge(samp_q, 1)
                if f == 1:
                    pe.wait_ge(samp_dve, samp_at("out", 0))
                for j in range(2 * HALF):
                    m = flip(ps[:, j // 4, (j % 4) * P:(j % 4 + 1) * P], pages[:, j, 256:384])
                m.then_inc(samp_pe, 1)
                for j in range(2 * HALF):
                    m = flip(ps[:, 2 + j // 4, (j % 4) * P:(j % 4 + 1) * P], wins[:, j, 0:P])
                for j in range(2 * HALF):
                    for kind in range(2):
                        m = mm(ps[:, 4, 16 * kind + 2 * j:16 * kind + 2 * j + 2],
                               pages[:, j, kind * P:(kind + 1) * P], avg[:, :], True, True)
                m.then_inc(samp_pe, 1)
                pe.wait_ge(samp_dve, samp_at("means", f))
                mm(ps[:, 4, 64:80], wc_k[:, :], mean_s[:, 0, :], True, True)
                mm(ps[0:16, 4, P:2 * P], mean_s[:, 1, :], wc_v[:, :], True, True)
                mm(ps[:, 4, 256:256 + NG], tsel[:, f * SROWS:(f + 1) * SROWS], gates[0:NS, PT, :],
                   True, True).then_inc(samp_pe, 1)
                pe.wait_ge(samp_dve, samp_at("cmp", f))
                q4 = qbd[:, f * HALF:(f + 1) * HALF].rearrange("p s g c t -> p (s g c t)")
                for bank, kc, kn in ((5, kTc_s, 0), (6, kTc_w, 1)):
                    for s in range(HALF):
                        mm(ps[32 * s:32 * s + 32, bank, 0:PAST], q4[:, 32 * s:32 * s + 32],
                           kc[:, s * PAST:(s + 1) * PAST], True, True)
                    mm(ps[:, bank, PAST:PAST + NS], q4, k_new[:, kn, :], True, True)
                mm(ps[:, 7, 0:16], q4, kc_s, True, True).then_inc(samp_pe, 1)
                pe.wait_ge(samp_act, f + 1)
                for bank, buf in ((0, ls_s), (1, ls_w)):
                    flip(ps[:, bank, 0:P], buf[:, 0:P])
                    flip(ps[:, bank, P:2 * P], buf[:, P:2 * P])
                    flip(ps[0:NS, bank, 2 * P:3 * P], buf[:, PAST:PAST + NS])
                flip(ps[0:16, 2, 0:P], ls_c).then_inc(samp_pe, 1)
                pe.wait_ge(samp_dve, samp_at("probT", f))
                mm(ps[:, 3, 0:P], pt_c[0:16, :], vc_s[0:16, :], True, True)
                for b, pt, new, old in ((1, pt_s, v_s, lambda s, j: pages[:, 2 * s + j, 384:512]),
                                        (2, pt_w, v_w, lambda s, j: wins[:, 2 * s + j, P:2 * P])):
                    o = ps[:, 3, b * P:(b + 1) * P]
                    m = mm(o, pt[0:NS, 2, :], new[0:NS, PT, :], True, False)
                    for s in range(HALF):
                        for j in range(2):
                            m = mm(ps[32 * s:32 * s + 32, 3, b * P:(b + 1) * P],
                                   pt[:, j, 32 * s:32 * s + 32], old(s, j), False, j == 1)
                m.then_inc(samp_pe, 1)
                pe.wait_ge(samp_dve, samp_at("res", f))
                flip(ps[:, 4, 0:P], res_s).then_inc(samp_pe, 1)

            pe.wait_ge(samp_dve, samp_at("out", 1))
            pe.wait_ge(outa_in, 32)

            def turn_h1(i):
                pe.wait_ge(h1_ready, i + 1)
                if i >= 1:
                    pe.wait_ge(h1T_ready, i)
                r = rows(i)
                for k in range(KC):
                    m = flip(ps[:, 6 + k // 4, (k % 4) * P:(k % 4) * P + r], h1[i % 2][0:r, k * P:(k + 1) * P])
                m.then_inc(h1_turned, 1)

            for i in range(TILES):
                if i >= 3:
                    pe.wait_ge(x1_ready, i - 2)
                b0, r = 2 * (i % 3), rows(i)
                for n in range(2):
                    for k in range(KC):
                        m = mm(ps[0:r, b0 + n, :], yT[:, k, tok(i)], w_outa[:, k, n * 512:(n + 1) * 512],
                               k == 0, k == KC - 1)
                m.then_inc(outa_done, 1)
                if i >= 1:
                    turn_h1(i - 1)
            turn_h1(TILES - 1)

            pe.wait_ge(h1T_ready, TILES)
            for n, (kind, c) in enumerate(order_c):
                if n < 2:
                    pe.wait_ge(x1_ready, TILES)
                else:
                    pe.wait_ge(pc_act, n - 1)
                if kind in "xz":
                    w = c if kind == "x" else KC + c
                    pe.wait_ge(wc_in[w % 3], 16 * (w // 3 + 1))
                    for t in range(3):
                        for k in range(KC):
                            m = mm(ps[:, 3 * (n % 2) + t, 0:THIRD], w_c[w % 3][:, k, :],
                                   h1T[:, k, t * THIRD:(t + 1) * THIRD], k == 0, k == KC - 1)
                else:
                    pe.wait_ge(wg_in, 32)
                    pe.wait_ge(conv_ready, c + 1)
                    for t in range(3):
                        m = mm(ps[:, 3 * (n % 2) + t, 0:THIRD], w_rg[:, 0 if kind == "r" else 1, c, :],
                               xc[c % 2][:, t * THIRD:(t + 1) * THIRD], True, True)
                m.then_inc(pc_done, 1)

            pe.wait_ge(small_ready, 1)
            for c in range(KC):
                m = flip(ps[0:36, 6 + c // 4, (c % 4) * P:(c % 4 + 1) * P], small_out[:, c, :])
            m.then_inc(small_pe, 1)

            pe.wait_ge(outc_in, 32)
            pe.wait_ge(y_ready, KC)
            pe.wait_ge(pc_act, len(order_c))
            for i in range(TILES):
                if i >= 3:
                    pe.wait_ge(o_ready, i - 2)
                b0, r = 2 * (i % 3), rows(i)
                for n in range(2):
                    for k in range(KC):
                        m = mm(ps[0:r, b0 + n, :], yT[:, k, tok(i)], w_outc[:, k, n * 512:(n + 1) * 512],
                               k == 0, k == KC - 1)
                m.then_inc(outc_done, 1)

        @block.vector
        def _(dve):
            v = nc.vector
            chain = [0]

            def link(i):
                chain[0] += 1
                i.then_inc(dve_chain, 1)
                dve.wait_ge(dve_chain, chain[0])

            dve.wait_ge(prep_pe, 1)
            v.tensor_copy(vecT[:, :], ps[:, 3, 0:NVEC]).then_inc(prep_dve, 1)

            def prepared():
                dve.wait_ge(prep_pe, 2)
                v.tensor_copy(rel_rows[0:HEADS, :].rearrange("p (a b) -> p a b", a=3), ps[0:HEADS, 0:3, 0:REL // 3]
                              ).then_inc(prep_dve, 1)
                dve.wait_ge(prep_pe, 3)
                v.tensor_copy(pe_mean[:, :], ps[:, 3, 508:510]).then_inc(prep_dve, 1)
                v.tensor_tensor(wspT[:, :, :], ps[:, 4, :].rearrange("p (g j) -> p g j", g=4),
                                spread(tril[:, :], 4, 1), ALU.mult).then_inc(prep_dve, 1)
                v.tensor_copy(stT[:, :, :], ps[:, 5, 0:KC * NS].rearrange("p (k s) -> p k s", k=KC)
                              ).then_inc(prep_dve, 1)
                dve.wait_ge(prep_dve, 5)

            def scale_x(i):
                dve.wait_ge(scaled, i + 1)
                r = rows(i)
                x = x_row[i % 3][0:r, :]
                v.tensor_scalar(x, x, rstd[0:r, 0, i:i + 1], None, ALU.mult).then_inc(normed, 1)

            def feature_major(dst, i, norm):
                r = rows(i)
                src = ps[:, 6:8, :].rearrange("p b (k t) -> p (b k) t", t=P)[:, :, 0:r]
                return v.tensor_tensor(dst[:, :, tok(i)], src, spread(vecT[:, norm:norm + KC], r), ALU.mult)

            def keys(i):
                r = rows(i)
                dve.wait_ge(k_turned, i + 1)
                e = v.tensor_copy(kT_s[:, tok(i)], ps[:, 3, 0:r])
                e = v.tensor_copy(kT_w[:, tok(i)], ps[:, 3, P:P + r])
                if i < PT:
                    e = v.tensor_tensor(mean_p[:, :, 2 * i:2 * i + 2],
                                        ps[:, 3, 256:260].rearrange("p (k n) -> p k n", k=2),
                                        spread(pe_mean[:, :], 2), ALU.add)
                e.then_inc(kT_ready, 1)

            def ln_center(i):
                r = rows(i)
                dve.wait_ge(ln_scaled, i + 1)
                v.tensor_scalar(vn[0:r, i, :], vn[0:r, i, :], mv[0:r, i, 0:1], rstd_v[0:r, i:i + 1],
                                ALU.subtract, ALU.mult).then_inc(ln_mid, 1)

            def turned_x(i):
                dve.wait_ge(x_turned, i + 1)
                feature_major(hT, i, VEC["norm_a"]).then_inc(hT_ready, 1)

            scale_x(0)
            scale_x(1)
            dve.wait_ge(prep_dve, 1)
            turned_x(0)
            for i in range(TILES):
                r = rows(i)
                if i + 2 < TILES:
                    scale_x(i + 2)
                if i >= 1:
                    keys(i - 1)
                if i + 1 < TILES:
                    turned_x(i + 1)
                dve.wait_ge(kvA_done, i + 1)
                if i >= 2:
                    dve.wait_ge(rows_out[i % 2], 16 * sent_rows(i))
                v.tensor_copy(kv_row[i % 2][0:r, 512:768], ps[0:r, 1, 0:256])
                v.tensor_copy(v_w[0:r, i, :], ps[0:r, 1, P:2 * P])
                if i == 0:
                    dve.wait_ge(consts_in, NCONST)
                v.tensor_tensor(gates[0:r, i, :], ps[0:r, 1, 256:KVG - 512], b_gate[0:r, :], ALU.add
                                ).then_inc(kvB_out, 1)
                if i >= 1:
                    ln_center(i - 1)
                dve.wait_ge(v_out, i + 1)
                link(v.bn_stats(bn[0:r, :], vn[0:r, i, :]))
                v.bn_aggr(mv[0:r, i, :], bn[0:r, :]).then_inc(ln_stats, 1)
                if i == 0:
                    prepared()
            keys(TILES - 1)
            ln_center(TILES - 1)
            dve.wait_ge(kT_ready, TILES)
            v.tensor_copy(mean_rep[:, :, :], spread(mean_p[:, 1, :], HEADS, 1)).then_inc(cmp_rep, 1)

            def compressed():
                dve.wait_ge(cmp_pe, 1)
                v.tensor_copy(kc_bd[0:HD, 0, :], ps[0:HD, 6, 0:NB])
                v.tensor_copy(kc_bd[HD:P, 1, :], ps[HD:P, 6, 0:NB])
                v.tensor_tensor(vc_bd[:, :, :, :],
                                spread(ps[:, 6, P:2 * P].rearrange("p (g d) -> p g d", g=KVH), HPG, 2),
                                spread(headrow[:, :].rearrange("p (g h) -> p g h", g=KVH), HD, 3),
                                ALU.mult).then_inc(cmp_ready, 1)
                dve.wait_ge(diag_in, 16 * 36)
                v.tensor_tensor(wspT_s[:, :, :], wspT_s[:, :, :], spread(tril_s[:, :], 4, 1), ALU.mult
                                ).then_inc(prep_dve, 1)

            for b, (kT, vv) in enumerate(((kT_s, v_s), (kT_w, v_w))):
                v.tensor_copy(k_new[:, b, :], kT[:, SEQ:TOK])
                dve.wait_ge(split_hi, b + 1)
                for g in range(KVH):
                    gp = slice(g * HD, (g + 1) * HD)
                    v.tensor_tensor(k_lo[gp, b, :], kT[gp, 0:SEQ], k_hi[gp, b, g, :].bitcast(F32), ALU.subtract)
                    e = v.tensor_tensor(v_hl[:, b, g, :, HD:2 * HD], vv[:, 0:PT, gp],
                                        v_hl[:, b, g, :, 0:HD].bitcast(F32), ALU.subtract)
                e.then_inc(split_lo, 1)
            dve.wait_ge(split_lo, 2)

            dve.wait_ge(rel_out, 16 * HEADS)
            for n, (kind, j, who) in enumerate(FM_A):
                if n == 5:
                    compressed()
                if who != "dve":
                    continue
                dve.wait_ge(fm_done, n + 1)
                src = ps[:, 3 * (n % 2):3 * (n % 2) + 3, 0:THIRD]
                if kind == "u":
                    fm_wait(dve, n - 1)
                    y = yT[:, 4 + j, :].rearrange("p (a b) -> p a b", a=3)
                    v.tensor_tensor(y, src, y, ALU.mult).then_inc(fm_dve, 1)
                else:
                    v.tensor_scalar(qT[:, j, :].rearrange("p (a b) -> p a b", a=3), src, -HD ** -0.5, None,
                                    ALU.mult).then_inc(fm_dve, 1)
            for i in range(TILES):
                r = rows(i)
                dve.wait_ge(mix_done, i + 1)
                src = ps[:, 6 + i % 2, :].rearrange("p (g t) -> p g t", t=P)[:, :, 0:r]
                tmp = part_sb[:, 0:4 * r].rearrange("p (g t) -> p g t", g=4)
                if i >= 1:
                    dve.wait_ge(mix_used, i)
                if i < PT:
                    link(v.tensor_tensor(tmp, src, b_sp[:, :, :], ALU.add))
                else:
                    for g in range(4):
                        e = v.tensor_tensor(tmp[:, g, :].rearrange("p (s t) -> p s t", t=NNEW),
                                            src[:, g, :].rearrange("p (s t) -> p s t", t=NNEW),
                                            spread(b_sp[:, g, 0:NNEW], NSEQ, 1), ALU.add)
                    link(e)
                y = yT[:, 4:8, tok(i)]
                v.tensor_tensor(y, y, tmp, ALU.mult).then_inc(mix_used, 1)

            dve.wait_ge(bias_in, 16 * HEADS)
            v.tensor_tensor(bias_far, bias[:, :, SEQ - WCOLS:SEQ - WIN], spread(far[:, :], HEADS, 1), ALU.add
                            ).then_inc(far_ready, 1)
            dve.wait_ge(far_ready, 1)
            dve.wait_ge(gates_ready, 1)
            dve.wait_ge(vn_out, 16)

            for what, n in steps:
                k = bank_use.get((what, n))
                if k is not None:
                    dve.wait_ge(turned, k + 1)
                    bank = ps[:, 4 + k % 2, :]
                if what == "split_q":
                    dve.wait_ge(q_hi, n + 1)
                    for g in range(KVH):
                        gp = slice(g * HD, (g + 1) * HD)
                        other = slice((1 - g) * HD, (2 - g) * HD)
                        hs = slice(g * HPG, (g + 1) * HPG)
                        e = v.tensor_tensor(q_hl[other, n % 2, hs, :], qT[gp, :, tok(n)],
                                            q_hl[gp, n % 2, hs, :].bitcast(F32), ALU.subtract)
                    e.then_inc(q_lo, 1)
                elif what == "scores":
                    kind, i, h = units[n]
                    cols, first = key_cols(kind, i)
                    slot = 2 * (n % 2)
                    dve.wait_ge(scores_done, n + 1)
                    if kind == "c":
                        if i >= 1:
                            dve.wait_ge(turned, bank_use["c_turn", i - 1] + 1)
                            dve.wait_ge(logits_ready, n - 16)
                        m0 = 14 - 2 * i
                        src = ps[:, slot, 0:HPG * 2 * NB].rearrange("p (c g n) -> p g c n", c=HPG, g=KVH)
                        table = bias[:, :, BLK - 1::BLK]
                        for g in range(KVH):
                            hs = slice(g * HPG, (g + 1) * HPG)
                            e = v.tensor_tensor(lc[:, hs, 0:cols], src[:, g, :, 0:cols],
                                                table[:, hs, m0:m0 + cols], ALU.add)
                        link(e)
                        link(v.tensor_reduce(lmin[:, :], lc[:, :, 0:cols], AX.X, ALU.min))
                        v.tensor_tensor(lc[:, :, 0:cols], lc[:, :, 0:cols], spread(lmin[:, :], cols),
                                        ALU.subtract).then_inc(logits_ready, 1)
                    else:
                        buf = probs[kind][:, h % HPG, :]
                        m = negm[:, n % 4:n % 4 + 1]
                        src = flat[:, slot * 512:slot * 512 + cols]
                        if cols == WCOLS and kind == "w":
                            fm = far_min[:, n % 2:n % 2 + 1]
                            dve.wait_ge(logits_ready, n - 1)
                            link(v.tensor_tensor_reduce(buf[:, 0:P], src[:, 0:P], bias_far[:, h, :], 1.0, 3e38,
                                                        ALU.add, ALU.min, fm))
                            v.tensor_tensor_reduce(buf[:, P:cols], src[:, P:cols], bias[:, h, SEQ - WIN:SEQ],
                                                   1.0, fm, ALU.add, ALU.min, m
                                                   ).then_inc(logits_ready, 1)
                        else:
                            v.tensor_tensor_reduce(buf[:, 0:cols], src, bias[:, h, SEQ - cols:SEQ], 1.0, 3e38,
                                                   ALU.add, ALU.min, m).then_inc(logits_ready, 1)
                elif what == "c_turn":
                    v.tensor_copy(probT_c, bank[:, 0:P]).then_inc(bank_empty, 1)
                    dve.wait_ge(probs_ready, 17 * n + 1)
                    link(v.tensor_reduce(sums[:, n % 2, 0, :], lc[:, :, 0:2 * n + 2], AX.X, ALU.add))
                    link(v.reciprocal(inv[:, 0, :], sums[:, n % 2, 0, :]))
                    if n >= 1:
                        dve.wait_ge(bank_empty, bank_use["c_values", n - 1] + 1)
                    link(v.tensor_tensor(coef[:, 0, :], inv[:, 0, :], gates[:, n, 0:HEADS], ALU.mult))
                    if n == 0:
                        link(v.tensor_scalar(coef[:, 0, :], coef[:, 0, :], rowok[:, 0:1], None, ALU.mult))
                elif what == "c_values":
                    if n >= 1:
                        dve.wait_ge(acc_ready, 2 * n)
                    v.tensor_tensor(acc_c.rearrange("p (h d) -> p h d", d=HD),
                                    bank.rearrange("p (h d) -> p h d", d=HD),
                                    spread(coef[:, 0, :], HD), ALU.mult).then_inc(bank_empty, 1)
                elif what == "turn":
                    f = nth_turn[n]
                    dve.wait_ge(p_hi, f + 1)
                    v.tensor_tensor(p_hl[:, f % 2, 1, :], bank, p_hl[:, f % 2, 0, :].bitcast(F32),
                                    ALU.subtract).then_inc(bank_empty, 1)
                elif what == "back":
                    i, g = n
                    hs = slice(g * HPG, (g + 1) * HPG)
                    link(v.reciprocal(inv[:, 1:3, hs], sums[:, i % 2, 1:3, hs]))
                    g3 = gates[:, i, :].rearrange("p (b h) -> p b h", b=3)
                    link(v.tensor_tensor(coef[:, 1:3, hs], inv[:, 1:3, hs], g3[:, 1:3, hs], ALU.mult))
                    if i + g >= 1:
                        dve.wait_ge(acc_ready, 2 * i + g)
                    v.tensor_tensor(gated[:, :, :, :], bank.rearrange("p (b c d) -> p b c d", b=2, c=HPG),
                                    spread(coef[:, 1:3, hs], HD, 3), ALU.mult).then_inc(bank_empty, 1)
                    dve.wait_ge(bank_empty, k + 1)
                    if i >= 1:
                        dve.wait_ge(turned, bank_use["out", i - 1] + 1)
                    a = acc[:, g * 256:(g + 1) * 256].rearrange("p (c d) -> p c d", c=HPG)
                    ac = acc_c[:, g * 256:(g + 1) * 256].rearrange("p (c d) -> p c d", c=HPG)
                    link(v.tensor_tensor(a, gated[:, 0], ac, ALU.add))
                    v.tensor_tensor(a, gated[:, 1], a, ALU.add).then_inc(acc_ready, 1)
                elif what == "out":
                    y = yT[:, 0:4, tok(n)]
                    v.tensor_tensor(y, bank.rearrange("p (j t) -> p j t", t=P), y, ALU.mult
                                    ).then_inc(bank_empty, 1)

            dve.wait_ge(bias_s_in, 16 * 12)
            for s in range(HALF):
                o = slice(32 * s, 32 * s + 32)
                e = v.tensor_copy(bias_b[o, NBP * s:NBP * s + NBP], bias_c[o, BLK - 1::BLK])
            for g in range(KVH):
                gp = slice(g * HD, (g + 1) * HD)
                for s in range(NSEQ):
                    e = v.tensor_copy(qbd[gp, s, g, :, :], qT[gp, :, SEQ + s * NNEW:SEQ + (s + 1) * NNEW])
            e.then_inc(samp_q, 1)
            for f in range(2):
                if f == 1:
                    dve.wait_ge(samp_dve, samp_at("out", 0))
                dve.wait_ge(samp_pe, samp_pe_at("keys0", f))
                v.tensor_copy(kTc_s, flat[:, 0:1024]).then_inc(samp_dve, 1)
                dve.wait_ge(samp_pe, samp_pe_at("keys1", f))
                v.tensor_copy(kTc_w, flat[:, 1024:2048]).then_inc(samp_dve, 1)
                v.tensor_tensor(mean_s, ps[:, 4, 0:32].rearrange("p (k n) -> p k n", k=2),
                                spread(pe_mean[:, :], 16), ALU.add).then_inc(samp_dve, 1)
                dve.wait_ge(samp_pe, samp_pe_at("cmp", f))
                v.tensor_copy(kc_s, ps[:, 4, 64:80])
                v.tensor_copy(vc_s[0:16, :], ps[0:16, 4, P:2 * P])
                link(v.tensor_tensor(gate_rows, ps[:, 4, 256:256 + NG].rearrange("p (b h) -> p b h", b=3),
                                     spread(hsel[:, :], 3, 1), ALU.mult))
                v.tensor_reduce(coef_g, gate_rows, AX.X, ALU.add).then_inc(samp_dve, 1)
                dve.wait_ge(samp_pe, samp_pe_at("scores", f))

                def add_min(buf, src, tab, at, first):
                    return v.tensor_tensor_reduce(buf, src, tab, 1.0, first, ALU.add, ALU.min, at)

                e = add_min(ls_c, ps[:, 7, 0:16], bias_b[:, :], neg_s[:, 0:1], 3e38)
                for b, bank, buf in ((1, 5, ls_s), (2, 6, ls_w)):
                    link(add_min(buf[:, 0:PAST], ps[:, bank, 0:PAST], bias_c[:, :], lmin[:, b:b + 1], 3e38))
                    link(add_min(buf[:, PAST:PAST + NS], ps[:, bank, PAST:PAST + NS], bias_n[:, f, :],
                                 lmin[:, 4 + b:5 + b], 3e38))
                v.tensor_tensor(neg_s[:, 1:3], lmin[:, 1:3], lmin[:, 5:7], ALU.min).then_inc(samp_dve, 1)
                dve.wait_ge(samp_pe, samp_pe_at("turned", f))
                for bank, pt in ((0, pt_s), (1, pt_w)):
                    v.tensor_copy(pt[:, 0:2, :], ps[:, bank, 0:2 * P].rearrange("p (a b) -> p a b", a=2))
                    v.tensor_copy(pt[0:NS, 2, :], ps[0:NS, bank, 2 * P:3 * P])
                v.tensor_copy(pt_c[0:16, :], ps[0:16, 2, 0:P]).then_inc(samp_dve, 1)
                link(v.reciprocal(coef_s, sum_s))
                link(v.tensor_tensor(coef_s, coef_s, coef_g, ALU.mult))
                dve.wait_ge(samp_pe, samp_pe_at("values", f))
                link(v.tensor_scalar(res_s, ps[:, 3, 0:P], coef_s[:, 0:1], None, ALU.mult))
                link(v.scalar_tensor_tensor(out=res_s, in0=ps[:, 3, P:2 * P], scalar=coef_s[:, 1:2], in1=res_s,
                                            op0=ALU.mult, op1=ALU.add))
                v.scalar_tensor_tensor(out=res_s, in0=ps[:, 3, 2 * P:3 * P], scalar=coef_s[:, 2:3], in1=res_s,
                                       op0=ALU.mult, op1=ALU.add).then_inc(samp_dve, 1)
                dve.wait_ge(samp_pe, samp_pe_at("out", f))
                for h in range(HEADS):
                    g, j, o = h // HPG, h // 2, (h % 2) * HD
                    c0 = SEQ + f * HALF * NNEW
                    y = yT[o:o + HD, j, c0:c0 + HALF * NNEW].rearrange("p (s t) -> p s t", t=NNEW)
                    src = ps[g * HD:(g + 1) * HD, 4, 0:P].rearrange("p (s h t) -> p s h t", s=HALF, h=HEADS)
                    e = v.tensor_tensor(y, src[:, :, h, :], y, ALU.mult)
                e.then_inc(samp_dve, 1)

            lm = vecT[:, VEC["lru_lambda"]:VEC["lru_lambda"] + KC]
            link(v.tensor_scalar(lam[:, 2, :], lm, -1.0, None, ALU.mult))
            v.tensor_tensor(lam[:, 0, :], lm, lam[:, 2, :], ALU.max).then_inc(lam_ready, 1)

            def fm_h1(i):
                dve.wait_ge(h1_turned, i + 1)
                feature_major(h1T, i, VEC["norm_c"]).then_inc(h1T_ready, 1)

            for i in range(TILES):
                r, b0 = rows(i), 2 * (i % 3) * 512
                dve.wait_ge(outa_done, i + 1)
                dve.wait_ge(xa_in[i % 2], 16 * (i // 2 + 1))
                v.tensor_tensor(x1[0:r, i, :], flat[0:r, b0:b0 + D], x_again[i % 2][0:r, :], ALU.add
                                ).then_inc(x1_ready, 1)
                if i >= 1:
                    fm_h1(i - 1)
                dve.wait_ge(scaled, TILES + i + 1)
                v.tensor_scalar(h1[i % 2][0:r, :], x1[0:r, i, :], rstd[0:r, 1, i:i + 1], None, ALU.mult
                                ).then_inc(h1_ready, 1)
            fm_h1(TILES - 1)
            dve.wait_ge(lam_exp, 1)
            link(v.tensor_scalar(lam[:, 3, :], lam[:, 1, :], 2.0, None, ALU.add))
            link(v.reciprocal(lam[:, 3, :], lam[:, 3, :]))
            link(v.tensor_tensor(lam[:, 3, :], lam[:, 3, :], lam[:, 1, :], ALU.mult))
            link(v.tensor_tensor(lam[:, 4, :], lam[:, 3, :], lam[:, 3, :], ALU.mult))
            link(v.tensor_scalar(lam[:, 5, :], lam[:, 4, :], 1.0 / 17, 1.0 / 15, ALU.mult, ALU.add))
            for k in (13, 11, 9, 7, 5, 3, 1):
                link(v.tensor_tensor(lam[:, 5, :], lam[:, 5, :], lam[:, 4, :], ALU.mult))
                link(v.tensor_scalar(lam[:, 5, :], lam[:, 5, :], 1.0 / k, None, ALU.add))
            link(v.tensor_tensor(lam[:, 5, :], lam[:, 5, :], lam[:, 3, :], ALU.mult))
            link(v.tensor_scalar(lam[:, 5, :], lam[:, 5, :], 2.0, None, ALU.mult))
            link(v.tensor_scalar(lam[:, 2, :], lam[:, 2, :], 0.0, None, ALU.max))
            link(v.tensor_tensor(lam[:, 5, :], lam[:, 5, :], lam[:, 2, :], ALU.add))
            link(v.tensor_scalar(lam[:, 4, :], lam[:, 5, :], 8.0, None, ALU.mult))
            v.tensor_scalar(lam[:, 5, :], lam[:, 4, :], -1.0, None, ALU.mult).then_inc(lam_ready, 1)

            link(v.memset(xin[:, 0:3], 0.0))
            link(v.tensor_copy(bS[:, :, :, 0], stT[:, :, 24:32]))

            def conv(c):
                n = order_c_at[("x", c)]
                dve.wait_ge(pc_act, n + 1)
                if c >= 1:
                    dve.wait_ge(conv_ready, c)
                link(v.tensor_copy(xin_s[:, :, 0:3], stT[:, c, 0:24].rearrange("p (s k) -> p s k", k=3)))
                v.tensor_copy(small_out[:, c, 8:32].rearrange("p (s k) -> p s k", k=3), xin_s[:, :, 4:7])
                v.tensor_copy(small_out[:, c, 33:36], xin[:, SEQ:SEQ + 3])
                cw = VEC["conv_w"] + c
                cb = vecT[:, VEC["conv_b"] + c:VEC["conv_b"] + c + 1]
                outp = xc[c % 2][:, 0:SEQ]
                outs_ = xc[c % 2][:, SEQ:TOK].rearrange("p (s t) -> p s t", t=NNEW)
                v.tensor_scalar(outp, xin[:, 0:SEQ], vecT[:, cw:cw + 1], cb, ALU.mult, ALU.add)
                link(v.tensor_scalar(outs_, xin_s[:, :, 0:NNEW], vecT[:, cw:cw + 1], cb, ALU.mult, ALU.add))
                for k in range(1, 4):
                    w = vecT[:, cw + 8 * k:cw + 8 * k + 1]
                    v.scalar_tensor_tensor(out=outp, in0=xin[:, k:k + SEQ], scalar=w, in1=outp,
                                           op0=ALU.mult, op1=ALU.add)
                    e = v.scalar_tensor_tensor(out=outs_, in0=xin_s[:, :, k:k + NNEW], scalar=w, in1=outs_,
                                               op0=ALU.mult, op1=ALU.add)
                    if k < 3:
                        link(e)
                e.then_inc(conv_ready, 1)

            def recur(c):
                dve.wait_ge(ta_ready, c + 1)
                link(v.tensor_scalar(e_buf, t_buf, 1.0, None, ALU.add))
                link(v.reciprocal(e_buf, e_buf))
                v.scalar_tensor_tensor(out=t_buf, in0=t_buf, scalar=2.0, in1=e_buf, op0=ALU.mult, op1=ALU.mult
                                       ).then_inc(m_ready, 1)
                v.tensor_tensor(ig_buf, ig_buf, xc[c % 2], ALU.mult).then_inc(dve_chain, 1)
                chain[0] += 1
                dve.wait_ge(dve_chain, chain[0])
                dve.wait_ge(sq_ready, c + 1)
                link(v.tensor_tensor(t_buf, t_buf, ig_buf, ALU.mult))
                v.tensor_copy(bS[:, c, :, 1:NNEW + 1], t_buf[:, SEQ:TOK].rearrange("p (s t) -> p s t", t=NNEW))
                v.tensor_tensor_scan(yT[:, c, 0:SEQ], r_buf[:, 0:SEQ], t_buf[:, 0:SEQ], 0.0, ALU.mult, ALU.add
                                     ).then_inc(h_ready, 1)

            for c in range(KC):
                if c < 1:
                    conv(c)
                if c + 1 < KC:
                    conv(c + 1)
                recur(c)
            hS = t_buf[:, 0:KC * NSEQ * (NNEW + 1)]
            dve.wait_ge(h_ready, KC)
            link(v.tensor_tensor_scan(hS, aS[:, :, :, :].rearrange("p c s t -> p (c s t)"),
                                      bS[:, :, :, :].rearrange("p c s t -> p (c s t)"), 0.0,
                                      ALU.mult, ALU.add))
            hS4 = hS.rearrange("p (c s t) -> p c s t", c=KC, s=NSEQ)
            for c in range(KC):
                v.tensor_copy(yT[:, c, SEQ:TOK].rearrange("p (s t) -> p s t", t=NNEW), hS4[:, c, :, 1:NNEW + 1])
            v.tensor_copy(small_out[:, :, 0:8], hS4[:, :, :, NNEW])
            v.tensor_copy(small_out[:, :, 32:33], yT[:, :, SEQ - 1:SEQ]).then_inc(small_ready, 1)
            dve.wait_ge(small_ready, 1)
            for c in range(KC):
                n = order_c_at[("z", c)]
                dve.wait_ge(pc_act, n + 1)
                v.tensor_tensor(yT[:, c, :], yT[:, c, :], sz_buf[c % 2], ALU.mult).then_inc(y_ready, 1)
            dve.wait_ge(small_pe, 1)
            v.tensor_copy(small_tm[0:36, :], flat[0:36, 6 * 512:8 * 512]).then_inc(small_rows, 1)

            def finish(i):
                r = rows(i)
                if i == 0:
                    dve.wait_ge(fin_in, 16)
                dve.wait_ge(scaled, 2 * TILES + i + 1)
                v.scalar_tensor_tensor(out=y_row[i % 2][0:r, :], in0=x1[0:r, i, :], scalar=rstd[0:r, 2, i:i + 1],
                                       in1=fin_g[0:r, :], op0=ALU.mult, op1=ALU.mult).then_inc(y_row_ready, 1)

            for i in range(TILES):
                r, b0 = rows(i), 2 * (i % 3) * 512
                dve.wait_ge(outc_done, i + 1)
                v.tensor_tensor(x1[0:r, i, :], flat[0:r, b0:b0 + D], x1[0:r, i, :], ALU.add).then_inc(o_ready, 1)
                if i >= 1:
                    finish(i - 1)
            finish(TILES - 1)


_WEIGHTS = ["x_prompt", "x_sample", "cache_nsa", "cache_win", "state_lru_h", "state_lru_conv", "page_table",
            "norm_a", "w_in_a", "b_gate_a", "pe_cmp", "w_cmp", "gmlp_ln_g", "gmlp_ln_b", "w_spatial",
            "b_spatial", "w_out_a", "norm_c", "w_in_c", "conv_w", "conv_b", "w_rg_a", "b_rg_a", "w_rg_x",
            "b_rg_x", "lru_lambda", "w_out_c", "rel_bias", "final_norm"]
_OUTS = [("y_prompt", (1, SEQ, D)), ("y_sample", (NSEQ, NNEW, D)),
         ("nsa_rows_prompt", (1, 1, SEQ, 4, KVH, HD)), ("nsa_rows_sample", (1, NSEQ, NNEW, 4, KVH, HD)),
         ("win_rows_prompt", (1, 1, WIN, 2, KVH, HD)), ("win_rows_sample", (1, NSEQ, NNEW, 2, KVH, HD)),
         ("gmlp_v_sample", (1, NSEQ, NNEW, 512)), ("lru_h_prompt", (1, 1, D)), ("lru_h_sample", (1, NSEQ, D)),
         ("lru_conv_prompt", (1, 1, 3, D)), ("lru_conv_sample", (1, NSEQ, 3, D))]


def kernel(**inputs):
    import concourse.bacc as _bacc
    from concourse.bass_utils import run_bass_kernel_spmd as _run

    nc = _bacc.Bacc("TRN2", target_bir_lowering=False, num_devices=1)
    arrays, ins, outs = {}, {}, {}
    given = {n: np.ascontiguousarray(inputs[n]) for n in _WEIGHTS}
    given.update(constants())
    for name, a in given.items():
        arrays[f"in_{name}"] = a
        ins[name] = nc.dram_tensor(f"in_{name}", a.shape, mybir.dt.from_np(a.dtype), kind="ExternalInput").ap()
    for name, shape in _OUTS:
        outs[name] = nc.dram_tensor(f"out_{name}", shape, F32, kind="ExternalOutput").ap()
    build(nc, ins, outs)
    r = _run(nc, [arrays], core_ids=[0])
    return tuple(r.results[0][f"out_{name}"] for name, _ in _OUTS)
```

```python
import math
from contextlib import ExitStack

import concourse.bass as bass
from concourse import mybir
import numpy as np

ALU = mybir.AluOpType
ACT = mybir.ActivationFunctionType
AX = mybir.AxisListType
F32 = mybir.dt.float32
F32R = mybir.dt.float32r

P = 128
D = 1024
KC = D // P
SEQ = 1024
NSEQ, NNEW = 8, 4
NS = NSEQ * NNEW
TOK = SEQ + NS
TILES = SEQ // P + 1
PT = SEQ // P
THIRD = TOK // 3
HEADS, KVH, HD = 8, 2, 64
HPG = HEADS // KVH
KV = 6 * KVH * HD
NG = 3 * HEADS
KVG = KV + NG
BLK = 64
NB = SEQ // BLK
WIN = 512
WCOLS = WIN + P
PAST = 256
PAGE = 128
NBP = PAST // BLK
BUCKETS, MAX_DIST = 32, 1024
REL = SEQ + P
REL_TOP = SEQ - 1
BIG = 1e30
EPS = 1e-6
Q0, KV0, G0, Z0 = 0, 512, 512 + KV, 512 + KV + NG
U0, V0, ZG0 = Z0 + 512, Z0 + 1024, Z0 + 1536
HALF = NSEQ // 2
SROWS = HALF * HEADS * NNEW
VEC = {"norm_a": 0, "norm_c": 8, "conv_w": 16, "conv_b": 48, "b_rg_a": 56, "b_rg_x": 64, "lru_lambda": 72}
NVEC = 80


def rows(i):
    return P if i < PT else NS


def tok(i):
    return slice(i * P, i * P + rows(i))


def constants():
    c = {}
    d = np.arange(REL_TOP, REL_TOP - REL, -1)
    exact = BUCKETS // 2
    df = np.maximum(d, 1).astype(np.float32)
    large = exact + (np.log(df / np.float32(exact)) / np.float32(math.log(MAX_DIST / exact))
                     * np.float32(BUCKETS - exact)).astype(np.int32)
    bucket = np.where(d < exact, d, np.minimum(large, BUCKETS - 1))
    hot = np.zeros((BUCKETS + 1, REL), np.float32)
    hot[bucket[d >= 0], np.nonzero(d >= 0)[0]] = -1.0
    hot[BUCKETS, d < 0] = 1.0
    c["c_hot"] = hot
    k = np.arange(P)
    c["c_ident"] = np.eye(P, dtype=np.float32)
    c["c_two_i"] = np.concatenate([np.eye(HD, dtype=np.float32)] * 2)
    c["c_tril"] = (k[:, None] <= k[None, :]).astype(np.float32)
    c["c_far"] = np.where(k[None, :] < k[:, None], BIG, 0.0).astype(np.float32)
    c["c_avg"] = ((k[:, None] // BLK == np.arange(2)[None, :]) / BLK).astype(np.float32)
    c["c_rowok"] = (k[:, None] >= BLK - 1).astype(np.float32)
    c["c_headrow"] = (k[:, None] // NB == np.arange(HEADS)[None, :]).astype(np.float32)
    r = np.arange(SROWS)
    s, h, t = r // (HEADS * NNEW), r // NNEW % HEADS, r % NNEW
    c["c_hsel"] = (h[:, None] == np.arange(HEADS)[None, :]).astype(np.float32)
    n = np.arange(NS)
    c["c_tsel"] = np.concatenate(
        [(n[:, None] == ((HALF * f + s) * NNEW + t)[None, :]) for f in range(2)], 1).astype(np.float32)
    c["c_tril_s"] = ((n[:, None] // NNEW == n[None, :] // NNEW)
                     & (n[:, None] % NNEW <= n[None, :] % NNEW)).astype(np.float32)
    return c


def attention_units():
    units = []
    for i in range(PT):
        units.append(("c", i, 0))
        for g in range(KVH):
            units += [(kind, i, g * HPG + c) for kind in "sw" for c in range(HPG)]
    return units


GROUPS = [(kind, i, g) for i in range(PT) for g in range(KVH) for kind in "sw"]


def last_unit(j):
    return 17 * (j // 4) + 4 * (j % 4) + 4


def key_cols(kind, i):
    if kind == "c":
        return 2 * i + 2, 0
    first = 0 if kind == "s" else max(0, i - WIN // P)
    return (i + 1 - first) * P, first * P


FEW = 2


def attention_steps():
    steps = [("split_q", 0)] + [("scores", n) for n in range(1 + HPG)]
    soon = [[2, ("c_turn", 0)], [3, ("c_values", 0)]]
    unit = 1 + HPG
    waiting = []

    def one_block():
        for x in soon:
            x[0] -= 1
        for x in [x for x in soon if x[0] <= 0]:
            soon.remove(x)
            steps.append(x[1])

    def values():
        j, b = waiting.pop(0)
        kind, i, g = GROUPS[j]
        steps.append(("values", (j, b)))
        if b == key_cols(kind, i)[0] // P - 1:
            steps.append(("copy_o", j))
            if kind == "w":
                soon.append([1 if i == 0 and g == 0 else 2, ("back", (i, g))])
                if g == KVH - 1:
                    soon.append([4, ("out", i)])

    for j, (kind, i, g) in enumerate(GROUPS):
        nk = key_cols(kind, i)[0] // P
        more = []
        if j + 1 < len(GROUPS):
            more = list(range(unit, last_unit(j + 1) + 1))
            unit = max(unit, last_unit(j + 1) + 1)
        if j % 4 == 3 and i + 1 < PT:
            soon += [[nk + 4, ("c_turn", i + 1)], [nk + 6, ("c_values", i + 1)]]
        if j % 4 == 1 and i + 1 < PT:
            steps.append(("split_q", i + 1))
        for b in range(nk):
            if len(waiting) == 2:
                values()
            steps.append(("turn", (j, b)))
            waiting.append((j, b))
            take = -(-len(more) // max(1, nk - 1 - b))
            for n in more[:take]:
                steps.append(("scores", n))
            more = more[take:]
            if b == nk - 1 and j + 2 < len(GROUPS) and key_cols(*GROUPS[j + 1][:2])[0] // P <= FEW:
                steps += [("scores", n) for n in range(unit, last_unit(j + 2) + 1)]
                unit = last_unit(j + 2) + 1
            one_block()
    while waiting:
        values()
        one_block()
    while soon:
        one_block()
    return steps


def act_order(steps):
    order, pending = [], []
    for x in steps:
        if x[0] == "scores":
            pending.append(x)
            continue
        need = -1
        if x[0] == "turn":
            need = last_unit(x[1][0])
        elif x[0] == "c_turn":
            need = 17 * x[1]
        while pending and pending[0][1] <= need:
            order.append(pending.pop(0))
        order.append(x)
        if x[0] == "turn":
            order += pending
            pending = []
    return order + pending


def bank_uses(steps):
    return {x: k for k, x in enumerate(x for x in steps
                                       if x[0] in ("c_turn", "c_values", "turn", "back", "out"))}


FM_A = ([("z", j, "act") for j in range(4)]
        + [x for j in range(4) for x in (("zg", j, "act"), ("u", j, "dve"))]
        + [("q", j, "dve") for j in range(4)])


MIX_BEFORE = [range(0, 2), range(2, 4), range(4, 6), range(6, TILES)]


class Half:
    pass


def build(nc, ins, outs):
    ctx = ExitStack()
    with ctx:
        def sb(name, shape):
            return ctx.enter_context(nc.sbuf_tensor(name, shape, F32))

        def sem(name):
            return ctx.enter_context(nc.semaphore(name))

        ps = ctx.enter_context(nc.psum_tensor("ps", [P, 8, 512], F32))
        flat = ps[:, :, :].rearrange("p b n -> p (b n)")
        arena_cols = [8 * TOK, 8640, 27904]
        sb("arena", [P, sum(arena_cols)])
        arena_at = nc.sbuf_base - 4 * sum(arena_cols)

        def placed(name, at, shape, dt):
            return nc.alloc_sbuf_tensor_at(name, shape, dt, offset=arena_at + 4 * at)

        AT_Q, AT_W = arena_cols[0], arena_cols[0] + arena_cols[1]
        region_y = placed("region_y", 0, [P, arena_cols[0]], F32)
        region_q = placed("region_q", AT_Q, [P, arena_cols[1]], F32)
        region_w = placed("region_w", AT_W, [P, arena_cols[2]], F32)

        def view(region, at, *shape):
            n = int(np.prod(shape))
            v = region[:, at:at + n]
            if len(shape) == 2:
                v = v.rearrange("p (a b) -> p a b", a=shape[0])
            if len(shape) == 3:
                v = v.rearrange("p (a b c) -> p a b c", a=shape[0], b=shape[1])
            return v

        w_kvg = view(region_y, 0, KC, KVG)
        yT = view(region_y, 0, 8, TOK)
        hot = view(region_q, 0, REL)
        rel_rows = view(region_q, REL, REL)
        wsp_in = view(region_q, 2 * REL, 4, P)
        vec_in = view(region_q, 2 * REL + 512, P)
        state_in = view(region_q, 2 * REL + 640, D)
        pe_in = view(region_q, 2 * REL + 640 + D, 2, P)
        qT = view(region_q, 0, HPG, TOK)
        kT_s = view(region_q, 4 * TOK, TOK)
        kT_w = view(region_q, 5 * TOK, TOK)
        v_s = view(region_q, 6 * TOK, TILES, P)
        v_w = view(region_q, 6 * TOK + TILES * P, TILES, P)
        h1T = view(region_q, 0, KC, TOK)
        hT = view(region_w, 0, KC, TOK)
        w_v = view(region_w, 8448, KC, 512)
        vn = view(region_w, 16896, TILES, 512)
        kv_row = [view(region_w, 21504 + KVG * j, KVG) for j in range(2)]
        x_row = [view(region_w, 23088 + D * j, D) for j in range(3)]
        junk = view(region_w, 26160, D)
        hT_lo = placed("hT_lo", AT_W, [P, KC, TOK], F32R)
        hT_hi = placed("hT_hi", AT_W + 8448, [P, KC, TOK], F32R)
        w_fm = [view(region_w, 23552 + D * j, KC, P) for j in range(2)]
        w_fm_hl = [placed(f"w_fm_hl{j}", AT_W + at, [P, 2, KC, P], F32R) for j, at in enumerate((25600, 21504))]
        bias = view(region_w, 0, HEADS, SEQ)
        k_hi = placed("k_hi", AT_W + 8448, [P, 2, KVH, SEQ], F32R)
        k_lo = placed("k_lo", AT_W + 25600, [P, 2, SEQ], F32R)
        v_hl = placed("v_hl", AT_W + 21504, [P, 2, KVH, PT, 2 * HD], F32R)
        q_hl = placed("q_hl", AT_Q + 4 * TOK, [P, 2, HEADS, P], F32R)
        p_hl = placed("p_hl", AT_W + 19200, [P, 2, 2, 512], F32R)
        probs = {"s": view(region_w, 12544, HPG, SEQ), "w": view(region_w, 16640, HPG, WCOLS)}
        bias_far = view(region_q, 6 * TOK, HEADS, P)
        probT_c = view(region_q, 6 * TOK + TILES * P, P)
        pages_of = [view(region_w, 8448, 2 * HALF, 512), view(region_w, 21504, 2 * HALF, 512)]
        wins_of = [view(region_w, 25600, 2 * HALF, 256), view(region_w, 12544, 2 * HALF, 256)]

        def half_buffers(f):
            at = 17408 + 1840 * f
            kT = (region_w, 14592) if f == 0 else (region_q, 4 * TOK)
            h = Half()
            h.pages, h.wins = pages_of[f], wins_of[f]
            h.kTc = [view(kT[0], kT[1] + D * b, 2 * HALF * P) for b in range(2)]
            h.logits = [view(region_w, at + 288 * b, PAST + NS) for b in range(2)]
            h.logits_c = view(region_w, at + 576, 16)
            h.probT = [view(region_w, at + 592 + 384 * b, 3, P) for b in range(2)]
            h.probT_c = view(region_w, at + 1360, P)
            h.result = view(region_w, at + 1488, P)
            h.mean = view(region_w, at + 1616, 2, 16)
            h.kc = view(region_w, at + 1648, 16)
            h.vc = view(region_w, at + 1664, P)
            h.gate_rows = view(region_w, at + 1792, 3, HEADS)
            h.coef = view(region_w, at + 1816, 3)
            h.gate = view(region_w, at + 1819, 3)
            h.sums = view(region_w, at + 1822, 3)
            h.neg = view(region_w, at + 1825, 3)
            h.least = view(region_w, at + 1828, 4)
            return h

        halves = [half_buffers(f) for f in range(2)]
        w_outa = view(region_w, 0, KC, D)
        w_outa_lo = placed("w_outa_lo", AT_W, [P, KC, D], F32R)
        w_outa_hi = placed("w_outa_hi", AT_W + 16640, [P, KC, D], F32R)
        ya_hl = [placed(f"ya_hl{j}", AT_W + at, [P, 2, KC, P], F32R) for j, at in enumerate((24832, 13312))]
        x1 = [view(region_w, 8192 + D * j, D) for j in range(3)]
        h1 = [view(region_w, 11264 + D * j, D) for j in range(2)]
        h1T_lo = placed("h1T_lo", AT_Q, [P, KC, TOK], F32R)
        h1T_hi = placed("h1T_hi", 0, [P, KC, TOK], F32R)
        w_c = [view(region_w, at, KC, P) for at in (15616, 0)]
        w_c_hl = [placed(f"w_c_hl{j}", AT_W + at, [P, 2, KC, P], F32R) for j, at in enumerate((16640, 1024))]
        sz_buf = [view(region_w, 3072 + TOK * j, TOK) for j in range(2)]
        xin = view(region_w, 6144, 3 + SEQ)
        xin_s = view(region_w, 6144 + 1027, NSEQ, 7)
        xc = [view(region_w, 7232 + TOK * j, TOK) for j in range(2)]
        r_buf = view(region_w, 9344, TOK)
        t_buf = view(region_w, 10400, TOK)
        e_buf = view(region_w, 11456, TOK)
        ig_buf = view(region_w, 12512, TOK)
        w_rg = view(region_w, 13568, 2, KC, P)
        w_outc = view(region_w, 6144, KC, D)
        states = view(region_w, 19456, KC, TOK)
        w_outc_hi = placed("w_outc_hi", 0, [P, KC, D], F32R)
        w_outc_lo = placed("w_outc_lo", AT_W + 6144, [P, KC, D], F32R)
        y_hi = placed("y_hi", AT_Q, [P, KC, TOK], F32R)
        y_lo = placed("y_lo", AT_W + 19456, [P, KC, TOK], F32R)
        small_tm = view(region_w, 0, D)
        x1_again = [view(region_w, at, D) for at in (1024, 2048, 15616)]
        y_row = [view(region_w, 16640 + D * j, D) for j in range(2)]

        ident = sb("ident", [P, P])
        tril = sb("tril", [P, P])
        far = sb("far", [P, P])
        avg = sb("avg", [P, 2])
        rowok = sb("rowok", [P, 1])
        headrow = sb("headrow", [P, HEADS])
        hsel = sb("hsel", [P, HEADS])
        tsel = sb("tsel", [NS, 2 * SROWS])
        tril_s = sb("tril_s", [NS, NS])
        rel_in = sb("rel_in", [BUCKETS + 1, HEADS])
        vecT = sb("vecT", [P, NVEC])
        region_m = sb("region_m", [P, 1024])
        wspT = view(region_m, 0, 4, P)
        b_sp = view(region_m, 512, 4, P)
        aS = view(region_m, 0, KC, NSEQ, NNEW + 1)
        bS = view(region_m, 320, KC, NSEQ, NNEW + 1)
        small_out = view(region_m, 640, KC, 36)
        region_g = sb("region_g", [P, D])
        ln_g = region_g[:, 0:512]
        ln_b = region_g[:, 512:1024]
        fin_g = region_g
        wspT_s = sb("wspT_s", [NS, 4, NS])
        b_gate = sb("b_gate", [P, NG])
        wc_k = sb("wc_k", [P, P])
        wc_v = sb("wc_v", [P, P])
        pe_mean = sb("pe_mean", [P, 2])
        mean_p = sb("mean_p", [P, 2, NB])
        mean_rep = sb("mean_rep", [P, HEADS, NB])
        kc_bd = sb("kc_bd", [P, KVH, NB])
        vc_bd = sb("vc_bd", [P, KVH, HPG, HD])
        gates = sb("gates", [P, TILES, NG])
        half_neg = sb("half_neg", [P, 1])
        ss = sb("ss", [P, 3, TILES])
        ms = sb("ms", [P, 3, TILES])
        rstd = sb("rstd", [P, 3, TILES])
        bn = sb("bn", [P, 6])
        mv = sb("mv", [P, TILES, 2])
        mv_e = sb("mv_e", [P, TILES])
        rstd_v = sb("rstd_v", [P, TILES])
        negm = sb("negm", [P, 16])
        sums = sb("sums", [P, 2, 3, HEADS])
        inv = sb("inv", [P, 3, HEADS])
        coef = sb("coef", [P, 3, HEADS])
        lc = sb("lc", [P, HEADS, NB])
        lmin = sb("lmin", [P, HEADS])
        acc = sb("acc", [P, 512])
        acc_c = view(region_q, 6 * TOK + TILES * P + P, 512)
        far_min = sb("far_min", [P, 2])
        part_sb = sb("part_sb", [P, 512])
        part_2 = sb("part_2", [P, 512])
        o_T = [part_sb, part_2]
        gated = sb("gated", [P, 2, HPG, HD])
        two_i = sb("two_i", [P, HD])
        k_new = sb("k_new", [P, 2, NS])
        bias_c = sb("bias_c", [P, PAST])
        bias_n = sb("bias_n", [P, 2, NS])
        bias_b = sb("bias_b", [P, 16])
        qbd = sb("qbd", [P, NSEQ, KVH, HPG, NNEW])
        stT = sb("stT", [P, KC, NS])
        lam = sb("lam", [P, 6, KC])
        pt_tab = sb("pt_tab", [1, NSEQ * 2])
        pt_tab = pt_tab[:, :].bitcast(mybir.dt.int32)

        rel_dram = nc.dram_tensor("rel_rows_dram", (HEADS, P * (REL + 1)), F32, kind="Internal").ap()

        def rel_skewed(first_head, heads, shifts, at, n):
            dims = [[P * (REL + 1), heads], [REL, shifts], [1, n]]
            return bass.AP(rel_dram.tensor, first_head * P * (REL + 1) + at, dims)

        x1_dram = nc.dram_tensor("x1_dram", (TOK, D), F32, kind="Internal").ap()

        zeroed = sem("zeroed")
        first_in = sem("first_in")
        consts_in = sem("consts_in")
        diag_in = sem("diag_in")
        x_in = [sem(f"x_in{j}") for j in range(3)]
        kvg_in = sem("kvg_in")
        wv_in = sem("wv_in")
        fmw_in = [sem(f"fmw_in{j}") for j in range(2)]
        h_hi = sem("h_hi")
        h_lo = sem("h_lo")
        wf_hi = sem("wf_hi")
        wf_lo = sem("wf_lo")
        prep_pe = sem("prep_pe")
        prep_dve = sem("prep_dve")
        rel_out = sem("rel_out")
        squared = sem("squared")
        scaled = sem("scaled")
        normed = sem("normed")
        x_turned = sem("x_turned")
        hT_ready = sem("hT_ready")
        kvA_done = sem("kvA_done")
        v_done = sem("v_done")
        kvA_out = sem("kvA_out")
        v_out = sem("v_out")
        kvB_out = sem("kvB_out")
        k_turned = sem("k_turned")
        kT_ready = sem("kT_ready")
        rows_out = [sem(f"rows_out{j}") for j in range(2)]
        ln_stats = sem("ln_stats")
        ln_scaled = sem("ln_scaled")
        ln_mid = sem("ln_mid")
        vn_ready = sem("vn_ready")
        vn_out = sem("vn_out")
        fm_done = sem("fm_done")
        fm_act = sem("fm_act")
        fm_dve = sem("fm_dve")
        cmp_rep = sem("cmp_rep")
        cmp_pe = sem("cmp_pe")
        cmp_ready = sem("cmp_ready")
        mix_done = sem("mix_done")
        mix_used = sem("mix_used")
        gates_ready = sem("gates_ready")
        bias_in = [sem("bias_in0"), sem("bias_in1")]
        split_hi = sem("split_hi")
        k_hi_own = sem("k_hi_own")
        k_hi_other = sem("k_hi_other")
        split_lo = sem("split_lo")
        q_hi = sem("q_hi")
        q_lo = sem("q_lo")
        p_hi = sem("p_hi")
        bias_s_in = sem("bias_s_in")
        scores_done = sem("scores_done")
        logits_ready = sem("logits_ready")
        probs_ready = sem("probs_ready")
        turned = sem("turned")
        bank_empty = sem("bank_empty")
        values_done = sem("values_done")
        o_copied = sem("o_copied")
        acc_ready = sem("acc_ready")
        samp_in = [sem("samp_in0"), sem("samp_in1")]
        samp_pe = [sem("samp_pe0"), sem("samp_pe1")]
        samp_q = sem("samp_q")
        samp_dve = [sem("samp_dve0"), sem("samp_dve1")]
        samp_act = [sem("samp_act0"), sem("samp_act1")]
        outa_in = sem("outa_in")
        xa_in = [sem(f"xa_in{j}") for j in range(3)]
        ya_hi = sem("ya_hi")
        ya_lo = sem("ya_lo")
        woa_hi = sem("woa_hi")
        woa_lo = sem("woa_lo")
        outa_done = sem("outa_done")
        x1_ready = sem("x1_ready")
        h1_ready = sem("h1_ready")
        h1_turned = sem("h1_turned")
        h1T_ready = sem("h1T_ready")
        x1_sent = [sem(f"x1_sent{j}") for j in range(3)]
        x1_in = [sem(f"x1_in{j}") for j in range(3)]
        h1_hi = sem("h1_hi")
        h1_lo = sem("h1_lo")
        wc_hi = sem("wc_hi")
        wc_lo = sem("wc_lo")
        igx_ready = sem("igx_ready")
        wc_in = [sem(f"wc_in{j}") for j in range(2)]
        wg_in = sem("wg_in")
        fin_in = sem("fin_in")
        aS_zero = sem("aS_zero")
        lam_exp = sem("lam_exp")
        lam_ready = sem("lam_ready")
        pc_done = sem("pc_done")
        pc_act = sem("pc_act")
        conv_ready = sem("conv_ready")
        ta_ready = sem("ta_ready")
        m_ready = sem("m_ready")
        sq_ready = sem("sq_ready")
        h_ready = sem("h_ready")
        y_ready = sem("y_ready")
        outc_in = sem("outc_in")
        yc_hi = sem("yc_hi")
        yc_lo = sem("yc_lo")
        woc_hi = sem("woc_hi")
        woc_lo = sem("woc_lo")
        outc_done = sem("outc_done")
        o_ready = sem("o_ready")
        y_row_ready = sem("y_row_ready")
        y_out = [sem(f"y_out{j}") for j in range(2)]
        small_ready = sem("small_ready")
        small_pe = sem("small_pe")
        small_rows = sem("small_rows")
        small_sent = sem("small_sent")
        dve_chain = sem("dve_chain")
        pool_chain = sem("pool_chain")
        act_chain = sem("act_chain")

        units = attention_units()
        steps = attention_steps()
        bank_use = bank_uses(steps)

        turn_order = [x for x in steps if x[0] == "turn"]
        nth_turn = {x[1]: f for f, x in enumerate(turn_order)}

        def spread(ap, n, axis=2):
            x = ap.unsqueeze(axis)
            shape = list(x.shape)
            shape[axis] = n
            return x.to_broadcast(shape)

        fm_count = []
        counts = {"act": 0, "dve": 0}
        for _, _, who in FM_A:
            counts[who] += 1
            fm_count.append(counts[who])

        def fm_loads(n):
            return sum(2 if FM_A[m][0] == "q" else 1 for m in range(n % 2, n, 2))

        def fm_wait(eng, n):
            eng.wait_ge(fm_act if FM_A[n][2] == "act" else fm_dve, fm_count[n])

        order_c = []
        for c in range(KC + 1):
            if c < KC:
                order_c.append(("x", c))
            else:
                order_c.append(("z", 0))
            if c >= 1:
                order_c += [("r", c - 1), ("i", c - 1)]
        order_c += [("z", c) for c in range(1, KC)]
        order_c_at = {x: n for n, x in enumerate(order_c)}

        def pc_of(n):
            if n == KC:
                return order_c_at[("z", 0)] + 1
            return order_c_at[("x", n) if n < KC else ("z", n - KC)] + 1

        def sent_rows(i):
            return sum(2 if j >= (SEQ - WIN) // P else 1 for j in range(i % 2, i, 2))

        SAMP_DVE = ["keys0", "keys1", "means", "cmp", "logits", "probT", "res", "out"]
        SAMP_PE = ["keys0", "keys1", "cmp", "scores", "turned", "values", "out"]

        SAMP_ORDER = [(x - 3 * f, f) for x in range(len(SAMP_PE) + 3) for f in (1, 0) if 0 <= x - 3 * f < len(SAMP_PE)]

        def samp_at(step):
            return SAMP_DVE.index(step) + 1

        def samp_pe_at(step):
            return SAMP_PE.index(step) + 1

        block = ctx.enter_context(nc.Block())
        w_in_k = ins["w_in_a"][0].rearrange("(k p) n -> p k n", p=P)
        w_inc_k = ins["w_in_c"][0].rearrange("(k p) n -> p k n", p=P)
        hot_h = [(tril, "c_tril"), (far, "c_far"), (avg, "c_avg"), (rowok, "c_rowok"),
                 (headrow, "c_headrow"), (hsel, "c_hsel"), (two_i, "c_two_i"), (tsel, "c_tsel"), (tril_s, "c_tril_s")]
        const_loads = [(t[:, :], ins[n]) for t, n in hot_h]
        const_loads += [(hot[0:BUCKETS + 1, :], ins["c_hot"])]
        first_loads = [(ident[:, :], ins["c_ident"])]
        first_loads += [(vec_in[VEC[n]:VEC[n] + 8, :], ins[n][0].rearrange("(k p) -> k p", p=P))
                        for n in ("norm_a", "norm_c", "conv_b", "b_rg_a", "b_rg_x", "lru_lambda")]
        first_loads += [(vec_in[16:48, :], ins["conv_w"][0].rearrange("t (k p) -> (t k) p", p=P))]
        const_loads += [(wsp_in, ins["w_spatial"][0].rearrange("g i j -> i g j"))]
        const_loads += [(state_in[0:24, :], ins["state_lru_conv"][0].rearrange("s k c -> (s k) c")),
                        (state_in[24:32, :], ins["state_lru_h"][0])]
        const_loads += [(pe_in[0:BLK, kind, g * HD:(g + 1) * HD], ins["pe_cmp"][0, kind])
                        for kind in range(2) for g in range(2)]
        const_loads += [(b_sp[:, :, :], ins["b_spatial"][0].partition_broadcast(P)),
                        (ln_g, ins["gmlp_ln_g"][0].partition_broadcast(P)),
                        (ln_b, ins["gmlp_ln_b"][0].partition_broadcast(P)),
                        (b_gate[:, :], ins["b_gate_a"][0].partition_broadcast(P)),
                        (pt_tab, ins["page_table"].rearrange("s j -> (s j)").rearrange("(a n) -> a n", a=1)),
                        (rel_in[0:BUCKETS, :], ins["rel_bias"])]
        NCONST = 16 * len(const_loads)
        NFIRST = 16 * len(first_loads)

        @block.sync
        def _(sp):
            def load_x(i):
                if i >= 3:
                    sp.wait_ge(x_turned, i - 2)
                src = ins["x_prompt"][0, tok(i), :] if i < PT else ins["x_sample"].rearrange("s t d -> (s t) d")
                sp.dma_start(x_row[i % 3][0:rows(i), :], src).then_inc(x_in[i % 3], 16)

            load_x(0)
            with nc.allow_non_contiguous_dma("small vectors"):
                for dst, src in first_loads[0::2]:
                    sp.dma_start(dst, src).then_inc(first_in, 16)
            load_x(1)
            for k in range(0, KC, 4):
                sp.dma_start(w_kvg[:, k:k + 4, :], w_in_k[:, k:k + 4, KV0:KV0 + KVG]).then_inc(kvg_in, 16)
            load_x(2)
            for k in range(0, KC, 4):
                sp.dma_start(w_v[:, k:k + 4, :], w_in_k[:, k:k + 4, V0:V0 + 512]).then_inc(wv_in, 16)

            def load_fm(n):
                kind, j, _ = FM_A[n]
                if n == 0:
                    sp.wait_ge(x_turned, TILES)
                if n >= 2:
                    sp.wait_ge(wf_lo, n - 1)
                dst, s = w_fm[n % 2], fmw_in[n % 2]
                if kind == "q":
                    for g in range(2):
                        c0 = Q0 + (g * HPG + j) * HD
                        sp.dma_start(dst[:, :, g * HD:(g + 1) * HD], w_in_k[:, :, c0:c0 + HD]).then_inc(s, 16)
                else:
                    c0 = {"z": Z0, "zg": ZG0, "u": U0}[kind] + j * P
                    sp.dma_start(dst, w_in_k[:, :, c0:c0 + P]).then_inc(s, 16)

            for i in range(3, TILES):
                load_x(i)
            for n in range(len(FM_A)):
                load_fm(n)
            sp.wait_ge(rel_out, 16 * HEADS)
            sp.wait_ge(fm_done, len(FM_A))
            for half in range(2):
                c0 = SEQ // 2 * (1 - half)
                for h in range(HEADS):
                    sp.dma_start(bias[:, h, c0:c0 + SEQ // 2], rel_skewed(h, 1, P, P - 1 + c0, SEQ // 2)
                                 ).then_inc(bias_in[half], 16)

            def load_outa():
                sp.wait_ge(logits_ready, len(units))
                for k in range(0, KC, 4):
                    sp.dma_start(w_outa[:, k:k + 4, :],
                                 ins["w_out_a"][0].rearrange("(k p) n -> p k n", p=P)[:, k:k + 4, :]
                                 ).then_inc(outa_in, 16)

            for f in range(2):
                if f == 0:
                    sp.wait_ge(mix_used, TILES)
                    sp.wait_ge(vn_out, 16)
                    sp.wait_ge(rows_out[0], 16 * 8)
                    sp.wait_ge(rows_out[1], 16 * 6)
                    sp.wait_ge(consts_in, NCONST)
                    sp.wait_ge(scores_done, len(units))
                else:
                    sp.wait_ge(bank_empty, len(bank_use))
                for j in range(2 * HALF):
                    at = f * 2 * HALF + j
                    page = sp.value_load(pt_tab[0:1, at:at + 1], min_val=0,
                                         max_val=ins["cache_nsa"].shape[1] - 1)
                    sp.dma_start(pages_of[f][:, j, :],
                                 ins["cache_nsa"][0, bass.ds(page, 1), :, :, :, :].rearrange(
                                     "a t k g d -> (a t) (k g d)")).then_inc(samp_in[f], 16)
                for s in range(HALF):
                    sp.dma_start(wins_of[f][:, 2 * s:2 * s + 2, :],
                                 ins["cache_win"][0, f * HALF + s].rearrange(
                                     "(j t) k g d -> t j (k g d)", t=P)).then_inc(samp_in[f], 16)

            load_outa()

            def spill(i):
                sp.wait_ge(x1_ready, i + 1)
                sp.dma_start(x1_dram[tok(i), :], x1[i % 3][0:rows(i), :]).then_inc(x1_sent[i % 3], 16)

            def load_x1(i):
                src = ins["x_prompt"][0, tok(i), :] if i < PT else ins["x_sample"].rearrange("s t d -> (s t) d")
                sp.dma_start(x1[i % 3][0:rows(i), :], src).then_inc(xa_in[i % 3], 16)

            for f in range(2):
                sp.wait_ge(samp_pe[f], samp_pe_at("values"))
            for i in range(3):
                load_x1(i)
            for i in range(TILES - 3):
                spill(i)
                sp.wait_ge(x1_sent[i % 3], 16 * (i // 3 + 1))
                sp.wait_ge(h1_ready, i + 1)
                load_x1(i + 3)

            def load_wc(n):
                if n >= 2:
                    sp.wait_ge(wc_lo, n - 1)
                if n == 1:
                    sp.wait_ge(outa_done, TILES)
                sp.dma_start(w_c[n % 2], w_inc_k[:, :, n * P:(n + 1) * P]).then_inc(wc_in[n % 2], 16)

            load_wc(0)
            spill(TILES - 3)
            spill(TILES - 2)
            sp.dma_start(fin_g[:, :], ins["final_norm"].partition_broadcast(P)).then_inc(fin_in, 16)
            load_wc(1)
            sp.wait_ge(h1_turned, TILES)
            for m, name in enumerate(("w_rg_a", "w_rg_x")):
                sp.dma_start(w_rg[:, m], ins[name][0].rearrange("c i j -> i c j")).then_inc(wg_in, 16)
            spill(TILES - 1)
            for n in range(2, 2 * KC):
                load_wc(n)
                if n == KC + 3:
                    sp.wait_ge(small_ready, 1)
                    for k in range(0, KC, 4):
                        sp.dma_start(w_outc[:, k:k + 4, :],
                                     ins["w_out_c"][0].rearrange("(k p) n -> p k n", p=P)[:, k:k + 4, :]
                                     ).then_inc(outc_in, 16)

            def reload_x1(i):
                if i >= 3:
                    sp.wait_ge(y_row_ready, i - 2)
                sp.wait_ge(x1_sent[i % 3], 16 * (i // 3 + 1))
                sp.dma_start(x1_again[i % 3][0:rows(i), :], x1_dram[tok(i), :]).then_inc(x1_in[i % 3], 16)

            sp.wait_ge(pc_done, len(order_c))
            for i in range(3):
                reload_x1(i)

            sp.wait_ge(small_rows, 1)
            so = small_tm
            sp.dma_start(outs["lru_h_sample"][0], so[0:8, :]).then_inc(small_sent, 16)
            sp.dma_start(outs["lru_conv_sample"][0].rearrange("s k c -> (s k) c"), so[8:32, :]
                         ).then_inc(small_sent, 16)
            sp.dma_start(outs["lru_h_prompt"][0], so[32:33, :]).then_inc(small_sent, 16)
            sp.dma_start(outs["lru_conv_prompt"][0, 0], so[33:36, :]).then_inc(small_sent, 16)
            for i in range(TILES):
                sp.wait_ge(y_row_ready, i + 1)
                dst = outs["y_prompt"][0, tok(i), :] if i < PT else outs["y_sample"].rearrange("s t d -> (s t) d")
                sp.dma_start(dst, y_row[i % 2][0:rows(i), :]).then_inc(y_out[i % 2], 16)
                if i + 3 < TILES:
                    reload_x1(i + 3)
            sp.wait_ge(small_sent, 64)
            sp.wait_ge(y_out[0], 16 * 5)
            sp.wait_ge(y_out[1], 16 * 4)

        @block.gpsimd
        def _(pool):
            pool.memset(rel_in[:, :], BIG).then_inc(zeroed, 1)
            pool.memset(wc_k[:, :], 0.0).then_inc(zeroed, 1)
            pool.memset(wc_v[:, :], 0.0).then_inc(zeroed, 1)
            pool.memset(wspT_s[:, :, :], 0.0).then_inc(zeroed, 1)
            pool.memset(half_neg[:, :], -0.5).then_inc(zeroed, 1)
            pool.memset(lc[:, :, :], 0.0).then_inc(zeroed, 1)
            pool.memset(kc_bd[:, :, :], 0.0).then_inc(zeroed, 1)
            pool.memset(qbd[:, :, :, :, :], 0.0).then_inc(zeroed, 1)
            pool.memset(bias_n[:, :, :], BIG).then_inc(zeroed, 1)
            pool.memset(bias_b[:, :], BIG).then_inc(zeroed, 1)

            rms_chain = [0]

            def rms(norm, i, want):
                r = rows(i)
                pool.wait_ge(squared, want)
                pool.tensor_scalar(ms[0:r, norm, i:i + 1], ss[0:r, norm, i:i + 1], 1.0 / D, EPS,
                                   ALU.mult, ALU.add).then_inc(pool_chain, 1)
                rms_chain[0] += 1
                pool.wait_ge(pool_chain, rms_chain[0])
                pool.tensor_tensor(rstd[0:r, norm, i:i + 1], ms[0:r, norm, i:i + 1], half_neg[0:r, :],
                                   ALU.pow).then_inc(scaled, 1)

            def ln(i):
                r = rows(i)
                pool.wait_ge(ln_stats, i + 1)
                pool.tensor_scalar(mv_e[0:r, i:i + 1], mv[0:r, i, 1:2], EPS, None, ALU.add
                                   ).then_inc(pool_chain, 1)
                rms_chain[0] += 1
                pool.wait_ge(pool_chain, rms_chain[0])
                pool.tensor_tensor(rstd_v[0:r, i:i + 1], mv_e[0:r, i:i + 1], half_neg[0:r, :],
                                   ALU.pow).then_inc(ln_scaled, 1)

            def ln_affine(i):
                r = rows(i)
                pool.wait_ge(ln_mid, i + 1)
                pool.wait_ge(consts_in, NCONST)
                pool.tensor_tensor(vn[0:r, i, :], vn[0:r, i, :], ln_g[0:r, :], ALU.mult).then_inc(pool_chain, 1)
                rms_chain[0] += 1
                pool.wait_ge(pool_chain, rms_chain[0])
                pool.tensor_tensor(vn[0:r, i, :], vn[0:r, i, :], ln_b[0:r, :], ALU.add).then_inc(vn_ready, 1)

            def send_rows(i):
                pool.wait_ge(kvA_out, i + 1)
                pool.wait_ge(kvB_out, i + 1)
                src = kv_row[i % 2]
                if i < PT:
                    pool.dma_start(outs["nsa_rows_prompt"][0, 0, tok(i)].rearrange("t k g d -> t (k g d)"),
                                   src[:, 0:512]).then_inc(rows_out[i % 2], 16)
                    if i >= (SEQ - WIN) // P:
                        at = i * P - (SEQ - WIN)
                        pool.dma_start(outs["win_rows_prompt"][0, 0, at:at + P].rearrange("t k g d -> t (k g d)"),
                                       src[:, 512:768]).then_inc(rows_out[i % 2], 16)
                else:
                    pool.dma_start(outs["nsa_rows_sample"][0].rearrange("s t k g d -> (s t) (k g d)"),
                                   src[0:NS, 0:512]).then_inc(rows_out[i % 2], 16)
                    pool.dma_start(outs["win_rows_sample"][0].rearrange("s t k g d -> (s t) (k g d)"),
                                   src[0:NS, 512:768]).then_inc(rows_out[i % 2], 16)

            rms(0, 0, 1)
            rms(0, 1, 2)
            for i in range(TILES):
                if i + 2 < TILES:
                    rms(0, i + 2, i + 3)
                if i >= 1:
                    ln(i - 1)
                    ln_affine(i - 1)
                send_rows(i)
                if i == 0:
                    pool.wait_ge(prep_dve, 2)
                    for h in range(HEADS):
                        pool.dma_start(bass.AP(rel_dram.tensor, h * P * (REL + 1), [[REL, 1], [REL + 1, P], [1, REL]]),
                                       spread(rel_rows[h:h + 1, :], P, 1)).then_inc(rel_out, 16)
            ln(TILES - 1)
            ln_affine(TILES - 1)
            pool.wait_ge(vn_ready, TILES)
            pool.dma_start(outs["gmlp_v_sample"][0].rearrange("s t c -> (s t) c"), vn[0:NS, PT, :]
                           ).then_inc(vn_out, 16)
            pool.wait_ge(zeroed, 10)
            for kind, t in ((0, wc_k), (1, wc_v)):
                for g in range(2):
                    pool.dma_start(t[g * HD:(g + 1) * HD, g * HD:(g + 1) * HD], ins["w_cmp"][0, kind]
                                   ).then_inc(diag_in, 16)
            corner = ins["w_spatial"][0, :, 0:NNEW, 0:NNEW]
            with nc.allow_non_contiguous_dma("4 x 4 corners of the spatial weights"):
                for g in range(4):
                    for s in range(NSEQ):
                        pool.dma_start(wspT_s[s * NNEW:(s + 1) * NNEW, g, s * NNEW:(s + 1) * NNEW],
                                       corner[g].rearrange("i j -> j i")).then_inc(diag_in, 16)
            pool.wait_ge(rel_out, 16 * HEADS)
            for s in range(HALF):
                o = 32 * s
                pool.dma_start(bias_c[o:o + 32, :],
                               rel_skewed(0, HEADS, NNEW, REL_TOP - PAST, PAST)
                               ).then_inc(bias_s_in, 16)
                for f in range(2):
                    c0 = (f * HALF + s) * NNEW
                    pool.dma_start(bias_n[o:o + 32, f, c0:c0 + NNEW],
                                   rel_skewed(0, HEADS, NNEW, REL_TOP, NNEW)
                                   ).then_inc(bias_s_in, 16)
            for g in range(KVH):
                pool.wait_ge(k_hi_own, g + 1)
                if g:
                    pool.wait_ge(k_hi_other, g)
                other = slice((1 - g) * HD, (2 - g) * HD)
                pool.tensor_copy(k_hi[other, 1, g, :], k_hi[g * HD:(g + 1) * HD, 1, g, :].bitcast(F32)
                                 ).then_inc(k_hi_other, 1)
            pool.wait_ge(k_hi_other, 2)
            pool.wait_ge(mix_used, TILES)
            pool.memset(aS, 0.0).then_inc(aS_zero, 1)
            for i in range(TILES):
                rms(1, i, TILES + i + 1)
            for c in range(KC):
                pool.wait_ge(pc_act, order_c_at[("i", c)] + 1)
                pool.wait_ge(conv_ready, c + 1)
                if c:
                    pool.wait_ge(igx_ready, c)
                pool.tensor_tensor(ig_buf, ig_buf, xc[c % 2], ALU.mult).then_inc(igx_ready, 1)
            for i in range(TILES):
                rms(2, i, 2 * TILES + i + 1)
            pool.wait_ge(vn_out, 16)
            pool.wait_ge(rows_out[0], 16 * 8)
            pool.wait_ge(rows_out[1], 16 * 6)

        @block.scalar
        def _(act):
            with nc.allow_non_contiguous_dma("small vectors"):
                for dst, src in first_loads[1::2]:
                    act.dma_start(dst, src).then_inc(first_in, 16)

            def square(i):
                act.wait_ge(x_in[i % 3], 16 * (i // 3 + 1))
                if i >= 1:
                    act.wait_ge(squared, i)
                r = rows(i)
                nc.scalar.activation(junk[0:r, :], x_row[i % 3][0:r, :], ACT.Square,
                                     accum_out=ss[0:r, 0, i:i + 1]).then_inc(squared, 1)

            square(0)
            square(1)
            with nc.allow_non_contiguous_dma("small vectors"):
                for n, (dst, src) in enumerate(const_loads):
                    if n == len(const_loads) - 1:
                        act.wait_ge(zeroed, 1)
                    act.dma_start(dst, src).then_inc(consts_in, 16)
            for i in range(TILES):
                r = rows(i)
                if i + 2 < TILES:
                    square(i + 2)
                act.wait_ge(kvA_done, i + 1)
                if i >= 2:
                    n = i % 2
                    act.wait_ge(rows_out[n], 16 * sent_rows(i))
                    act.wait_ge(k_turned, i - 1)
                nc.scalar.copy(kv_row[i % 2][0:r, 0:512], ps[0:r, 0, :])
                nc.scalar.copy(v_s[0:r, i, :], ps[0:r, 0, 384:512]).then_inc(kvA_out, 1)
                act.wait_ge(v_done, i + 1)
                nc.scalar.copy(vn[0:r, i, :], ps[0:r, 2, :]).then_inc(v_out, 1)
                nc.scalar.copy(hT_hi[:, 4:KC, tok(i)], hT[:, 4:KC, tok(i)]).then_inc(h_hi, 1)
            def split_w(n):
                kind = FM_A[n][0]
                act.wait_ge(fmw_in[n % 2], 16 * (fm_loads(n) + (2 if kind == "q" else 1)))
                if n == 0:
                    act.wait_ge(squared, TILES)
                if n == 1:
                    act.wait_ge(rows_out[0], 16 * 8)
                    act.wait_ge(rows_out[1], 16 * 6)
                    act.wait_ge(k_turned, TILES)
                if n >= 2:
                    act.wait_ge(fm_done, n - 1)
                nc.scalar.copy(w_fm_hl[n % 2][:, 0], w_fm[n % 2]).then_inc(wf_hi, 1)

            split_w(0)
            for k in range(4):
                nc.scalar.copy(hT_hi[:, k, :], hT[:, k, :]).then_inc(h_hi, 1)
            split_w(1)
            act.wait_ge(kvB_out, TILES)
            nc.scalar.activation(gates[:, 0:PT, :], gates[:, 0:PT, :], ACT.Sigmoid)
            nc.scalar.activation(gates[0:NS, PT, :], gates[0:NS, PT, :], ACT.Sigmoid).then_inc(gates_ready, 1)
            for n, (kind, j, who) in enumerate(FM_A):
                if who == "act":
                    act.wait_ge(fm_done, n + 1)
                    dst = yT[:, j if kind == "z" else 4 + j, :].rearrange("p (a b) -> p a b", a=3)
                    nc.scalar.activation(dst, ps[:, 3 * (n % 2):3 * (n % 2) + 3, 0:THIRD], ACT.Silu
                                         ).then_inc(fm_act, 1)
                if n + 2 < len(FM_A):
                    split_w(n + 2)

            act.wait_ge(fm_done, len(FM_A))
            act.wait_ge(k_turned, TILES)
            for b, kT in ((1, kT_w), (0, kT_s)):
                for g in range(KVH):
                    gp = slice(g * HD, (g + 1) * HD)
                    nc.scalar.copy(k_hi[gp, b, g, :], kT[gp, 0:SEQ]).then_inc(k_hi_own, 1)
            for b, vv in ((1, v_w), (0, v_s)):
                for g in range(KVH):
                    gp = slice(g * HD, (g + 1) * HD)
                    nc.scalar.copy(v_hl[:, b, g, :, 0:HD], vv[:, 0:PT, gp]).then_inc(split_hi, 1)
            for g in range(KVH):
                other = slice((1 - g) * HD, (2 - g) * HD)
                nc.scalar.copy(k_hi[other, 0, g, :], kT_s[g * HD:(g + 1) * HD, 0:SEQ]).then_inc(split_hi, 1)


            for what, n in act_order(steps):
                if what == "split_q":
                    if n >= 2:
                        act.wait_ge(scores_done, 17 * (n - 1))
                    if n == 0:
                        act.wait_ge(fm_dve, counts["dve"])
                        act.wait_ge(split_hi, 6)
                        act.wait_ge(split_lo, 4)
                        act.wait_ge(vn_out, 16)
                    for g in range(KVH):
                        gp = slice(g * HD, (g + 1) * HD)
                        e = nc.scalar.copy(q_hl[gp, n % 2, g * HPG:(g + 1) * HPG, :], qT[gp, :, tok(n)])
                    e.then_inc(q_hi, 1)
                elif what == "scores":
                    kind, i, h = units[n]
                    cols, _ = key_cols(kind, i)
                    act.wait_ge(logits_ready, n + 1)
                    if kind == "c":
                        nc.scalar.activation(lc[:, :, 0:cols], lc[:, :, 0:cols], ACT.Exp, scale=-1.0
                                             ).then_inc(probs_ready, 1)
                    else:
                        buf = probs[kind][:, h % HPG, 0:cols]
                        b = 1 if kind == "s" else 2
                        nc.scalar.activation(buf, buf, ACT.Exp, bias=negm[:, n % 16:n % 16 + 1], scale=-1.0,
                                             accum_out=sums[:, i % 2, b, h:h + 1]).then_inc(probs_ready, 1)
                elif what == "turn":
                    f = nth_turn[n]
                    k = bank_use[what, n]
                    act.wait_ge(turned, k + 1)
                    if f >= 2:
                        act.wait_ge(values_done, f - 1)
                    nc.scalar.copy(p_hl[:, f % 2, 0, :], ps[:, 4 + k % 3, :]).then_inc(p_hi, 1)
                elif what == "copy_o":
                    kind, i, g = GROUPS[n]
                    last = (n, key_cols(kind, i)[0] // P - 1)
                    act.wait_ge(values_done, nth_turn[last] + 1)
                    if n >= 2:
                        pi, pg = GROUPS[n - 2][1:]
                        act.wait_ge(turned, bank_use["back", (pi, pg)] + 1)
                    nc.scalar.copy(o_T[n % 2][:, :], ps[:, 7, :]).then_inc(o_copied, 1)

            for f in range(2):
                act.wait_ge(samp_dve[f], samp_at("logits"))
                h = halves[f]
                for b, (buf, w) in enumerate(((h.logits_c, 16), (h.logits[0], PAST + NS), (h.logits[1], PAST + NS))):
                    e = nc.scalar.activation(buf[:, 0:w], buf[:, 0:w], ACT.Exp, bias=h.neg[:, b:b + 1],
                                             scale=-1.0, accum_out=h.sums[:, b:b + 1])
                e.then_inc(samp_act[f], 1)

            def h1_high(i):
                act.wait_ge(h1T_ready, i + 1)
                nc.scalar.copy(h1T_hi[:, :, tok(i)], h1T[:, :, tok(i)]).then_inc(h1_hi, 1)

            def split_wc(n):
                act.wait_ge(wc_in[n % 2], 16 * (n // 2 + 1))
                if n >= 2:
                    act.wait_ge(pc_done, pc_of(n - 2))
                nc.scalar.copy(w_c_hl[n % 2][:, 0], w_c[n % 2]).then_inc(wc_hi, 1)

            def ya_high(i):
                for f in range(2):
                    act.wait_ge(samp_dve[f], samp_at("out"))
                nc.scalar.copy(ya_hl[i % 2][:, 0, :, 0:rows(i)], yT[:, :, tok(i)]).then_inc(ya_hi, 1)

            ya_high(0)
            act.wait_ge(outa_in, 32)
            for k in range(KC):
                nc.scalar.copy(w_outa_hi[:, k, :], w_outa[:, k, :]).then_inc(woa_hi, 1)
            ya_high(1)

            for i in range(TILES):
                r = rows(i)
                if i == TILES - 1:
                    act.wait_ge(outa_done, TILES)
                    split_wc(0)
                act.wait_ge(x1_ready, i + 1)
                if i + 2 < TILES:
                    ya_high(i + 2)
                if i >= 2:
                    act.wait_ge(h1_turned, i - 1)
                nc.scalar.activation(h1[i % 2][0:r, :], x1[i % 3][0:r, :], ACT.Square,
                                     accum_out=ss[0:r, 1, i:i + 1]).then_inc(squared, 1)
                if i >= 1:
                    h1_high(i - 1)
            h1_high(TILES - 1)
            split_wc(1)

            act.wait_ge(lam_ready, 1)
            nc.scalar.activation(lam[:, 1, :], lam[:, 0, :], ACT.Exp, scale=-1.0).then_inc(lam_exp, 1)

            def bank3(n):
                return ps[:, 3 * (n % 2):3 * (n % 2) + 3, 0:THIRD]

            for n, (kind, c) in enumerate(order_c):
                act.wait_ge(pc_done, n + 1)
                if kind == "x":
                    if c >= 1:
                        act.wait_ge(conv_ready, c)
                    b0 = 3 * (n % 2)
                    nc.scalar.copy(xin[:, 3:3 + 2 * THIRD].rearrange("p (a b) -> p a b", a=2),
                                   ps[:, b0:b0 + 2, 0:THIRD])
                    nc.scalar.copy(xin[:, 3 + 2 * THIRD:3 + SEQ], ps[:, b0 + 2, 0:SEQ - 2 * THIRD])
                    nc.scalar.copy(xin_s[:, :, 3:7],
                                   ps[:, b0 + 2, SEQ - 2 * THIRD:THIRD].rearrange("p (s t) -> p s t", t=NNEW)
                                   ).then_inc(pc_act, 1)
                    split_wc(c + 2)
                elif kind == "r":
                    if c >= 1:
                        act.wait_ge(h_ready, c)
                    if c == 0:
                        act.wait_ge(lam_ready, 2)
                    nc.scalar.activation(r_buf.rearrange("p (a b) -> p a b", a=3), bank3(n), ACT.Sigmoid,
                                         bias=vecT[:, VEC["b_rg_a"] + c:VEC["b_rg_a"] + c + 1]
                                         ).then_inc(pc_act, 1)
                    r_at = n
                elif kind == "i":
                    nc.scalar.activation(ig_buf.rearrange("p (a b) -> p a b", a=3), bank3(n), ACT.Sigmoid,
                                         bias=vecT[:, VEC["b_rg_x"] + c:VEC["b_rg_x"] + c + 1]
                                         ).then_inc(pc_act, 1)
                    act.wait_ge(pc_act, n + 1)
                    if c == 0:
                        act.wait_ge(aS_zero, 1)
                    nc.scalar.activation(t_buf, r_buf, ACT.Tanh, scale=lam[:, 4, c:c + 1])
                    nc.scalar.activation(aS[:, c, :, 1:NNEW + 1],
                                         r_buf[:, SEQ:TOK].rearrange("p (s t) -> p s t", t=NNEW),
                                         ACT.Exp, scale=lam[:, 5, c:c + 1]).then_inc(act_chain, 1)
                    act.wait_ge(act_chain, c + 1)
                    nc.scalar.activation(r_buf, r_buf, ACT.Exp, scale=lam[:, 5, c:c + 1]
                                         ).then_inc(ta_ready, 1)
                    act.wait_ge(m_ready, c + 1)
                    nc.scalar.activation(t_buf, t_buf, ACT.Sqrt).then_inc(sq_ready, 1)
                else:
                    if c >= 2:
                        act.wait_ge(y_ready, c - 1)
                    nc.scalar.activation(sz_buf[c % 2].rearrange("p (a b) -> p a b", a=3), bank3(n), ACT.Silu
                                         ).then_inc(pc_act, 1)
                    if c + 2 < KC:
                        split_wc(KC + c + 2)

            def y_high(i):
                nc.scalar.copy(y_hi[:, :, tok(i)], states[:, :, tok(i)]).then_inc(yc_hi, 1)

            act.wait_ge(pc_done, len(order_c))
            act.wait_ge(y_ready, KC)
            y_high(0)
            act.wait_ge(outc_in, 32)
            for k in range(KC):
                nc.scalar.copy(w_outc_hi[:, k, :], w_outc[:, k, :]).then_inc(woc_hi, 1)
            y_high(1)

            for i in range(TILES):
                r = rows(i)
                if i + 2 < TILES:
                    y_high(i + 2)
                act.wait_ge(o_ready, i + 1)
                if i >= 2:
                    act.wait_ge(y_out[i % 2], 16 * (i // 2))
                if i == 0:
                    act.wait_ge(y_ready, KC)
                nc.scalar.activation(y_row[i % 2][0:r, :], x1_again[i % 3][0:r, :], ACT.Square,
                                     accum_out=ss[0:r, 2, i:i + 1]).then_inc(squared, 1)

        @block.tensor
        def _(pe):
            def mm(out, l, r, start, stop):
                return nc.tensor.matmul(out, l, r, start=start, stop=stop, skip_group_check=True)

            def flip(out, x):
                k = x.shape[0]
                return nc.tensor.transpose(out, x, ident[0:k, 0:k])

            pe.wait_ge(first_in, NFIRST)
            flip(ps[:, 3, 0:NVEC], vec_in[0:NVEC, :]).then_inc(prep_pe, 1)

            def prepare():
                pe.wait_ge(consts_in, NCONST)
                pe.wait_ge(zeroed, 10)
                pe.wait_ge(kvA_out, 1)
                pe.wait_ge(kvB_out, 1)
                pe.wait_ge(v_out, 1)
                for j in range(3):
                    m = mm(ps[0:HEADS, j, 0:REL // 3], rel_in[:, :], hot[0:BUCKETS + 1, j * 384:(j + 1) * 384],
                           True, True)
                m.then_inc(prep_pe, 1)
                for kind in range(2):
                    m = mm(ps[:, 3, 508 + kind:509 + kind], pe_in[0:BLK, kind, :], avg[0:BLK, 0:1], True, True)
                for g in range(4):
                    flip(ps[:, 4, g * P:(g + 1) * P], wsp_in[:, g, :])
                for k in range(KC):
                    m = flip(ps[:, 5, k * NS:(k + 1) * NS], state_in[0:NS, k * P:(k + 1) * P])
                m.then_inc(prep_pe, 1)

            def turn_x(i):
                pe.wait_ge(normed, i + 1)
                if i >= 1:
                    pe.wait_ge(hT_ready, i)
                r = rows(i)
                for k in range(KC):
                    m = flip(ps[:, 6 + k // 4, (k % 4) * P:(k % 4) * P + r], x_row[i % 3][0:r, k * P:(k + 1) * P])
                m.then_inc(x_turned, 1)

            turn_x(0)
            pe.wait_ge(kvg_in, 32)
            for i in range(TILES):
                r = rows(i)
                if i + 1 < TILES:
                    turn_x(i + 1)
                pe.wait_ge(hT_ready, i + 1)
                if i == 0:
                    pe.wait_ge(prep_dve, 1)
                else:
                    pe.wait_ge(kvA_out, i)
                    pe.wait_ge(kvB_out, i)
                    if i == 1:
                        pe.wait_ge(prep_dve, 5)
                for a, b, bank in ((0, 512, 0), (512, KVG, 1)):
                    for k in range(KC):
                        m = mm(ps[0:r, bank, 0:b - a], hT[:, k, tok(i)], w_kvg[:, k, a:b], k == 0, k == KC - 1)
                m.then_inc(kvA_done, 1)
                if i == 0:
                    pe.wait_ge(wv_in, 32)
                else:
                    pe.wait_ge(v_out, i)
                for k in range(KC):
                    m = mm(ps[0:r, 2, :], hT[:, k, tok(i)], w_v[:, k, :], k == 0, k == KC - 1)
                m.then_inc(v_done, 1)
                pe.wait_ge(kvA_out, i + 1)
                pe.wait_ge(kvB_out, i + 1)
                if i >= 1:
                    pe.wait_ge(kT_ready, i)
                row = kv_row[i % 2]
                flip(ps[:, 3, 0:r], row[0:r, 256:384])
                m = flip(ps[:, 3, P:P + r], row[0:r, 512:640])
                if i < PT:
                    for kind in range(2):
                        m = mm(ps[:, 3, 256 + 2 * kind:258 + 2 * kind], row[:, kind * P:(kind + 1) * P],
                               avg[:, :], True, True)
                m.then_inc(k_turned, 1)
                if i == 0:
                    prepare()

            def mix(i):
                r = rows(i)
                pe.wait_ge(vn_ready, i + 1)
                if i == 0:
                    pe.wait_ge(cmp_ready, 1)
                    pe.wait_ge(prep_dve, 6)
                if i >= 2:
                    pe.wait_ge(mix_used, i - 1)
                for g in range(4):
                    w = wspT[:, g, :] if i < PT else wspT_s[:, g, :]
                    m = mm(ps[:, 6 + i % 2, g * P:g * P + r], vn[0:r, i, g * P:(g + 1) * P], w, True, True)
                m.then_inc(mix_done, 1)

            for n, (kind, j, _) in enumerate(FM_A):
                if kind == "q":
                    for i in MIX_BEFORE[j]:
                        mix(i)
                pe.wait_ge(wf_lo, n + 1)
                if n == 0:
                    pe.wait_ge(kvB_out, TILES)
                    pe.wait_ge(v_out, TILES)
                elif n == 1:
                    pe.wait_ge(kT_ready, TILES)
                else:
                    fm_wait(pe, n - 2)
                for at, k in enumerate(list(range(4, KC)) + list(range(4))):
                    if n == 0:
                        pe.wait_ge(h_lo, TILES + (k + 1 if k < 4 else 0))
                    for wi, h in ((0, hT_hi), (0, hT_lo), (1, hT_hi)):
                        for t in range(3):
                            m = mm(ps[:, 3 * (n % 2) + t, 0:THIRD], w_fm_hl[n % 2][:, wi, k, :],
                                   h[:, k, t * THIRD:(t + 1) * THIRD], at == 0 and (wi, h) == (0, hT_hi),
                                   at == KC - 1 and wi == 1)
                m.then_inc(fm_done, 1)
                if n == 4:
                    pe.wait_ge(diag_in, 16 * 36)
                    pe.wait_ge(hT_ready, TILES)
                    pe.wait_ge(cmp_rep, 1)
                    mm(ps[:, 6, 0:NB], wc_k[:, :], mean_p[:, 0, :], True, True)
                    mm(ps[:, 6, P:2 * P], mean_rep[:, :, :].rearrange("p h n -> p (h n)"), wc_v[:, :],
                       True, True).then_inc(cmp_pe, 1)

            pe.wait_ge(split_lo, 4)
            pe.wait_ge(split_hi, 6)
            pe.wait_ge(k_hi_other, 2)
            pe.wait_ge(fm_act, counts["act"])
            pe.wait_ge(fm_dve, counts["dve"])
            pe.wait_ge(mix_used, TILES)

            for what, n in steps:
                k = bank_use.get((what, n))
                if k is not None and k >= 3:
                    pe.wait_ge(bank_empty, k - 2)
                if what == "scores":
                    kind, i, h = units[n]
                    cols, first = key_cols(kind, i)
                    slot = 2 * (n % 2)
                    if n >= 2:
                        pe.wait_ge(logits_ready, n - 1)
                    if kind == "c":
                        pe.wait_ge(q_lo, i + 1)
                        for c in range(HPG):
                            m = mm(ps[:, slot, c * 2 * NB:(c + 1) * 2 * NB], qT[:, c, tok(i)],
                                   kc_bd[:, :, :].rearrange("p g n -> p (g n)"), True, True)
                    else:
                        g, b = h // HPG, 0 if kind == "s" else 1
                        gp = slice(g * HD, (g + 1) * HD)
                        for a in range(0, cols, 512):
                            w = min(512, cols - a)
                            o = ps[:, slot + a // 512, 0:w]
                            keys = slice(first + a, first + a + w)
                            mm(o, q_hl[:, i % 2, h, :], k_hi[:, b, g, keys], True, False)
                            m = mm(o, q_hl[gp, i % 2, h, :], k_lo[gp, b, keys], False, True)
                    m.then_inc(scores_done, 1)
                elif what == "c_turn":
                    pe.wait_ge(probs_ready, 17 * n + 1)
                    flip(ps[:, 4 + k % 3, 0:P], lc[:, :, :].rearrange("p h n -> p (h n)")).then_inc(turned, 1)
                elif what == "c_values":
                    pe.wait_ge(bank_empty, bank_use["c_turn", n] + 1)
                    mm(ps[:, 4 + k % 3, :], probT_c, vc_bd[:, :, :, :].rearrange("p g h d -> p (g h d)"),
                       True, True).then_inc(turned, 1)
                elif what == "turn":
                    j, b = n
                    kind, i, g = GROUPS[j]
                    pe.wait_ge(probs_ready, last_unit(j) + 1)
                    for c in range(HPG):
                        m = flip(ps[:, 4 + k % 3, c * P:(c + 1) * P], probs[kind][:, c, b * P:(b + 1) * P])
                    m.then_inc(turned, 1)
                elif what == "values":
                    j, b = n
                    kind, i, g = GROUPS[j]
                    cols, first = key_cols(kind, i)
                    f = nth_turn[n]
                    pe.wait_ge(bank_empty, bank_use["turn", n] + 1)
                    if b == 0 and j >= 1:
                        pe.wait_ge(o_copied, j)
                    v = v_hl[:, 0 if kind == "s" else 1, g, first // P + b, :]
                    o = ps[:, 7, :]
                    mm(o, v, p_hl[:, f % 2, 0, :], b == 0, False)
                    mm(o, v, p_hl[:, f % 2, 1, :], False, b == cols // P - 1).then_inc(values_done, 1)
                elif what == "back":
                    i, g = n
                    pe.wait_ge(o_copied, 4 * i + 2 * g + 2)
                    for b in range(2):
                        for c in range(HPG):
                            m = mm(ps[:, 4 + k % 3, (b * HPG + c) * HD:(b * HPG + c + 1) * HD],
                                   o_T[b][:, c * P:(c + 1) * P], two_i[:, :], True, True)
                    m.then_inc(turned, 1)
                elif what == "out":
                    pe.wait_ge(acc_ready, 2 * (n + 1))
                    for j in range(4):
                        m = flip(ps[:, 4 + k % 3, j * P:(j + 1) * P], acc[:, j * P:(j + 1) * P])
                    m.then_inc(turned, 1)

            pe.wait_ge(bank_empty, len(bank_use))
            pe.wait_ge(samp_q, 1)

            def turn_pages(f, bank, h):
                pe.wait_ge(samp_in[f], 16 * (2 * HALF + HALF))
                for j in range(2 * HALF):
                    m = flip(ps[:, bank + j // 4, (j % 4) * P:(j % 4 + 1) * P], h.pages[:, j, 256:384])
                return m

            def turn_wins(f, bank, h):
                for j in range(2 * HALF):
                    flip(ps[:, bank + 2 + j // 4, (j % 4) * P:(j % 4 + 1) * P], h.wins[:, j, 0:P])
                pe.wait_ge(samp_dve[f], samp_at("keys0"))
                for j in range(2 * HALF):
                    for kind in range(2):
                        m = mm(ps[:, bank, 16 * kind + 2 * j:16 * kind + 2 * j + 2],
                               h.pages[:, j, kind * P:(kind + 1) * P], avg[:, :], True, True)
                return m

            def compress(f, bank, h):
                pe.wait_ge(samp_dve[f], samp_at("means"))
                mm(ps[:, bank + 1, 64:80], wc_k[:, :], h.mean[:, 0, :], True, True)
                mm(ps[0:16, bank + 1, P:2 * P], h.mean[:, 1, :], wc_v[:, :], True, True)
                return mm(ps[:, bank + 1, 256:256 + NG], tsel[:, f * SROWS:(f + 1) * SROWS], gates[0:NS, PT, :],
                          True, True)

            def score(f, bank, h):
                pe.wait_ge(samp_dve[f], samp_at("cmp"))
                q4 = qbd[:, f * HALF:(f + 1) * HALF].rearrange("p s g c t -> p (s g c t)")
                for b in range(2):
                    for s in range(HALF):
                        mm(ps[32 * s:32 * s + 32, bank + 2 + b, 0:PAST], q4[:, 32 * s:32 * s + 32],
                           h.kTc[b][:, s * PAST:(s + 1) * PAST], True, True)
                    mm(ps[:, bank + 2 + b, PAST:PAST + NS], q4, k_new[:, b, :], True, True)
                return mm(ps[:, bank, 0:16], q4, h.kc, True, True)

            def turn_probs(f, bank, h):
                pe.wait_ge(samp_act[f], 1)
                for b, buf in enumerate(h.logits):
                    flip(ps[:, bank + 1 + b, 0:P], buf[:, 0:P])
                    flip(ps[:, bank + 1 + b, P:2 * P], buf[:, P:2 * P])
                    flip(ps[0:NS, bank + 1 + b, 2 * P:3 * P], buf[:, PAST:PAST + NS])
                return flip(ps[0:16, bank + 3, 0:P], h.logits_c)

            def add_values(f, bank, h):
                pe.wait_ge(samp_dve[f], samp_at("probT"))
                mm(ps[:, bank, 0:P], h.probT_c[0:16, :], h.vc[0:16, :], True, True)
                for b, new, old in ((0, v_s, lambda s, j: h.pages[:, 2 * s + j, 384:512]),
                                    (1, v_w, lambda s, j: h.wins[:, 2 * s + j, P:2 * P])):
                    at = (b + 1) * P
                    mm(ps[:, bank, at:at + P], h.probT[b][0:NS, 2, :], new[0:NS, PT, :], True, False)
                    for s in range(HALF):
                        for j in range(2):
                            m = mm(ps[32 * s:32 * s + 32, bank, at:at + P],
                                   h.probT[b][:, j, 32 * s:32 * s + 32], old(s, j), False, j == 1)
                return m

            def turn_result(f, bank, h):
                pe.wait_ge(samp_dve[f], samp_at("res"))
                return flip(ps[:, bank + 1, 0:P], h.result)

            step = (turn_pages, turn_wins, compress, score, turn_probs, add_values, turn_result)
            for x, f in SAMP_ORDER:
                step[x](f, 4 * f, halves[f]).then_inc(samp_pe[f], 1)

            def turn_h1(i):
                pe.wait_ge(h1_ready, i + 1)
                if i >= 1:
                    pe.wait_ge(h1T_ready, i)
                r = rows(i)
                for k in range(KC):
                    m = flip(ps[:, 6 + k // 4, (k % 4) * P:(k % 4) * P + r], h1[i % 2][0:r, k * P:(k + 1) * P])
                m.then_inc(h1_turned, 1)

            for i in range(TILES):
                if i >= 3:
                    pe.wait_ge(x1_ready, i - 2)
                b0, r = 2 * (i % 3), rows(i)
                pe.wait_ge(ya_lo, i + 1)
                for k in range(KC):
                    if i == 0:
                        pe.wait_ge(woa_lo, k + 1)
                    for part, w in ((0, w_outa_hi), (0, w_outa_lo), (1, w_outa_hi)):
                        for n in range(2):
                            m = mm(ps[0:r, b0 + n, :], ya_hl[i % 2][:, part, k, 0:r], w[:, k, n * 512:(n + 1) * 512],
                                   k == 0 and (part, w) == (0, w_outa_hi), k == KC - 1 and part == 1)
                m.then_inc(outa_done, 1)
                if i >= 1:
                    turn_h1(i - 1)

            for n, (kind, c) in enumerate(order_c):
                if n == 0:
                    pe.wait_ge(wc_lo, 1)
                    for t in range(3):
                        if t < 2:
                            pe.wait_ge(x1_ready, TILES - 2)
                            pe.wait_ge(h1_lo, -(-(t + 1) * THIRD // P))
                        else:
                            turn_h1(TILES - 1)
                            pe.wait_ge(x1_ready, TILES)
                            pe.wait_ge(h1_lo, TILES)
                        for k in range(KC):
                            for part, h in ((0, h1T_hi), (0, h1T_lo), (1, h1T_hi)):
                                m = mm(ps[:, t, 0:THIRD], w_c_hl[0][:, part, k, :],
                                       h[:, k, t * THIRD:(t + 1) * THIRD], k == 0 and (part, h) == (0, h1T_hi),
                                       k == KC - 1 and part == 1)
                    m.then_inc(pc_done, 1)
                    continue
                if n >= 2:
                    pe.wait_ge(pc_act, n - 1)
                if kind in "xz":
                    w = c if kind == "x" else KC + c
                    pe.wait_ge(wc_lo, w + 1)
                    for k in range(KC):
                        for part, h in ((0, h1T_hi), (0, h1T_lo), (1, h1T_hi)):
                            for t in range(3):
                                m = mm(ps[:, 3 * (n % 2) + t, 0:THIRD], w_c_hl[w % 2][:, part, k, :],
                                       h[:, k, t * THIRD:(t + 1) * THIRD], k == 0 and (part, h) == (0, h1T_hi),
                                       k == KC - 1 and part == 1)
                else:
                    pe.wait_ge(wg_in, 32)
                    pe.wait_ge(conv_ready, c + 1)
                    for t in range(3):
                        m = mm(ps[:, 3 * (n % 2) + t, 0:THIRD], w_rg[:, 0 if kind == "r" else 1, c, :],
                               xc[c % 2][:, t * THIRD:(t + 1) * THIRD], True, True)
                m.then_inc(pc_done, 1)

            pe.wait_ge(small_ready, 1)
            for c in range(KC):
                m = flip(ps[0:36, 6 + c // 4, (c % 4) * P:(c % 4 + 1) * P], small_out[:, c, :])
            m.then_inc(small_pe, 1)

            pe.wait_ge(pc_act, len(order_c))
            for i in range(TILES):
                if i >= 3:
                    pe.wait_ge(o_ready, i - 2)
                pe.wait_ge(yc_lo, i + 1)
                b0, r = 2 * (i % 3), rows(i)
                for k in range(KC):
                    if i == 0:
                        pe.wait_ge(woc_lo, k + 1)
                    for y, w in ((y_hi, w_outc_hi), (y_hi, w_outc_lo), (y_lo, w_outc_hi)):
                        for n in range(2):
                            m = mm(ps[0:r, b0 + n, :], y[:, k, tok(i)], w[:, k, n * 512:(n + 1) * 512],
                                   k == 0 and (y, w) == (y_hi, w_outc_hi), k == KC - 1 and y is y_lo)
                m.then_inc(outc_done, 1)

        @block.vector
        def _(dve):
            v = nc.vector
            chain = [0]

            def link(i):
                chain[0] += 1
                i.then_inc(dve_chain, 1)
                dve.wait_ge(dve_chain, chain[0])

            dve.wait_ge(prep_pe, 1)
            v.tensor_copy(vecT[:, :], ps[:, 3, 0:NVEC]).then_inc(prep_dve, 1)

            def prepared():
                dve.wait_ge(prep_pe, 2)
                v.tensor_copy(rel_rows[0:HEADS, :].rearrange("p (a b) -> p a b", a=3), ps[0:HEADS, 0:3, 0:REL // 3]
                              ).then_inc(prep_dve, 1)
                dve.wait_ge(prep_pe, 3)
                v.tensor_copy(pe_mean[:, :], ps[:, 3, 508:510]).then_inc(prep_dve, 1)
                v.tensor_tensor(wspT[:, :, :], ps[:, 4, :].rearrange("p (g j) -> p g j", g=4),
                                spread(tril[:, :], 4, 1), ALU.mult).then_inc(prep_dve, 1)
                v.tensor_copy(stT[:, :, :], ps[:, 5, 0:KC * NS].rearrange("p (k s) -> p k s", k=KC)
                              ).then_inc(prep_dve, 1)
                dve.wait_ge(prep_dve, 5)

            def scale_x(i):
                dve.wait_ge(scaled, i + 1)
                r = rows(i)
                x = x_row[i % 3][0:r, :]
                v.tensor_scalar(x, x, rstd[0:r, 0, i:i + 1], None, ALU.mult).then_inc(normed, 1)

            def feature_major(dst, i, norm):
                r = rows(i)
                src = ps[:, 6:8, :].rearrange("p b (k t) -> p (b k) t", t=P)[:, :, 0:r]
                return v.tensor_tensor(dst[:, :, tok(i)], src, spread(vecT[:, norm:norm + KC], r), ALU.mult)

            def keys(i):
                r = rows(i)
                dve.wait_ge(k_turned, i + 1)
                e = v.tensor_copy(kT_s[:, tok(i)], ps[:, 3, 0:r])
                e = v.tensor_copy(kT_w[:, tok(i)], ps[:, 3, P:P + r])
                if i < PT:
                    e = v.tensor_tensor(mean_p[:, :, 2 * i:2 * i + 2],
                                        ps[:, 3, 256:260].rearrange("p (k n) -> p k n", k=2),
                                        spread(pe_mean[:, :], 2), ALU.add)
                e.then_inc(kT_ready, 1)

            def ln_center(i):
                r = rows(i)
                dve.wait_ge(ln_scaled, i + 1)
                v.tensor_scalar(vn[0:r, i, :], vn[0:r, i, :], mv[0:r, i, 0:1], rstd_v[0:r, i:i + 1],
                                ALU.subtract, ALU.mult).then_inc(ln_mid, 1)

            def h_low(i):
                dve.wait_ge(h_hi, i + 1)
                v.tensor_tensor(hT_lo[:, 4:KC, tok(i)], hT[:, 4:KC, tok(i)],
                                hT_hi[:, 4:KC, tok(i)].bitcast(F32), ALU.subtract).then_inc(h_lo, 1)

            def turned_x(i):
                dve.wait_ge(x_turned, i + 1)
                feature_major(hT, i, VEC["norm_a"]).then_inc(hT_ready, 1)

            scale_x(0)
            scale_x(1)
            dve.wait_ge(prep_dve, 1)
            turned_x(0)
            for i in range(TILES):
                r = rows(i)
                if i + 2 < TILES:
                    scale_x(i + 2)
                if i >= 1:
                    keys(i - 1)
                if i + 1 < TILES:
                    turned_x(i + 1)
                if i >= 1:
                    h_low(i - 1)
                dve.wait_ge(kvA_done, i + 1)
                if i >= 2:
                    dve.wait_ge(rows_out[i % 2], 16 * sent_rows(i))
                v.tensor_copy(kv_row[i % 2][0:r, 512:768], ps[0:r, 1, 0:256])
                v.tensor_copy(v_w[0:r, i, :], ps[0:r, 1, P:2 * P])
                if i == 0:
                    dve.wait_ge(consts_in, NCONST)
                v.tensor_tensor(gates[0:r, i, :], ps[0:r, 1, 256:KVG - 512], b_gate[0:r, :], ALU.add
                                ).then_inc(kvB_out, 1)
                if i >= 1:
                    ln_center(i - 1)
                dve.wait_ge(v_out, i + 1)
                link(v.bn_stats(bn[0:r, :], vn[0:r, i, :]))
                v.bn_aggr(mv[0:r, i, :], bn[0:r, :]).then_inc(ln_stats, 1)
                if i == 0:
                    prepared()
            def split_wlo(n):
                dve.wait_ge(wf_hi, n + 1)
                v.tensor_tensor(w_fm_hl[n % 2][:, 1], w_fm[n % 2], w_fm_hl[n % 2][:, 0].bitcast(F32),
                                ALU.subtract).then_inc(wf_lo, 1)

            h_low(TILES - 1)
            split_wlo(0)
            for k in range(4):
                dve.wait_ge(h_hi, TILES + k + 1)
                v.tensor_tensor(hT_lo[:, k, :], hT[:, k, :], hT_hi[:, k, :].bitcast(F32), ALU.subtract
                                ).then_inc(h_lo, 1)
                if k == 0:
                    keys(TILES - 1)
                    ln_center(TILES - 1)
            dve.wait_ge(kT_ready, TILES)
            v.tensor_copy(mean_rep[:, :, :], spread(mean_p[:, 1, :], HEADS, 1)).then_inc(cmp_rep, 1)

            def compressed():
                dve.wait_ge(cmp_pe, 1)
                v.tensor_copy(kc_bd[0:HD, 0, :], ps[0:HD, 6, 0:NB])
                v.tensor_copy(kc_bd[HD:P, 1, :], ps[HD:P, 6, 0:NB])
                v.tensor_tensor(vc_bd[:, :, :, :],
                                spread(ps[:, 6, P:2 * P].rearrange("p (g d) -> p g d", g=KVH), HPG, 2),
                                spread(headrow[:, :].rearrange("p (g h) -> p g h", g=KVH), HD, 3),
                                ALU.mult).then_inc(cmp_ready, 1)
                dve.wait_ge(diag_in, 16 * 36)
                v.tensor_tensor(wspT_s[:, :, :], wspT_s[:, :, :], spread(tril_s[:, :], 4, 1), ALU.mult
                                ).then_inc(prep_dve, 1)

            dve.wait_ge(rel_out, 16 * HEADS)
            def mixed(i):
                r = rows(i)
                dve.wait_ge(mix_done, i + 1)
                src = ps[:, 6 + i % 2, :].rearrange("p (g t) -> p g t", t=P)[:, :, 0:r]
                tmp = part_sb[:, 0:4 * r].rearrange("p (g t) -> p g t", g=4)
                if i >= 1:
                    dve.wait_ge(mix_used, i)
                if i < PT:
                    link(v.tensor_tensor(tmp, src, b_sp[:, :, :], ALU.add))
                else:
                    for g in range(4):
                        e = v.tensor_tensor(tmp[:, g, :].rearrange("p (s t) -> p s t", t=NNEW),
                                            src[:, g, :].rearrange("p (s t) -> p s t", t=NNEW),
                                            spread(b_sp[:, g, 0:NNEW], NSEQ, 1), ALU.add)
                    link(e)
                y = yT[:, 4:8, tok(i)]
                v.tensor_tensor(y, y, tmp, ALU.mult).then_inc(mix_used, 1)

            for n, (kind, j, who) in enumerate(FM_A):
                if n == 7:
                    compressed()
                if kind == "q":
                    for i in MIX_BEFORE[j]:
                        mixed(i)
                if n == 0:
                    split_wlo(1)
                if who != "dve":
                    if n + 2 < len(FM_A):
                        split_wlo(n + 2)
                    continue
                dve.wait_ge(fm_done, n + 1)
                src = ps[:, 3 * (n % 2):3 * (n % 2) + 3, 0:THIRD]
                if kind == "u":
                    fm_wait(dve, n - 1)
                    y = yT[:, 4 + j, :].rearrange("p (a b) -> p a b", a=3)
                    v.tensor_tensor(y, src, y, ALU.mult).then_inc(fm_dve, 1)
                else:
                    v.tensor_scalar(qT[:, j, :].rearrange("p (a b) -> p a b", a=3), src, -HD ** -0.5, None,
                                    ALU.mult).then_inc(fm_dve, 1)
                if n + 2 < len(FM_A):
                    split_wlo(n + 2)
            for b, kT in ((1, kT_w), (0, kT_s)):
                v.tensor_copy(k_new[:, b, :], kT[:, SEQ:TOK])
                for g in range(KVH):
                    gp = slice(g * HD, (g + 1) * HD)
                    dve.wait_ge(k_hi_own, 2 * (1 - b) + g + 1)
                    v.tensor_tensor(k_lo[gp, b, :], kT[gp, 0:SEQ], k_hi[gp, b, g, :].bitcast(F32), ALU.subtract)
            for b, vv in ((1, v_w), (0, v_s)):
                for g in range(KVH):
                    gp = slice(g * HD, (g + 1) * HD)
                    dve.wait_ge(split_hi, 2 * (1 - b) + g + 1)
                    v.tensor_tensor(v_hl[:, b, g, :, HD:2 * HD], vv[:, 0:PT, gp],
                                    v_hl[:, b, g, :, 0:HD].bitcast(F32), ALU.subtract).then_inc(split_lo, 1)
            dve.wait_ge(split_lo, 4)
            dve.wait_ge(bias_in[0], 16 * HEADS)
            dve.wait_ge(gates_ready, 1)
            dve.wait_ge(vn_out, 16)

            def sample_queries():
                dve.wait_ge(bias_s_in, 16 * 12)
                for s in range(HALF):
                    o = slice(32 * s, 32 * s + 32)
                    e = v.tensor_copy(bias_b[o, NBP * s:NBP * s + NBP], bias_c[o, BLK - 1::BLK])
                for g in range(KVH):
                    gp = slice(g * HD, (g + 1) * HD)
                    for s in range(NSEQ):
                        e = v.tensor_copy(qbd[gp, s, g, :, :], qT[gp, :, SEQ + s * NNEW:SEQ + (s + 1) * NNEW])
                e.then_inc(samp_q, 1)

            for what, n in steps:
                k = bank_use.get((what, n))
                if k is not None:
                    dve.wait_ge(turned, k + 1)
                    bank = ps[:, 4 + k % 3, :]
                if what == "split_q":
                    if n == PT - 1:
                        sample_queries()
                    dve.wait_ge(q_hi, n + 1)
                    for g in range(KVH):
                        gp = slice(g * HD, (g + 1) * HD)
                        other = slice((1 - g) * HD, (2 - g) * HD)
                        hs = slice(g * HPG, (g + 1) * HPG)
                        e = v.tensor_tensor(q_hl[other, n % 2, hs, :], qT[gp, :, tok(n)],
                                            q_hl[gp, n % 2, hs, :].bitcast(F32), ALU.subtract)
                    e.then_inc(q_lo, 1)
                elif what == "scores":
                    kind, i, h = units[n]
                    cols, first = key_cols(kind, i)
                    slot = 2 * (n % 2)
                    dve.wait_ge(scores_done, n + 1)
                    if n >= 16:
                        dve.wait_ge(probs_ready, n - 15)
                    if kind == "c" and i == PT // 2:
                        dve.wait_ge(bias_in[1], 16 * HEADS)
                        link(v.tensor_tensor(bias_far, bias[:, :, SEQ - WCOLS:SEQ - WIN],
                                             spread(far[:, :], HEADS, 1), ALU.add))
                    if kind == "c":
                        if i >= 1:
                            dve.wait_ge(turned, bank_use["c_turn", i - 1] + 1)
                            dve.wait_ge(logits_ready, n - 16)
                        m0 = 14 - 2 * i
                        src = ps[:, slot, 0:HPG * 2 * NB].rearrange("p (c g n) -> p g c n", c=HPG, g=KVH)
                        table = bias[:, :, BLK - 1::BLK]
                        for g in range(KVH):
                            hs = slice(g * HPG, (g + 1) * HPG)
                            e = v.tensor_tensor(lc[:, hs, 0:cols], src[:, g, :, 0:cols],
                                                table[:, hs, m0:m0 + cols], ALU.add)
                        link(e)
                        link(v.tensor_reduce(lmin[:, :], lc[:, :, 0:cols], AX.X, ALU.min))
                        v.tensor_tensor(lc[:, :, 0:cols], lc[:, :, 0:cols], spread(lmin[:, :], cols),
                                        ALU.subtract).then_inc(logits_ready, 1)
                    else:
                        buf = probs[kind][:, h % HPG, :]
                        m = negm[:, n % 16:n % 16 + 1]
                        src = flat[:, slot * 512:slot * 512 + cols]
                        if cols == WCOLS and kind == "w":
                            fm = far_min[:, n % 2:n % 2 + 1]
                            dve.wait_ge(logits_ready, n - 1)
                            link(v.tensor_tensor_reduce(buf[:, 0:P], src[:, 0:P], bias_far[:, h, :], 1.0, 3e38,
                                                        ALU.add, ALU.min, fm))
                            v.tensor_tensor_reduce(buf[:, P:cols], src[:, P:cols], bias[:, h, SEQ - WIN:SEQ],
                                                   1.0, fm, ALU.add, ALU.min, m
                                                   ).then_inc(logits_ready, 1)
                        else:
                            v.tensor_tensor_reduce(buf[:, 0:cols], src, bias[:, h, SEQ - cols:SEQ], 1.0, 3e38,
                                                   ALU.add, ALU.min, m).then_inc(logits_ready, 1)
                elif what == "c_turn":
                    v.tensor_copy(probT_c, bank[:, 0:P]).then_inc(bank_empty, 1)
                    dve.wait_ge(probs_ready, 17 * n + 1)
                    link(v.tensor_reduce(sums[:, n % 2, 0, :], lc[:, :, 0:2 * n + 2], AX.X, ALU.add))
                    link(v.reciprocal(inv[:, 0, :], sums[:, n % 2, 0, :]))
                    if n >= 1:
                        dve.wait_ge(bank_empty, bank_use["c_values", n - 1] + 1)
                    link(v.tensor_tensor(coef[:, 0, :], inv[:, 0, :], gates[:, n, 0:HEADS], ALU.mult))
                    if n == 0:
                        link(v.tensor_scalar(coef[:, 0, :], coef[:, 0, :], rowok[:, 0:1], None, ALU.mult))
                elif what == "c_values":
                    if n >= 1:
                        dve.wait_ge(acc_ready, 2 * n)
                    v.tensor_tensor(acc_c.rearrange("p (h d) -> p h d", d=HD),
                                    bank.rearrange("p (h d) -> p h d", d=HD),
                                    spread(coef[:, 0, :], HD), ALU.mult).then_inc(bank_empty, 1)
                elif what == "turn":
                    f = nth_turn[n]
                    dve.wait_ge(p_hi, f + 1)
                    v.tensor_tensor(p_hl[:, f % 2, 1, :], bank, p_hl[:, f % 2, 0, :].bitcast(F32),
                                    ALU.subtract).then_inc(bank_empty, 1)
                elif what == "back":
                    i, g = n
                    hs = slice(g * HPG, (g + 1) * HPG)
                    link(v.reciprocal(inv[:, 1:3, hs], sums[:, i % 2, 1:3, hs]))
                    g3 = gates[:, i, :].rearrange("p (b h) -> p b h", b=3)
                    link(v.tensor_tensor(coef[:, 1:3, hs], inv[:, 1:3, hs], g3[:, 1:3, hs], ALU.mult))
                    if i + g >= 1:
                        dve.wait_ge(acc_ready, 2 * i + g)
                    v.tensor_tensor(gated[:, :, :, :], bank.rearrange("p (b c d) -> p b c d", b=2, c=HPG),
                                    spread(coef[:, 1:3, hs], HD, 3), ALU.mult).then_inc(bank_empty, 1)
                    dve.wait_ge(bank_empty, k + 1)
                    if i >= 1:
                        dve.wait_ge(turned, bank_use["out", i - 1] + 1)
                    a = acc[:, g * 256:(g + 1) * 256].rearrange("p (c d) -> p c d", c=HPG)
                    ac = acc_c[:, g * 256:(g + 1) * 256].rearrange("p (c d) -> p c d", c=HPG)
                    link(v.tensor_tensor(a, gated[:, 0], ac, ALU.add))
                    v.tensor_tensor(a, gated[:, 1], a, ALU.add).then_inc(acc_ready, 1)
                elif what == "out":
                    y = yT[:, 0:4, tok(n)]
                    v.tensor_tensor(y, bank.rearrange("p (j t) -> p j t", t=P), y, ALU.mult
                                    ).then_inc(bank_empty, 1)


            def keys_out(f, bank, h):
                v.tensor_copy(h.kTc[0], flat[:, bank * 512:bank * 512 + 1024]).then_inc(samp_dve[f], 1)

            def means_out(f, bank, h):
                v.tensor_copy(h.kTc[1], flat[:, bank * 512 + 1024:bank * 512 + 2048]).then_inc(samp_dve[f], 1)
                v.tensor_tensor(h.mean, ps[:, bank, 0:32].rearrange("p (k n) -> p k n", k=2),
                                spread(pe_mean[:, :], 16), ALU.add).then_inc(samp_dve[f], 1)

            def compressed_out(f, bank, h):
                v.tensor_copy(h.kc, ps[:, bank + 1, 64:80])
                v.tensor_copy(h.vc[0:16, :], ps[0:16, bank + 1, P:2 * P])
                link(v.tensor_tensor(h.gate_rows, ps[:, bank + 1, 256:256 + NG].rearrange("p (b h) -> p b h", b=3),
                                     spread(hsel[:, :], 3, 1), ALU.mult))
                v.tensor_reduce(h.gate, h.gate_rows, AX.X, ALU.add).then_inc(samp_dve[f], 1)

            def add_min(buf, src, tab, at):
                return v.tensor_tensor_reduce(buf, src, tab, 1.0, 3e38, ALU.add, ALU.min, at)

            def logits_out(f, bank, h):
                add_min(h.logits_c, ps[:, bank, 0:16], bias_b[:, :], h.neg[:, 0:1])
                for b, buf in enumerate(h.logits):
                    add_min(buf[:, 0:PAST], ps[:, bank + 2 + b, 0:PAST], bias_c[:, :], h.least[:, b:b + 1])
                    e = add_min(buf[:, PAST:PAST + NS], ps[:, bank + 2 + b, PAST:PAST + NS], bias_n[:, f, :],
                                h.least[:, 2 + b:3 + b])
                link(e)
                v.tensor_tensor(h.neg[:, 1:3], h.least[:, 0:2], h.least[:, 2:4], ALU.min).then_inc(samp_dve[f], 1)

            def probs_out(f, bank, h):
                for b, pt in enumerate(h.probT):
                    v.tensor_copy(pt[:, 0:2, :], ps[:, bank + 1 + b, 0:2 * P].rearrange("p (a b) -> p a b", a=2))
                    v.tensor_copy(pt[0:NS, 2, :], ps[0:NS, bank + 1 + b, 2 * P:3 * P])
                v.tensor_copy(h.probT_c[0:16, :], ps[0:16, bank + 3, 0:P]).then_inc(samp_dve[f], 1)
                link(v.reciprocal(h.coef, h.sums))
                link(v.tensor_tensor(h.coef, h.coef, h.gate, ALU.mult))

            def result_out(f, bank, h):
                link(v.tensor_scalar(h.result, ps[:, bank, 0:P], h.coef[:, 0:1], None, ALU.mult))
                link(v.scalar_tensor_tensor(out=h.result, in0=ps[:, bank, P:2 * P], scalar=h.coef[:, 1:2],
                                            in1=h.result, op0=ALU.mult, op1=ALU.add))
                v.scalar_tensor_tensor(out=h.result, in0=ps[:, bank, 2 * P:3 * P], scalar=h.coef[:, 2:3],
                                       in1=h.result, op0=ALU.mult, op1=ALU.add).then_inc(samp_dve[f], 1)

            def gated_out(f, bank, h):
                for head in range(HEADS):
                    g, j, o = head // HPG, head // 2, (head % 2) * HD
                    c0 = SEQ + f * HALF * NNEW
                    y = yT[o:o + HD, j, c0:c0 + HALF * NNEW].rearrange("p (s t) -> p s t", t=NNEW)
                    src = ps[g * HD:(g + 1) * HD, bank + 1, 0:P].rearrange("p (s h t) -> p s h t", s=HALF, h=HEADS)
                    e = v.tensor_tensor(y, src[:, :, head, :], y, ALU.mult)
                e.then_inc(samp_dve[f], 1)

            out = (keys_out, means_out, compressed_out, logits_out, probs_out, result_out, gated_out)
            for x, f in SAMP_ORDER:
                dve.wait_ge(samp_pe[f], x + 1)
                out[x](f, 4 * f, halves[f])

            lm = vecT[:, VEC["lru_lambda"]:VEC["lru_lambda"] + KC]
            link(v.tensor_scalar(lam[:, 2, :], lm, -1.0, None, ALU.mult))
            v.tensor_tensor(lam[:, 0, :], lm, lam[:, 2, :], ALU.max).then_inc(lam_ready, 1)

            def fm_h1(i):
                dve.wait_ge(h1_turned, i + 1)
                feature_major(h1T, i, VEC["norm_c"]).then_inc(h1T_ready, 1)

            def h1_low(i):
                dve.wait_ge(h1_hi, i + 1)
                v.tensor_tensor(h1T_lo[:, :, tok(i)], h1T[:, :, tok(i)], h1T_hi[:, :, tok(i)].bitcast(F32),
                                ALU.subtract).then_inc(h1_lo, 1)

            def split_wclo(n):
                dve.wait_ge(wc_hi, n + 1)
                v.tensor_tensor(w_c_hl[n % 2][:, 1], w_c[n % 2], w_c_hl[n % 2][:, 0].bitcast(F32),
                                ALU.subtract).then_inc(wc_lo, 1)

            def ya_low(i):
                r = rows(i)
                dve.wait_ge(ya_hi, i + 1)
                v.tensor_tensor(ya_hl[i % 2][:, 1, :, 0:r], yT[:, :, tok(i)], ya_hl[i % 2][:, 0, :, 0:r].bitcast(F32),
                                ALU.subtract).then_inc(ya_lo, 1)

            ya_low(0)
            for k in range(KC):
                dve.wait_ge(woa_hi, k + 1)
                v.tensor_tensor(w_outa_lo[:, k, :], w_outa[:, k, :], w_outa_hi[:, k, :].bitcast(F32),
                                ALU.subtract).then_inc(woa_lo, 1)
            ya_low(1)
            for i in range(TILES):
                r, b0 = rows(i), 2 * (i % 3) * 512
                dve.wait_ge(outa_done, i + 1)
                dve.wait_ge(xa_in[i % 3], 16 * (i // 3 + 1))
                v.tensor_tensor(x1[i % 3][0:r, :], flat[0:r, b0:b0 + D], x1[i % 3][0:r, :], ALU.add
                                ).then_inc(x1_ready, 1)
                if i + 2 < TILES:
                    ya_low(i + 2)
                if i >= 1:
                    fm_h1(i - 1)
                if i == TILES - 1:
                    split_wclo(0)
                if i >= 2:
                    h1_low(i - 2)
                dve.wait_ge(scaled, TILES + i + 1)
                v.tensor_scalar(h1[i % 2][0:r, :], x1[i % 3][0:r, :], rstd[0:r, 1, i:i + 1], None, ALU.mult
                                ).then_inc(h1_ready, 1)
            h1_low(TILES - 2)
            fm_h1(TILES - 1)
            h1_low(TILES - 1)
            split_wclo(1)
            dve.wait_ge(lam_exp, 1)
            link(v.tensor_scalar(lam[:, 3, :], lam[:, 1, :], 2.0, None, ALU.add))
            link(v.reciprocal(lam[:, 3, :], lam[:, 3, :]))
            link(v.tensor_tensor(lam[:, 3, :], lam[:, 3, :], lam[:, 1, :], ALU.mult))
            link(v.tensor_tensor(lam[:, 4, :], lam[:, 3, :], lam[:, 3, :], ALU.mult))
            link(v.tensor_scalar(lam[:, 5, :], lam[:, 4, :], 1.0 / 17, 1.0 / 15, ALU.mult, ALU.add))
            for k in (13, 11, 9, 7, 5, 3, 1):
                link(v.tensor_tensor(lam[:, 5, :], lam[:, 5, :], lam[:, 4, :], ALU.mult))
                link(v.tensor_scalar(lam[:, 5, :], lam[:, 5, :], 1.0 / k, None, ALU.add))
            link(v.tensor_tensor(lam[:, 5, :], lam[:, 5, :], lam[:, 3, :], ALU.mult))
            link(v.tensor_scalar(lam[:, 5, :], lam[:, 5, :], 2.0, None, ALU.mult))
            link(v.tensor_scalar(lam[:, 2, :], lam[:, 2, :], 0.0, None, ALU.max))
            link(v.tensor_tensor(lam[:, 5, :], lam[:, 5, :], lam[:, 2, :], ALU.add))
            link(v.tensor_scalar(lam[:, 4, :], lam[:, 5, :], 8.0, None, ALU.mult))
            v.tensor_scalar(lam[:, 5, :], lam[:, 4, :], -1.0, None, ALU.mult).then_inc(lam_ready, 1)

            link(v.memset(xin[:, 0:3], 0.0))
            link(v.tensor_copy(bS[:, :, :, 0], stT[:, :, 24:32]))

            def conv(c):
                n = order_c_at[("x", c)]
                dve.wait_ge(pc_act, n + 1)
                if c >= 1:
                    dve.wait_ge(conv_ready, c)
                link(v.tensor_copy(xin_s[:, :, 0:3], stT[:, c, 0:24].rearrange("p (s k) -> p s k", k=3)))
                v.tensor_copy(small_out[:, c, 8:32].rearrange("p (s k) -> p s k", k=3), xin_s[:, :, 4:7])
                v.tensor_copy(small_out[:, c, 33:36], xin[:, SEQ:SEQ + 3])
                cw = VEC["conv_w"] + c
                cb = vecT[:, VEC["conv_b"] + c:VEC["conv_b"] + c + 1]
                outp = xc[c % 2][:, 0:SEQ]
                outs_ = xc[c % 2][:, SEQ:TOK].rearrange("p (s t) -> p s t", t=NNEW)
                v.tensor_scalar(outp, xin[:, 0:SEQ], vecT[:, cw:cw + 1], cb, ALU.mult, ALU.add)
                link(v.tensor_scalar(outs_, xin_s[:, :, 0:NNEW], vecT[:, cw:cw + 1], cb, ALU.mult, ALU.add))
                for k in range(1, 4):
                    w = vecT[:, cw + 8 * k:cw + 8 * k + 1]
                    v.scalar_tensor_tensor(out=outp, in0=xin[:, k:k + SEQ], scalar=w, in1=outp,
                                           op0=ALU.mult, op1=ALU.add)
                    e = v.scalar_tensor_tensor(out=outs_, in0=xin_s[:, :, k:k + NNEW], scalar=w, in1=outs_,
                                               op0=ALU.mult, op1=ALU.add)
                    if k < 3:
                        link(e)
                e.then_inc(conv_ready, 1)
                split_wclo(c + 2)

            def recur(c):
                dve.wait_ge(ta_ready, c + 1)
                link(v.tensor_tensor(e_buf, r_buf, r_buf, ALU.mult))
                v.scalar_tensor_tensor(out=t_buf, in0=e_buf, scalar=1.0, in1=t_buf, op0=ALU.add, op1=ALU.mult
                                       ).then_inc(m_ready, 1)
                dve.wait_ge(igx_ready, c + 1)
                dve.wait_ge(sq_ready, c + 1)
                link(v.tensor_tensor(t_buf, t_buf, ig_buf, ALU.mult))
                v.tensor_copy(bS[:, c, :, 1:NNEW + 1], t_buf[:, SEQ:TOK].rearrange("p (s t) -> p s t", t=NNEW))
                v.tensor_tensor_scan(states[:, c, 0:SEQ], r_buf[:, 0:SEQ], t_buf[:, 0:SEQ], 0.0, ALU.mult, ALU.add
                                     ).then_inc(h_ready, 1)

            for c in range(KC):
                if c < 1:
                    conv(c)
                if c + 1 < KC:
                    conv(c + 1)
                else:
                    split_wclo(KC + 2)
                recur(c)
            split_wclo(KC + 3)
            hS = t_buf[:, 0:KC * NSEQ * (NNEW + 1)]
            dve.wait_ge(h_ready, KC)
            link(v.tensor_tensor_scan(hS, aS[:, :, :, :].rearrange("p c s t -> p (c s t)"),
                                      bS[:, :, :, :].rearrange("p c s t -> p (c s t)"), 0.0,
                                      ALU.mult, ALU.add))
            hS4 = hS.rearrange("p (c s t) -> p c s t", c=KC, s=NSEQ)
            for c in range(KC):
                v.tensor_copy(states[:, c, SEQ:TOK].rearrange("p (s t) -> p s t", t=NNEW), hS4[:, c, :, 1:NNEW + 1])
            v.tensor_copy(small_out[:, :, 0:8], hS4[:, :, :, NNEW])
            v.tensor_copy(small_out[:, :, 32:33], states[:, :, SEQ - 1:SEQ]).then_inc(small_ready, 1)
            dve.wait_ge(small_ready, 1)
            for c in range(KC):
                n = order_c_at[("z", c)]
                dve.wait_ge(pc_act, n + 1)
                if 2 <= c < KC - 2:
                    split_wclo(KC + c + 2)
                v.tensor_tensor(states[:, c, :], states[:, c, :], sz_buf[c % 2], ALU.mult).then_inc(y_ready, 1)
            def y_low(i):
                dve.wait_ge(yc_hi, i + 1)
                v.tensor_tensor(y_lo[:, :, tok(i)], states[:, :, tok(i)], y_hi[:, :, tok(i)].bitcast(F32),
                                ALU.subtract).then_inc(yc_lo, 1)

            dve.wait_ge(y_ready, KC)
            y_low(0)
            for k in range(KC):
                dve.wait_ge(woc_hi, k + 1)
                v.tensor_tensor(w_outc_lo[:, k, :], w_outc[:, k, :], w_outc_hi[:, k, :].bitcast(F32),
                                ALU.subtract).then_inc(woc_lo, 1)
            y_low(1)
            dve.wait_ge(small_pe, 1)
            v.tensor_copy(small_tm[0:36, :], flat[0:36, 6 * 512:8 * 512]).then_inc(small_rows, 1)

            def finish(i):
                r = rows(i)
                if i == 0:
                    dve.wait_ge(fin_in, 16)
                dve.wait_ge(scaled, 2 * TILES + i + 1)
                v.scalar_tensor_tensor(out=y_row[i % 2][0:r, :], in0=x1_again[i % 3][0:r, :], scalar=rstd[0:r, 2, i:i + 1],
                                       in1=fin_g[0:r, :], op0=ALU.mult, op1=ALU.mult).then_inc(y_row_ready, 1)

            for i in range(TILES):
                r, b0 = rows(i), 2 * (i % 3) * 512
                dve.wait_ge(outc_done, i + 1)
                dve.wait_ge(x1_in[i % 3], 16 * (i // 3 + 1))
                v.tensor_tensor(x1_again[i % 3][0:r, :], flat[0:r, b0:b0 + D], x1_again[i % 3][0:r, :], ALU.add
                                ).then_inc(o_ready, 1)
                if i + 2 < TILES:
                    y_low(i + 2)
                if i >= 1:
                    finish(i - 1)
            finish(TILES - 1)


_WEIGHTS = ["x_prompt", "x_sample", "cache_nsa", "cache_win", "state_lru_h", "state_lru_conv", "page_table",
            "norm_a", "w_in_a", "b_gate_a", "pe_cmp", "w_cmp", "gmlp_ln_g", "gmlp_ln_b", "w_spatial",
            "b_spatial", "w_out_a", "norm_c", "w_in_c", "conv_w", "conv_b", "w_rg_a", "b_rg_a", "w_rg_x",
            "b_rg_x", "lru_lambda", "w_out_c", "rel_bias", "final_norm"]
_OUTS = [("y_prompt", (1, SEQ, D)), ("y_sample", (NSEQ, NNEW, D)),
         ("nsa_rows_prompt", (1, 1, SEQ, 4, KVH, HD)), ("nsa_rows_sample", (1, NSEQ, NNEW, 4, KVH, HD)),
         ("win_rows_prompt", (1, 1, WIN, 2, KVH, HD)), ("win_rows_sample", (1, NSEQ, NNEW, 2, KVH, HD)),
         ("gmlp_v_sample", (1, NSEQ, NNEW, 512)), ("lru_h_prompt", (1, 1, D)), ("lru_h_sample", (1, NSEQ, D)),
         ("lru_conv_prompt", (1, 1, 3, D)), ("lru_conv_sample", (1, NSEQ, 3, D))]


def kernel(**inputs):
    import concourse.bacc as _bacc
    from concourse.bass_utils import run_bass_kernel_spmd as _run

    nc = _bacc.Bacc("TRN2", target_bir_lowering=False, num_devices=1)
    arrays, ins, outs = {}, {}, {}
    given = {n: np.ascontiguousarray(inputs[n]) for n in _WEIGHTS}
    given.update(constants())
    for name, a in given.items():
        arrays[f"in_{name}"] = a
        ins[name] = nc.dram_tensor(f"in_{name}", a.shape, mybir.dt.from_np(a.dtype), kind="ExternalInput").ap()
    for name, shape in _OUTS:
        outs[name] = nc.dram_tensor(f"out_{name}", shape, F32, kind="ExternalOutput").ap()
    build(nc, ins, outs)
    r = _run(nc, [arrays], core_ids=[0])
    return tuple(r.results[0][f"out_{name}"] for name, _ in _OUTS)
```
